# Optimizing a Trainium2 kernel written in Bass

```python
import math
import jax
import jax.numpy as jnp
from jax import lax
import numpy as np

D_MODEL = 1024
BATCH = 1
SEQ = 256
DEPTH = 2

F32 = jnp.float32
RMS_EPS = 1e-6
NEG = -1e30
N_ATTN_HEADS = 8
ATTN_HEAD_DIM = 64
ATTN_WIDTH = N_ATTN_HEADS * ATTN_HEAD_DIM
REL_BUCKETS = 32
REL_MAX_DIST = 1024
SSD_HEADS = 24
SSD_HEAD_DIM = 64
SSD_INNER = SSD_HEADS * SSD_HEAD_DIM
SSD_GROUPS = 4
SSD_STATE = 128
SSD_CONV = 4
SSD_CHUNK = 128
SSD_XBC = SSD_INNER + 2 * SSD_GROUPS * SSD_STATE
SWA_KV_HEADS = 2
SWA_WINDOW = 128
SWA_BLOCK = 128
GDN_HEADS = 12
GDN_HEAD_DIM = 128
GDN_INNER = GDN_HEADS * GDN_HEAD_DIM
GDN_CONV = 4
GDN_CHUNK = 64
MOBA_BLOCK = 256
MOBA_TOPK = 3
MOBA_QBLOCK = 128
FFN_DIM = 2816
FFN_CONV = 3
MIX_WIDTH = SSD_INNER + ATTN_WIDTH
AB_SIZES = (SSD_INNER, SSD_XBC, SSD_HEADS, ATTN_WIDTH, SWA_KV_HEADS * ATTN_HEAD_DIM, SWA_KV_HEADS * ATTN_HEAD_DIM)
AB_COLS = sum(AB_SIZES)
AB_SPLITS = tuple(int(v) for v in np.cumsum(AB_SIZES)[:-1])
CD_SIZES = (3 * GDN_INNER, GDN_INNER, GDN_HEADS, GDN_HEADS, ATTN_WIDTH, ATTN_WIDTH, ATTN_WIDTH)
CD_COLS = sum(CD_SIZES)
CD_SPLITS = tuple(int(v) for v in np.cumsum(CD_SIZES)[:-1])
N_EVEN = (DEPTH + 1) // 2
N_ODD = DEPTH // 2

kernel_name = 'hybrid_ssd_swa_gdn_moba_block'

def _rms(x):
    xf = x.astype(F32)
    return xf * lax.rsqrt(jnp.mean(xf * xf, axis=-1, keepdims=True) + RMS_EPS)

def rms_norm(x, w):
    return (_rms(x) * w.astype(F32)).astype(x.dtype)

def l2norm(t):
    t = t.astype(F32)
    return t * lax.rsqrt(jnp.sum(t * t, axis=-1, keepdims=True) + 1e-6)

def causal_dwconv(x, w, b=None):
    width, ch = w.shape
    y = lax.conv_general_dilated(x, w[:, None, :].astype(x.dtype), window_strides=(1,),
                                 padding=((width - 1, 0),), dimension_numbers=('NWC', 'WIO', 'NWC'),
                                 feature_group_count=ch)
    if b is not None:
        y = y + b.astype(x.dtype)
    return y

def rel_bucket(dist):
    max_exact = REL_BUCKETS // 2
    d = jnp.maximum(dist, 0)
    df = jnp.maximum(d, 1).astype(F32)
    large = max_exact + (jnp.log(df / max_exact) / math.log(REL_MAX_DIST / max_exact)
                         * (REL_BUCKETS - max_exact)).astype(jnp.int32)
    large = jnp.minimum(large, REL_BUCKETS - 1)
    return jnp.where(d < max_exact, d, large)

def ssd_chunked(x, dt, a, bm, cm):
    bsz, s, h, p = x.shape
    g, n = bm.shape[2], bm.shape[3]
    r = h // g
    q = SSD_CHUNK
    nc = s // q
    xdt = (x.astype(F32) * dt[..., None]).reshape(bsz, nc, q, g, r, p)
    acs = jnp.cumsum((dt * a).reshape(bsz, nc, q, g, r), axis=2)
    bc = bm.astype(F32).reshape(bsz, nc, q, g, n)
    cc = cm.astype(F32).reshape(bsz, nc, q, g, n)
    tri = jnp.tril(jnp.ones((q, q), bool))[:, :, None, None]
    diff = acs[:, :, :, None] - acs[:, :, None, :]
    lmat = jnp.where(tri, jnp.exp(jnp.where(tri, diff, 0.0)), 0.0)
    cb = jnp.einsum('bclgn,bcsgn->bclsg', cc, bc)
    y_diag = jnp.einsum('bclsg,bclsgr,bcsgrp->bclgrp', cb, lmat, xdt)
    decay_states = jnp.exp(acs[:, :, -1:] - acs)
    states = jnp.einsum('bclgn,bclgr,bclgrp->bcgrpn', bc, decay_states, xdt)
    chunk_decay = jnp.exp(acs[:, :, -1])

    def step(hs, inp):
        st, dec = inp
        return hs * dec[..., None, None] + st, hs

    h0 = jnp.zeros((bsz, g, r, p, n), F32)
    _, h_in = lax.scan(step, h0, (jnp.moveaxis(states, 1, 0), jnp.moveaxis(chunk_decay, 1, 0)))
    h_in = jnp.moveaxis(h_in, 0, 1)
    y_off = jnp.einsum('bclgn,bcgrpn,bclgr->bclgrp', cc, h_in, jnp.exp(acs))
    return (y_diag + y_off).reshape(bsz, s, h, p)

def mamba2_ssd_mixer(z, xbc, dt_raw, conv_w, conv_b, dt_bias, a_log, d_skip, norm_w):
    bsz, s, _ = z.shape
    xbc = jax.nn.silu(causal_dwconv(xbc, conv_w, conv_b))
    xs, bm, cm = jnp.split(xbc, [SSD_INNER, SSD_INNER + SSD_GROUPS * SSD_STATE], axis=-1)
    xs = xs.reshape(bsz, s, SSD_HEADS, SSD_HEAD_DIM)
    dt = jax.nn.softplus(dt_raw.astype(F32) + dt_bias.astype(F32))
    a = -jnp.exp(a_log.astype(F32))
    y = ssd_chunked(xs, dt, a, bm.reshape(bsz, s, SSD_GROUPS, SSD_STATE), cm.reshape(bsz, s, SSD_GROUPS, SSD_STATE))
    y = y + d_skip.astype(F32)[:, None] * xs.astype(F32)
    y = y.reshape(bsz, s, SSD_INNER) * jax.nn.silu(z.astype(F32))
    y = _rms(y.reshape(bsz, s, SSD_GROUPS, SSD_INNER // SSD_GROUPS)).reshape(bsz, s, SSD_INNER)
    return (y * norm_w.astype(F32)).astype(z.dtype)

def swa_sink_attention(q, k, v, sinks, rel_bias):
    bsz, s, hq, dh = q.shape
    hkv = k.shape[2]
    grp = hq // hkv
    blk = SWA_BLOCK
    nb = s // blk
    qb = q.reshape(bsz, nb, blk, hkv, grp, dh)
    kb = k.reshape(bsz, nb, blk, hkv, dh)
    vb = v.reshape(bsz, nb, blk, hkv, dh)

    def band(t):
        prev = jnp.pad(t, ((0, 0), (1, 0), (0, 0), (0, 0), (0, 0)))[:, :-1]
        return jnp.concatenate([prev, t], axis=2)

    kk, vv = band(kb), band(vb)
    dist = blk + jnp.arange(blk)[:, None] - jnp.arange(2 * blk)[None, :]
    kpos = jnp.arange(nb)[:, None] * blk - blk + jnp.arange(2 * blk)[None, :]
    mask = ((dist >= 0) & (dist < SWA_WINDOW))[None, :, :] & (kpos >= 0)[:, None, :]
    bias = rel_bias[rel_bucket(dist)].astype(F32).reshape(blk, 2 * blk, hkv, grp).transpose(2, 3, 0, 1)
    sc = jnp.einsum('bnqhgd,bnkhd->bnhgqk', qb, kk).astype(F32) * (dh ** -0.5) + bias
    sc = jnp.where(mask[None, :, None, None], sc, NEG)
    sink = jnp.broadcast_to(sinks.astype(F32).reshape(hkv, grp)[:, :, None, None], sc.shape[:-1] + (1,))
    p = jax.nn.softmax(jnp.concatenate([sc, sink], axis=-1), axis=-1)[..., :-1]
    o = jnp.einsum('bnhgqk,bnkhd->bnqhgd', p.astype(v.dtype), vv)
    return o.reshape(bsz, s, hq * dh)

def gated_delta_rule(q, k, v, g, beta):
    bsz, s, h, dk = q.shape
    dv = v.shape[-1]
    c = GDN_CHUNK
    nc = s // c

    def chunk(t):
        t = t.astype(F32).reshape((bsz, nc, c, h) + t.shape[3:])
        return jnp.moveaxis(t, (1, 3), (0, 2))

    q = chunk(q) * (dk ** -0.5)
    k, v, g, beta = chunk(k), chunk(v), chunk(g), chunk(beta)
    gc = jnp.cumsum(g, axis=-1)
    tri = jnp.tril(jnp.ones((c, c), bool))
    strict = jnp.tril(jnp.ones((c, c), bool), -1)
    diff = gc[..., :, None] - gc[..., None, :]
    decay = jnp.where(tri, jnp.exp(jnp.where(tri, diff, 0.0)), 0.0)
    kb = k * beta[..., None]
    m = jnp.where(strict, jnp.einsum('nbhcd,nbhsd->nbhcs', kb, k) * decay, 0.0)
    rhs = jnp.concatenate([v * beta[..., None], kb * jnp.exp(gc)[..., None]], axis=-1)
    sol = lax.linalg.triangular_solve(m + jnp.eye(c, dtype=F32), rhs, left_side=True, lower=True)
    u, w = sol[..., :dv], sol[..., dv:]
    attn = jnp.einsum('nbhcd,nbhsd->nbhcs', q, k) * decay
    g_last = gc[..., -1]
    q_dec = q * jnp.exp(gc)[..., None]
    k_dec = k * jnp.exp(g_last[..., None] - gc)[..., None]

    def step(state, xs):
        u_c, w_c, q_c, k_c, a_c, gl = xs
        v_new = u_c - jnp.einsum('bhcd,bhde->bhce', w_c, state)
        o = jnp.einsum('bhcd,bhde->bhce', q_c, state) + jnp.einsum('bhcs,bhse->bhce', a_c, v_new)
        state = state * jnp.exp(gl)[..., None, None] + jnp.einsum('bhcd,bhce->bhde', k_c, v_new)
        return state, o

    s0 = jnp.zeros((bsz, h, dk, dv), F32)
    _, o = lax.scan(step, s0, (u, w, q_dec, k_dec, attn, g_last))
    return jnp.moveaxis(o, (0, 2), (1, 3)).reshape(bsz, s, h, dv)

def moba_attention(q, k, v, rel_bias):
    bsz, s, h, dh = q.shape
    mb, qbs = MOBA_BLOCK, MOBA_QBLOCK
    nblk = -(-s // mb)
    sp = nblk * mb
    nq = sp // qbs
    topk = min(MOBA_TOPK, nblk - 1)
    scale = dh ** -0.5

    def prep(t):
        t = jnp.pad(t, ((0, 0), (0, sp - s), (0, 0), (0, 0)))
        return jnp.transpose(t, (0, 2, 1, 3))

    q, k, v = prep(q), prep(k), prep(v)
    kblk = k.reshape(bsz, h, nblk, mb, dh)
    vblk = v.reshape(bsz, h, nblk, mb, dh)
    kmean = jnp.mean(kblk.astype(F32), axis=3)
    qch = jnp.moveaxis(q.reshape(bsz, h, nq, qbs, dh), 2, 0)
    table = rel_bias.T.astype(F32)
    bi = jnp.arange(bsz)[:, None, None, None]
    hi = jnp.arange(h)[None, :, None, None]

    def one_block(args):
        ci, qi = args
        qpos = ci * qbs + jnp.arange(qbs)
        own = (ci * qbs) // mb
        k_own = lax.dynamic_index_in_dim(kblk, own, axis=2, keepdims=False)
        v_own = lax.dynamic_index_in_dim(vblk, own, axis=2, keepdims=False)
        dist_own = qpos[:, None] - (own * mb + jnp.arange(mb))[None, :]
        s_own = jnp.einsum('bhqd,bhtd->bhqt', qi, k_own).astype(F32) * scale + table[:, rel_bucket(dist_own)]
        s_own = jnp.where(dist_own >= 0, s_own, NEG)
        if topk == 0:
            p_own = jax.nn.softmax(s_own, axis=-1).astype(v_own.dtype)
            return jnp.einsum('bhqt,bhtd->bhqd', p_own, v_own)
        gate = jnp.einsum('bhqd,bhnd->bhqn', qi.astype(F32), kmean)
        gate = jnp.where(jnp.arange(nblk) < own, gate, NEG)
        _, idx = lax.top_k(gate, topk)
        kg = kblk[bi, hi, idx]
        vg = vblk[bi, hi, idx]
        dist_sel = qpos[None, None, :, None, None] - (idx[..., None] * mb + jnp.arange(mb))
        s_sel = (jnp.einsum('bhqd,bhqjtd->bhqjt', qi, kg).astype(F32) * scale
                 + table[hi[..., None], rel_bucket(dist_sel)])
        s_sel = jnp.where((idx < own)[..., None], s_sel, NEG).reshape(bsz, h, qbs, topk * mb)
        p = jax.nn.softmax(jnp.concatenate([s_sel, s_own], axis=-1), axis=-1).astype(v.dtype)
        p_sel = p[..., :topk * mb].reshape(bsz, h, qbs, topk, mb)
        p_own = p[..., topk * mb:]
        return jnp.einsum('bhqjt,bhqjtd->bhqd', p_sel, vg) + jnp.einsum('bhqt,bhtd->bhqd', p_own, v_own)

    out = lax.map(one_block, (jnp.arange(nq), qch))
    out = jnp.moveaxis(out, 0, 2).reshape(bsz, h, sp, dh)[:, :, :s]
    return jnp.transpose(out, (0, 2, 1, 3)).reshape(bsz, s, h * dh)

def ab_mixer(h, w_in, w_out, conv_w, conv_b, dt_bias, a_log, d_skip, norm_w, sinks, rel_bias):
    bsz, s, _ = h.shape
    proj = h @ w_in
    z, xbc, dt_raw, q, k, v = jnp.split(proj, AB_SPLITS, axis=-1)
    y_a = mamba2_ssd_mixer(z, xbc, dt_raw, conv_w, conv_b, dt_bias, a_log, d_skip, norm_w)
    y_b = swa_sink_attention(q.reshape(bsz, s, N_ATTN_HEADS, ATTN_HEAD_DIM),
                             k.reshape(bsz, s, SWA_KV_HEADS, ATTN_HEAD_DIM),
                             v.reshape(bsz, s, SWA_KV_HEADS, ATTN_HEAD_DIM), sinks, rel_bias)
    return jnp.concatenate([y_a, y_b.astype(h.dtype)], axis=-1) @ w_out

def cd_mixer(h, w_in, w_out, conv_w, dt_bias, a_log, norm_w, rel_bias):
    bsz, s, _ = h.shape
    proj = h @ w_in
    qkv, z, b_raw, a_raw, qd, kd, vd = jnp.split(proj, CD_SPLITS, axis=-1)
    qkv = jax.nn.silu(causal_dwconv(qkv, conv_w))
    qc, kc, vc = jnp.split(qkv, 3, axis=-1)
    hd = (bsz, s, GDN_HEADS, GDN_HEAD_DIM)
    beta = jax.nn.sigmoid(b_raw.astype(F32))
    g = -jnp.exp(a_log.astype(F32)) * jax.nn.softplus(a_raw.astype(F32) + dt_bias.astype(F32))
    o = gated_delta_rule(l2norm(qc.reshape(hd)), l2norm(kc.reshape(hd)), vc.reshape(hd), g, beta)
    o = _rms(o) * norm_w.astype(F32) * jax.nn.silu(z.astype(F32).reshape(hd))
    y_c = o.reshape(bsz, s, GDN_INNER).astype(h.dtype)
    ad = (bsz, s, N_ATTN_HEADS, ATTN_HEAD_DIM)
    y_d = moba_attention(qd.reshape(ad), kd.reshape(ad), vd.reshape(ad), rel_bias)
    return jnp.concatenate([y_c, y_d.astype(h.dtype)], axis=-1) @ w_out

def conv_ffn(h, w_up, conv_w, conv_b, w_down):
    u = causal_dwconv(h @ w_up, conv_w, conv_b)
    gate, val = jnp.split(u, 2, axis=-1)
    return (jax.nn.gelu(gate, approximate=True) * val) @ w_down

def setup_inputs(seed: int = 0) -> dict:
    key = jax.random.key(seed)
    ks = iter(jax.random.split(key, 32))

    def nrm(shape, scale):
        return jax.random.normal(next(ks), shape, F32) * scale

    def gain(shape):
        return 1.0 + 0.05 * jax.random.normal(next(ks), shape, F32)

    def dt_bias(shape):
        dt = jnp.exp(jax.random.uniform(next(ks), shape, F32, math.log(1e-3), math.log(1e-1)))
        return dt + jnp.log(-jnp.expm1(-dt))

    def a_log(shape):
        return jnp.log(jax.random.uniform(next(ks), shape, F32, 1.0, 16.0))

    return {
        'x': nrm((BATCH, SEQ, D_MODEL), 1.0),
        'c': nrm((BATCH, D_MODEL), 1.0),
        'rel_bias': nrm((REL_BUCKETS, N_ATTN_HEADS), 0.3),
        'norm_w': gain((DEPTH, 4, D_MODEL)),
        'ada_w': nrm((DEPTH, D_MODEL, 6 * D_MODEL), D_MODEL ** -0.5),
        'ada_b': nrm((DEPTH, 6 * D_MODEL), 0.01),
        'ab_w_in': nrm((N_EVEN, D_MODEL, AB_COLS), D_MODEL ** -0.5),
        'ab_w_out': nrm((N_EVEN, MIX_WIDTH, D_MODEL), MIX_WIDTH ** -0.5),
        'ssd_conv_w': nrm((N_EVEN, SSD_CONV, SSD_XBC), SSD_CONV ** -0.5),
        'ssd_conv_b': nrm((N_EVEN, SSD_XBC), 0.01),
        'ssd_dt_bias': dt_bias((N_EVEN, SSD_HEADS)),
        'ssd_a_log': a_log((N_EVEN, SSD_HEADS)),
        'ssd_d': gain((N_EVEN, SSD_HEADS)),
        'ssd_norm_w': gain((N_EVEN, SSD_INNER)),
        'swa_sinks': nrm((N_EVEN, N_ATTN_HEADS), 0.5),
        'cd_w_in': nrm((N_ODD, D_MODEL, CD_COLS), D_MODEL ** -0.5),
        'cd_w_out': nrm((N_ODD, MIX_WIDTH, D_MODEL), MIX_WIDTH ** -0.5),
        'gdn_conv_w': nrm((N_ODD, GDN_CONV, 3 * GDN_INNER), GDN_CONV ** -0.5),
        'gdn_dt_bias': dt_bias((N_ODD, GDN_HEADS)),
        'gdn_a_log': a_log((N_ODD, GDN_HEADS)),
        'gdn_norm_w': gain((N_ODD, GDN_HEAD_DIM)),
        'ffn_w_up': nrm((DEPTH, D_MODEL, 2 * FFN_DIM), D_MODEL ** -0.5),
        'ffn_conv_w': nrm((DEPTH, FFN_CONV, 2 * FFN_DIM), FFN_CONV ** -0.5),
        'ffn_conv_b': nrm((DEPTH, 2 * FFN_DIM), 0.01),
        'ffn_w_down': nrm((DEPTH, FFN_DIM, D_MODEL), FFN_DIM ** -0.5),
    }

def reference(x, c, rel_bias, norm_w, ada_w, ada_b, ab_w_in, ab_w_out, ssd_conv_w, ssd_conv_b,
              ssd_dt_bias, ssd_a_log, ssd_d, ssd_norm_w, swa_sinks, cd_w_in, cd_w_out, gdn_conv_w,
              gdn_dt_bias, gdn_a_log, gdn_norm_w, ffn_w_up, ffn_conv_w, ffn_conv_b, ffn_w_down):
    mods = jnp.einsum('bd,lde->lbe', jax.nn.silu(c), ada_w) + ada_b[:, None, :]
    for i in range(DEPTH):
        sh_m, sc_m, g_m, sh_f, sc_f, g_f = jnp.split(mods[i][:, None, :].astype(x.dtype), 6, axis=-1)
        h = rms_norm(x, norm_w[i, 0]) * (1 + sc_m) + sh_m
        if i % 2 == 0:
            j = i // 2
            y = ab_mixer(h, ab_w_in[j], ab_w_out[j], ssd_conv_w[j], ssd_conv_b[j], ssd_dt_bias[j],
                         ssd_a_log[j], ssd_d[j], ssd_norm_w[j], swa_sinks[j], rel_bias)
        else:
            j = i // 2
            y = cd_mixer(h, cd_w_in[j], cd_w_out[j], gdn_conv_w[j], gdn_dt_bias[j], gdn_a_log[j],
                         gdn_norm_w[j], rel_bias)
        x = x + g_m * rms_norm(y, norm_w[i, 1])
        h = rms_norm(x, norm_w[i, 2]) * (1 + sc_f) + sh_f
        y = conv_ffn(h, ffn_w_up[i], ffn_conv_w[i], ffn_conv_b[i], ffn_w_down[i])
        x = x + g_f * rms_norm(y, norm_w[i, 3])
    return x


_drawn_inputs = setup_inputs


def setup_inputs(seed=0):
    import zlib

    import numpy as np

    out = dict(_drawn_inputs(seed))
    spreads = {}
    factors = {'ssd_conv_b': 8.0,
     'ssd_d': 7.578,
     'swa_sinks': 7.823,
     'gdn_norm_w': 3.25,
     'ffn_conv_b': 8.0}
    for name, (base, spread) in spreads.items():
        noise = np.random.default_rng([zlib.crc32(name.encode()), seed]).standard_normal(out[name].shape)
        drawn = base * np.exp(spread * noise) if base else spread * noise
        out[name] = jnp.asarray(drawn.astype(out[name].dtype))
    for name, factor in factors.items():
        out[name] = (out[name] * factor).astype(out[name].dtype)
    return out
```

```python
from contextlib import ExitStack

import numpy as np

import concourse.bass as bass
from concourse import mybir

F32 = mybir.dt.float32
F32R = mybir.dt.float32r
ACT = mybir.ActivationFunctionType
ALU = mybir.AluOpType
AX = mybir.AxisListType
ds = bass.ds

P = 128
D_MODEL, SEQ = 1024, 256
DT = D_MODEL // P
NB = SEQ // P
AH, AD = 8, 64
SSD_H, SSD_P, SSD_G = 24, 64, 4
HPG = SSD_H // SSD_G
GH, GD, GC = 12, 128, 64
FT = 2816 // P
NEG = -1e30
EPS_COL = 1e-6

XBC_T, ZT, GQ_T, MIX_T = 20, 12, 36, 16


def layout():
    parts, n = {}, 0
    for name, count in (("dt0", 1), ("conv0", XBC_T), ("q0", 4), ("k0", 1), ("v0", 1), ("z0", ZT), ("out0", MIX_T),
                        ("up0", 2 * FT), ("down0", FT), ("dt1", 1), ("conv1", GQ_T), ("q1", 4), ("k1", 4), ("v1", 4),
                        ("z1", ZT), ("out1", MIX_T), ("up1", 2 * FT), ("down1", FT)):
        parts[name] = (n, count)
        n += count
    return parts, n


PARTS, UNITS = layout()
ADA_UNITS = 2 * 6 * DT

PRM, PRM_COLS = {}, 0
for _name, _rows in (("c", 8), ("ada_b", 96), ("norm", 64), ("conv0_w", 80), ("conv0_b", 20), ("ssd_norm", 12),
                     ("conv1_w", 144), ("gdn_norm", 1), ("up_w", 264), ("up_b", 88)):
    PRM[_name] = PRM_COLS
    PRM_COLS += _rows
PRM_G = -(-PRM_COLS // P)

ROW = {"dt_bias0": 0, "a_log0": 24, "d": 48, "sinks": 72, "dt_bias1": 80, "a_log1": 92}
ROW_COLS = 104

LEVELS = 6
CST, CST_COLS = {}, 0
for _name, _n in (("ident", 128), ("ones", 128), ("triu", 128), ("triu_chunk", 128), ("same_chunk", 128), ("chunk0", 128),
                  ("chunk1", 128), ("reverse", 128), ("keep", 128), ("keep_chunk", 64), ("level", LEVELS * 64),
                  ("ident_chunk", 64), ("eps", 1)):
    CST[_name] = CST_COLS
    CST_COLS += _n


def constants():
    c = np.zeros((P, CST_COLS), np.float32)
    p, f = np.arange(P)[:, None], np.arange(P)[None, :]
    put = lambda name, v: c.__setitem__((slice(None), slice(CST[name], CST[name] + v.shape[1])), v)
    put("ident", np.eye(P))
    put("ones", np.ones((P, P)))
    put("triu", p <= f)
    put("triu_chunk", (p <= f) & (p // GC == f // GC))
    put("same_chunk", p // GC == f // GC)
    put("chunk0", (p // GC == 0) & (f >= 0))
    put("chunk1", (p // GC == 1) & (f >= 0))
    put("reverse", p + f == P - 1)
    put("keep", np.where(f >= p, -NEG, NEG))
    s, t = p % GC, np.arange(GC)[None, :]
    put("keep_chunk", np.where(t >= s, -NEG, NEG))
    for lv in range(LEVELS):
        b = 1 << lv
        m = (s // (2 * b) == t // (2 * b)) & (s // b % 2 == 0) & (t // b % 2 == 1)
        c[:, CST["level"] + lv * GC:CST["level"] + (lv + 1) * GC] = m
    put("ident_chunk", s == t)
    put("eps", np.full((P, 1), EPS_COL))
    return c


def bucket_rows():
    starts = [0, 1, 2, 3, 4, 5, 6, 7, 8, 9, 10, 11, 12, 13, 14, 15, 16, 21, 27, 35, 46, 59, 77, 99, 128, 166, 216]
    r = np.zeros((33, 2, 384), np.float32)
    for v in range(2):
        for i in range(384):
            dist = 255 - i
            if dist < 0 or (v == 0 and dist >= 128):
                r[32, v, i] = NEG
            else:
                r[sum(dist >= s for s in starts) - 1, v, i] = 1
    return r


def build(nc, w_dram, ada_dram, x_dram, prm_dram, row_dram, cst_dram, bucket_dram, rel_dram, scratch, out_dram):
    with ExitStack() as ctx:
        sem = lambda name: ctx.enter_context(nc.semaphore(name))
        cursor = [-(-nc.sbuf_base // 32) * 32]

        def sb(name, shape, dt=F32, at=None):
            size = int(np.prod(shape[1:])) * 4
            off = cursor[0] if at is None else at
            t = nc.alloc_sbuf_tensor_at(name, [P] + list(shape[1:]), dt, offset=off)
            if at is None:
                cursor[0] += -(-size // 32) * 32
            return t

        def region(size):
            at = -(-cursor[0] // 32) * 32
            cursor[0] = at + size
            return at

        KB = 1024
        x = sb("x", [P, DT, SEQ])
        h_hi = sb("h_hi", [P, DT, SEQ], F32R)
        h_lo = sb("h_lo", [P, DT, SEQ], F32R)
        raw = sb("raw", [P, 4, 8, P])
        w_hi = sb("w_hi", [P, 4, 4, P], F32R)
        w_lo = sb("w_lo", [P, 4, 4, P], F32R)
        ada_w = sb("ada_w", [P, 2, 8, P])
        cst = sb("cst", [P, CST_COLS])
        prm = sb("prm", [P, PRM_G * P])
        rows = sb("rows", [P, ROW_COLS])
        mods = sb("mods", [P, 2, 6, DT])
        gain = sb("gain", [P, 2, 4, DT])
        c_silu = sb("c_silu", [P, DT])
        small = sb("small", [P, 28, 48])
        at_hi, at_lo = region(22 * KB), region(22 * KB)
        a_hi = sb("a_hi", [P, 22, SEQ], F32R, at=at_hi)
        a_lo = sb("a_lo", [P, 22, SEQ], F32R, at=at_lo)
        arena = region(78 * KB)
        assert cursor[0] <= nc.sbuf_usable_end, (cursor[0], nc.sbuf_usable_end)
        conv0 = sb("conv0", [P, XBC_T, SEQ], at=arena)
        conv1 = sb("conv1", [P, GQ_T, SEQ], at=arena)
        convs = (conv0, conv1)
        zs = sb("zs", [P, ZT, SEQ], at=arena + 36 * KB)
        sq = sb("sq", [P, DT, SEQ], at=arena)
        yr = sb("yr", [P, DT, SEQ], at=arena + 8 * KB)
        rn = sb("rn", [P, 2, SEQ], at=arena + 16 * KB)
        yg = sb("yg", [P, 2, SEQ], at=arena + 24 * KB)
        yv = sb("yv", [P, 2, SEQ], at=arena + 26 * KB)
        prod = sb("prod", [P, 2, SEQ], at=arena + 28 * KB)
        prm_rows = sb("prm_rows", [P, PRM_G, P], at=arena + 30 * KB)
        bucket = sb("bucket", [P, 2, 384], at=arena + 34 * KB)
        rel = sb("rel", [P, 8], at=arena + 37 * KB)
        bias_vec = sb("bias_vec", [P, 2, 384], at=arena + 38 * KB)
        scores = sb("scores", [P, AH, 384], at=at_hi)
        probs_t = sb("probs_t", [P, 2, 384], at=at_hi + 12 * KB)
        att_q = sb("att_q", [P, 4, SEQ], at=at_lo)
        att_k = sb("att_k", [P, 4, SEQ], at=at_lo + 4 * KB)
        att_v = sb("att_v", [P, NB, 512], at=at_lo + 8 * KB)
        bias = sb("bias", [P, AH, SEQ], at=arena + 48 * KB)
        hankel = sb("hankel", [P, AH, SEQ], at=arena + 56 * KB)
        xs_tok = sb("xs_tok", [P, NB, 1536], at=arena + 20 * KB)
        b_tok = sb("b_tok", [P, SSD_G, P], at=arena + 32 * KB)
        cb = sb("cb", [P, NB, SSD_G, P], at=arena + 48 * KB)
        h_in = sb("h_in", [P, 1536], at=arena + 52 * KB)
        xd = sb("xd", [P, 1536], at=arena + 58 * KB)
        lmat = sb("lmat", [P, 2, 4, P], at=arena + 64 * KB)
        mmat = sb("mmat", [P, 2, 4, P], at=arena + 68 * KB)
        cexp = sb("cexp", [P, 2, 4, P], at=arena + 72 * KB)
        y_ssd = sb("y_ssd", [P, ZT, SEQ], at=at_lo)
        y_sq = sb("y_sq", [P, 2, 3, SEQ], at=arena + 64 * KB)
        y_rn = sb("y_rn", [P, SSD_G, SEQ], at=arena + 70 * KB)
        y_mix = sb("y_mix", [P, ZT, SEQ], at=arena)
        NS = NB * GH
        v_tok = sb("v_tok", [P, NB, GH, GD], at=arena + 48 * KB)
        k_tok = sb("k_tok", [P, NB, GH, GD], at=arena + 24 * KB)
        attn_t = sb("attn_t", [P, NS, GC], at=arena + 60 * KB)
        inv_t = sb("inv_t", [P, NS, GC], at=arena + 66 * KB)
        state = sb("state", [P, GH, GD], at=arena + 72 * KB)
        dec = sb("dec", [P, NS, GC], at=at_hi)
        sys_t = sb("sys_t", [P, NS, GC], at=at_hi + 6 * KB)
        inv = sb("inv", [P, NS, GC], at=at_hi + 12 * KB)
        egc = sb("egc", [P, NS, P], at=at_lo)
        step_y = sb("step_y", [P, NS, GC], at=at_lo + 12 * KB)
        off_t = sb("off_t", [P, NS, GC], at=arena + 72 * KB)
        g_sq = sb("g_sq", [P, 2, 2, SEQ], at=at_hi)
        g_rn = sb("g_rn", [P, 2, 2, SEQ], at=at_hi + 4 * KB)
        resid = sb("resid", [P, 2, 4, GD], at=at_hi + 8 * KB)
        v_new = sb("v_new", [P, 3, 4, GD], at=at_hi + 12 * KB)
        o_sq = sb("o_sq", [P, 2, 2, SEQ], at=arena + 48 * KB)
        o_rn = sb("o_rn", [P, 2, 2, SEQ], at=arena + 52 * KB)
        o_t = sb("o_t", [P, 2, 2, SEQ], at=arena + 56 * KB)

        PB = [ctx.enter_context(nc.psum_tensor(f"proj{i}", [P, 512], F32)) for i in range(4)]
        AB = [ctx.enter_context(nc.psum_tensor(f"acc{i}", [P, 512], F32)) for i in range(4)]
        BANKS = PB + AB
        ada_ps = AB[3]

        def C(name, a=0, n=None, p0=0, p1=P):
            n = n or 128
            return cst[p0:p1, CST[name] + a:CST[name] + a + n]

        EPS = cst[:, CST["eps"]:CST["eps"] + 1]
        acc = lambda k: AB[k // 2][:, (k % 2) * SEQ:(k % 2 + 1) * SEQ]
        tile_at = lambda k: k if k < 12 else k + 6

        in_landed = [sem(f"in_landed{i}") for i in range(5)]
        bias_vec_stored, hankel_landed, out_stored = sem("bias_vec_stored"), sem("hankel_landed"), sem("out_stored")
        w_landed = [sem(f"w_landed{i}") for i in range(4)]
        ada_landed = [sem(f"ada_landed{i}") for i in range(2)]
        w_rounded, w_split, w_used = sem("w_rounded"), sem("w_split"), sem("w_used")
        ada_used, mods_read = sem("ada_used"), sem("mods_read")
        act_step, dve_step = sem("act_step"), sem("dve_step")
        rel_ones, prm_turned, prm_ready, c_ready = (sem(n) for n in ("rel_ones", "prm_turned", "prm_ready", "c_ready"))
        vec_mm, vec_copied, hankel_mm, bias_ready = (sem(n) for n in ("vec_mm", "vec_copied", "hankel_mm", "bias_ready"))
        squares, sums, roots, scaled, h_rounded, h_ready, x_ready = (
            sem(n) for n in ("squares", "sums", "roots", "scaled", "h_rounded", "h_ready", "x_ready"))
        dt_read, conv_first, conv_taps, conv_done = (sem(n) for n in ("dt_read", "conv_first", "conv_taps", "conv_done"))
        copied = sem("copied")
        up_first, up_taps, gelu_done, prod_done, g_rounded, g_ready = (
            sem(n) for n in ("up_first", "up_taps", "gelu_done", "prod_done", "g_rounded", "g_ready"))
        s_scored, s_biased, s_max, s_exp, s_norm = (sem(n) for n in ("s_scored", "s_biased", "s_max", "s_exp", "s_norm"))
        s_turned, s_copied, s_out, s_rounded, s_ready = (
            sem(n) for n in ("s_turned", "s_copied", "s_out", "s_rounded", "s_ready"))
        gate_abs, gate_exp, gate_ln, gate_ready = (sem(n) for n in ("gate_abs", "gate_exp", "gate_ln", "gate_ready"))
        d_turned, d_tok, d_cum_mm, d_cum, d_tail, d_xd = (sem(n) for n in ("ssd_turned", "ssd_tok", "ssd_cum_mm", "ssd_cum", "ssd_tail", "ssd_xd"))
        d_cb_mm, d_cb, d_state_mm, d_state = (sem(n) for n in ("ssd_cb_mm", "ssd_cb", "ssd_state_mm", "ssd_state"))
        d_decay_mm, d_diff, d_decay, d_mmat, d_y_mm, d_y = (
            sem(n) for n in ("ssd_decay_mm", "ssd_diff", "ssd_decay", "ssd_mmat", "ssd_y_mm", "ssd_y"))
        d_gated, d_sq, d_sum, d_root, d_mix, d_rounded, mix_ready = (
            sem(n) for n in ("ssd_gated", "ssd_sq", "ssd_sum", "ssd_root", "ssd_mix", "ssd_rounded", "mix_ready"))
        n_sq, n_sum, n_root, n_unit = (sem(n) for n in ("l2_sq", "l2_sum", "l2_root", "l2_unit"))
        v_turned, v_copied, k_turned, k_copied = (sem(n) for n in ("v_turned", "v_copied", "k_turned", "k_copied"))
        g_cum_mm, g_cum, g_tail, g_tot = (sem(n) for n in ("gdn_cum_mm", "gdn_cum", "gdn_tail", "gdn_total"))
        g_decay_mm, g_diff, g_decay, g_gram_mm, g_gram = (
            sem(n) for n in ("gdn_decay_mm", "gdn_diff", "gdn_decay", "gdn_gram_mm", "gdn_gram"))
        i_off, i_y_mm, i_y, i_z_mm, i_zt_mm, i_inv = (
            sem(n) for n in ("inv_off", "inv_y_mm", "inv_y", "inv_z_mm", "inv_zt_mm", "inv_done"))
        g_scaled = sem("gdn_scaled")
        c_ks_mm, c_resid, c_tr_mm, c_vnew, c_o_mm, c_o, c_u_mm, c_state = (
            sem(n) for n in ("scan_ks_mm", "scan_resid", "scan_tr_mm", "scan_vnew", "scan_o_mm", "scan_o", "scan_u_mm", "scan_state"))
        o_sqd, o_sum, o_root, o_mixed, o_rounded = (sem(n) for n in ("o_sqd", "o_sum", "o_root", "o_mixed", "o_rounded"))

        freed = {}
        totals = {}
        for name, (n0, cnt) in PARTS.items():
            key = {"dt": (dt_read, 1), "conv": (conv_taps, 3), "up": (up_taps, 2)}.get(name[:-1], (copied, 1))
            if name[:-1] in ("out", "down"):
                continue
            for n in range(n0, n0 + cnt):
                at = totals.get(name[:-1] if key[1] > 1 else str(key[0]), 0) + key[1]
                totals[name[:-1] if key[1] > 1 else str(key[0])] = at
                freed[n] = (key[0], at, key[1])

        def units(e, name, step):
            cnt = PARTS[name][1]
            for k in range(min(4, cnt)):
                step(k, 0, k)
            groups = max(cnt - 4, 0) // 4 - (name[:-1] == "out")
            if groups > 0:
                with e.Fori(0, groups) as i:
                    for j in range(4, 8):
                        step(4 * i + j, i, j)
            for k in range(4 + 4 * max(groups, 0), cnt):
                step(k, 0, k)

        def w_half(n, a):
            s = (2 * n + a) % 4
            return w_hi[:, s], w_lo[:, s], raw[:, n % 4, 4 * a:4 * a + 4]

        names = {}

        def S(name, a=0, n=48, p0=0, p1=P):
            names.setdefault(name, len(names))
            assert len(names) <= 28
            return small[p0:p1, names[name], a:a + n]

        def bc(ap, *shape):
            return ap.broadcast_to(list(shape))

        def one(ap):
            return ap.rearrange("p (a t) -> p a t", a=1)

        last_copy = {q: freed[PARTS[q][0] + PARTS[q][1] - 1][1] for q in ("v0", "z0", "v1", "z1")}
        SCAN = [(c, g) for c in range(SEQ // GC) for g in range(GH // 4)]
        block = ctx.enter_context(nc.Block())

        @block.sync
        def _(sp):
            def load_w(n, i=0):
                if n >= 4:
                    sp.wait_ge(w_split, 8 * i + 2 * n - 6)
                sp.dma_start(raw[:, n % 4].rearrange("p (o a) b -> p o (a b)", o=1),
                             w_dram[:, ds(4 * i + n, 1), :]).then_inc(w_landed[n % 4], 16)

            def load_ada(m, i=0):
                if m >= 2:
                    sp.wait_ge(ada_used, 4 * i + m - 1)
                sp.dma_start(ada_w[:, m % 2].rearrange("p (o a) b -> p o (a b)", o=1),
                             ada_dram[:, ds(4 * i + m, 1), :]).then_inc(ada_landed[m % 2], 16)

            def stream(n0, cnt, ada0=None):
                with sp.Fori(0, cnt // 4) as i:
                    for j in range(4):
                        load_w(n0 + j, i)
                        if ada0 is not None:
                            load_ada(ada0 + j, i)
                for n in range(n0 + cnt // 4 * 4, n0 + cnt):
                    load_w(n)

            def hankel_load(v):
                src = bass.AP(tensor=scratch.tensor, offset=v * 384, ap=[[1, P], [768, AH], [1, SEQ]])
                sp.dma_start(hankel[:, :, :], src).then_inc(hankel_landed, 16)

            sp.dma_start(prm_rows[:, :, :], prm_dram).then_inc(in_landed[0], 16)
            sp.dma_start(cst[:, :], cst_dram).then_inc(in_landed[1], 16)
            load_ada(0)
            load_ada(1)
            sp.dma_start(x[:, :, :], x_dram).then_inc(in_landed[2], 16)
            sp.dma_start(rows[:, :], row_dram.broadcast_to([P, ROW_COLS])).then_inc(in_landed[3], 16)
            sp.dma_start(bucket[0:33, :, :], bucket_dram).then_inc(in_landed[4], 16)
            sp.dma_start(rel[0:32, :], rel_dram).then_inc(in_landed[4], 16)
            for n in range(4):
                load_w(n)
            for m in range(2, 16):
                load_ada(m)
            sp.wait_ge(vec_copied, 1)
            sp.dma_start(scratch, bias_vec[0:AH, :, :]).then_inc(bias_vec_stored, 16)
            load_w(4)
            load_ada(16)
            sp.wait_ge(bias_vec_stored, 16)
            hankel_load(0)
            for k in range(1, 4):
                load_w(4 + k)
                load_ada(16 + k)
            n_z, n_out, n_up, n_q1 = PARTS["z0"][0] + 3, PARTS["out0"][0] + 3, PARTS["up0"][0] + 3, PARTS["q1"][0]
            stream(8, XBC_T - 4, 20)
            stream(4 + XBC_T, n_z - 4 - XBC_T)
            stream(n_z, ZT, 36)
            for m in range(48, 52):
                load_ada(m)
            stream(n_out, n_up - n_out)
            stream(n_up, 2 * FT, 52)
            stream(n_up + 2 * FT, n_q1 - n_up - 2 * FT)
            sp.wait_ge(x_ready, 2 * DT)
            hankel_load(1)
            stream(n_q1, UNITS - n_q1)
            sp.wait_ge(x_ready, 4 * DT)
            sp.dma_start(out_dram, x[:, :, :]).then_inc(out_stored, 16)
            sp.wait_ge(out_stored, 16)

        @block.tensor
        def _(pe):
            def mm(out, a, b, start=True, stop=True):
                return pe.matmul(out, a, b, start=start, stop=stop, skip_group_check=True)

            def ada_unit(m, i=0):
                pe.wait_ge(ada_landed[m % 2], 32 * i + 16 * (m // 2 + 1))
                for k in range(8):
                    last = mm(AB[3][:, ds(4 * i + m, 1)], ada_w[:, m % 2, k], c_silu[:, k:k + 1], k == 0, k == 7)
                last.then_inc(ada_used, 1)

            def project(name, ada0=None, token=False, norm=None):
                n0 = PARTS[name][0]

                def step(k, i, j):
                    n = n0 + j
                    if n - 4 in freed:
                        s, at, per = freed[n - 4]
                        pe.wait_ge(s, 4 * per * i + at)
                    for a in range(2):
                        if norm is not None and j == 0:
                            pe.wait_ge(h_ready, 8 * norm + 4 * a + 4)
                        pe.wait_ge(w_split, 8 * i + 2 * n + a + 1)
                        hi, lo, _ = w_half(n, a)
                        for q in range(4):
                            t = 4 * a + q
                            for p_, (u, v) in enumerate(((hi, h_hi), (hi, h_lo), (lo, h_hi))):
                                st, en = t == 0 and p_ == 0, t == 7 and p_ == 2
                                if token:
                                    for b in range(NB):
                                        c = slice(b * P, b * P + P)
                                        last = mm(PB[n % 4][:, c], v[:, t, c], u[:, q], st and b == 0, en)
                                else:
                                    last = mm(PB[n % 4][:, 0:SEQ], u[:, q], v[:, t], st, en)
                        last.then_inc(w_used, 1)
                    if ada0 is not None:
                        ada_unit(ada0 + j, i)

                units(pe, name, step)

            def accumulate(name, ready, first_ready, at):
                n0, cnt = PARTS[name]

                def step(k, i, j):
                    n = n0 + j
                    if ready is not None:
                        pe.wait_ge(ready, first_ready + k + 1)
                    for a in range(2):
                        pe.wait_ge(w_split, 8 * i + 2 * n + a + 1)
                        hi, lo, _ = w_half(n, a)
                        for q in range(4):
                            t = 4 * a + q
                            s = at(k)
                            for p_, (u, v) in enumerate(((hi, a_hi), (hi, a_lo), (lo, a_hi))):
                                last = mm(acc(t), u[:, q], v[:, ds(s, 1), :], j == 0 and p_ == 0 and t % 2 == 0,
                                          j == cnt - 1 and p_ == 2)
                        last.then_inc(w_used, 1)

                units(pe, name, step)

            def sum_squares(event):
                for k in range(DT):
                    pe.wait_ge(squares, event * DT + k + 1)
                    last = mm(PB[0][:, 0:SEQ], C("ones"), sq[:, k], k == 0, k == DT - 1)
                last.then_inc(sums, 1)

            def bias_tiles(layer):
                pe.wait_ge(hankel_landed, 16 * (layer + 1))
                for q in range(4):
                    last = mm(AB[q][:, :], C("reverse"), hankel[:, 2 * q:2 * q + 2, :])
                last.then_inc(hankel_mm, 1)

            def attention(layer):
                n8 = AH * layer
                pe.wait_ge(bias_ready, layer + 1)
                pe.wait_ge(copied, last_copy[f"v{layer}"])
                for h in range(AH):
                    p0, t = AD * (h % 2), h // 2
                    q_, k_ = att_q[p0:p0 + AD, t], att_k[p0:p0 + AD, t if layer else h // 4]
                    if h >= 4:
                        pe.wait_ge(s_biased, 2 * (n8 + h - 3))
                    mm(AB[h % 4][:, 0:SEQ], q_[:, P:2 * P], k_[:, 0:SEQ])
                    mm(AB[h % 4][:, SEQ:SEQ + P], q_[:, 0:P], k_[:, 0:P]).then_inc(s_scored, 1)

                def values(h):
                    p0, t = AD * (h % 2), h // 2
                    c0 = AD * (h if layer else h // 4)
                    o, pt = PB[t][p0:p0 + AD], probs_t[:, h % 2]
                    pe.wait_ge(s_copied, n8 + h + 1)
                    mm(o[:, 0:P], att_v[:, 0, c0:c0 + AD], pt[:, 2 * P:3 * P])
                    mm(o[:, P:2 * P], att_v[:, 0, c0:c0 + AD], pt[:, 0:P], True, False)
                    mm(o[:, P:2 * P], att_v[:, 1, c0:c0 + AD], pt[:, P:2 * P], False, True).then_inc(s_out, 1)

                for h in range(AH):
                    pe.wait_ge(s_norm, n8 + h + 1)
                    if h >= 4:
                        pe.wait_ge(s_copied, n8 + h - 3)
                    for b in range(3):
                        last = pe.transpose(AB[h % 4][:, b * P:b * P + P], scores[:, h, b * P:b * P + P], C("ident"))
                    last.then_inc(s_turned, 1)
                    if h:
                        values(h - 1)
                values(AH - 1)
                pe.wait_ge(s_ready, 4 * (layer + 1))

            def ssd_outputs(n):
                b, h0 = n // 6, 4 * (n % 6)
                pe.wait_ge(d_mmat, n + 1)
                if n >= 4:
                    pe.wait_ge(d_y, n - 3)
                for q in range(4):
                    h = h0 + q
                    p0 = SSD_P * (h % 2)
                    o, f = AB[n % 4][p0:p0 + SSD_P, (q // 2) * P:(q // 2 + 1) * P], slice(SSD_P * h, SSD_P * h + SSD_P)
                    last = mm(o, xs_tok[:, b, f], mmat[:, n % 2, q], True, b == 0)
                    if b:
                        last = mm(o, h_in[:, f], cexp[:, n % 2, q], False, True)
                last.then_inc(d_y_mm, 1)

            def ssd():
                pe.wait_ge(conv_done, XBC_T)
                pe.wait_ge(copied, last_copy["z0"])
                pe.wait_ge(mods_read, 3)
                for n in range(7):
                    if n >= 4:
                        pe.wait_ge(d_tok, n - 3)
                    for q in range(4):
                        t, b = 4 * (n % 3) + q, n // 3
                        src = conv0[:, t, b * P:b * P + P] if n < 6 else conv0[:, 12 + q, 0:P]
                        last = pe.transpose(AB[n % 4][:, q * P:q * P + P], src, C("ident"))
                    last.then_inc(d_turned, 1)
                for b in range(NB):
                    for g in range(SSD_G):
                        t = slice(b * P, b * P + P)
                        last = mm(PB[1 + b][:, g * P:g * P + P], conv0[:, 12 + g, t], conv0[:, 16 + g, t])
                    last.then_inc(d_cb_mm, 1)
                pe.wait_ge(gate_ready, 1)
                for b in range(NB):
                    mm(PB[0][:, 24 * b:24 * b + 24], C("triu"), S("da", 24 * b, 24))
                mm(PB[0][:, 48:72], C("ones"), S("da", 0, 24)).then_inc(d_cum_mm, 1)
                pe.wait_ge(d_xd, 1)
                pe.wait_ge(d_tok, 7)
                for g in range(SSD_G):
                    mm(AB[g][:, 0:384], b_tok[:, g], xd[:, 384 * g:384 * g + 384]).then_inc(d_state_mm, 1)
                pe.wait_ge(d_cum, 1)
                pe.wait_ge(d_cb, 2)
                pe.wait_ge(d_state, 4)
                for n in range(12):
                    b, h0 = n // 6, 4 * (n % 6)
                    if n >= 2:
                        pe.wait_ge(d_decay, n - 1)
                    for q in range(4):
                        col = S("da", 24 * b + h0 + q, 1)
                        last = mm(PB[n % 2][:, q * P:q * P + P], bc(col, P, P), C("triu"))
                    last.then_inc(d_decay_mm, 1)
                    if n:
                        ssd_outputs(n - 1)
                ssd_outputs(11)
                for g in range(SSD_G):
                    pe.wait_ge(d_sq, g + 1)
                    for k in range(3):
                        last = mm(PB[g][:, 0:SEQ], C("ones"), y_sq[:, g % 2, k], k == 0, k == 2)
                    last.then_inc(d_sum, 1)

            def stacks(out, a, b, m):
                for q in range(8):
                    for j in range(2):
                        r = slice(j * GC, j * GC + GC)
                        last = mm(out[r, q * GC:q * GC + GC], a(8 * m + q)[r], b(8 * m + q)[r])
                return last

            def gdn():
                pe.wait_ge(conv_done, XBC_T + GQ_T)
                pe.wait_ge(copied, last_copy["z1"])
                for n in range(12):
                    pe.wait_ge(n_sq, n + 1)
                    if n >= 4:
                        pe.wait_ge(n_root, n - 3)
                    mm(PB[n % 4][:, :], C("ones"), g_sq[:, n % 2]).then_inc(n_sum, 1)
                    if n % 2 == 0:
                        m = n // 2
                        if m >= 4:
                            pe.wait_ge(v_copied, m - 3)
                        for q in range(4):
                            b, h = (4 * m + q) // GH, (4 * m + q) % GH
                            last = pe.transpose(AB[m % 4][:, q * P:q * P + P], conv1[:, 24 + h, b * P:b * P + P], C("ident"))
                        last.then_inc(v_turned, 1)
                pe.wait_ge(gate_ready, 2)
                pe.wait_ge(n_root, 12)
                for q, name in enumerate(("triu_chunk", "same_chunk", "chunk0", "chunk1")):
                    last = mm(PB[0][:, 24 * q:24 * q + 24], C(name), S("da", 0, 24))
                last.then_inc(g_cum_mm, 1)
                pe.wait_ge(n_unit, 12)
                pe.wait_ge(v_copied, 6)
                for n in range(6):
                    if n >= 4:
                        pe.wait_ge(k_copied, n - 3)
                    for q in range(4):
                        b, h = (4 * n + q) // GH, (4 * n + q) % GH
                        last = pe.transpose(AB[n % 4][:, q * P:q * P + P], conv1[:, 12 + h, b * P:b * P + P], C("ident"))
                    last.then_inc(k_turned, 1)
                pe.wait_ge(g_cum, 1)
                for n in range(6):
                    if n >= 2:
                        pe.wait_ge(g_decay, n - 1)
                    for q in range(4):
                        last = mm(PB[n % 2][:, q * P:q * P + P], bc(S("da", 4 * n + q, 1), P, P), C("triu_chunk"))
                    last.then_inc(g_decay_mm, 1)
                pe.wait_ge(k_copied, 6)
                for m in range(3):
                    for w, rhs in ((0, 12), (1, 0)):
                        bank = 2 * m + w
                        if bank >= 4:
                            pe.wait_ge(g_gram, bank - 3)
                        for q in range(8):
                            b, h = (8 * m + q) // GH, (8 * m + q) % GH
                            for j in range(2):
                                t = slice(b * P + j * GC, b * P + j * GC + GC)
                                last = mm(AB[bank % 4][j * GC:j * GC + GC, q * GC:q * GC + GC], conv1[:, 12 + h, t],
                                          conv1[:, rhs + h, t])
                        last.then_inc(g_gram_mm, 1)
                of, iv, it, sy = (lambda s: off_t[:, s]), (lambda s: inv[:, s]), (lambda s: inv_t[:, s]), (lambda s: step_y[:, s])
                pe.wait_ge(g_gram, 6)
                pe.wait_ge(g_decay, 6)
                for lv in range(LEVELS):
                    for m in range(3):
                        pe.wait_ge(i_off, 3 * lv + m + 1)
                        if lv:
                            pe.wait_ge(i_inv, 3 * (lv - 1) + m + 1)
                        stacks(BANKS[m], of, iv if lv else (lambda s: C("ident_chunk", 0, GC)), m).then_inc(i_y_mm, 1)
                    if not lv:
                        continue
                    for m in range(3):
                        pe.wait_ge(i_y, 3 * (lv - 1) + m + 1)
                        if lv < LEVELS - 1:
                            stacks(BANKS[3 + m], it, sy, m).then_inc(i_z_mm, 1)
                        stacks(BANKS[m], sy, it, m).then_inc(i_zt_mm, 1)
                pe.wait_ge(i_inv, 3 * LEVELS)
                pe.wait_ge(g_scaled, 4)

                def ks(n):
                    c, g = SCAN[n]
                    if not c:
                        return
                    pe.wait_ge(c_state, 3 * (c - 1) + g + 1)
                    for q in range(4):
                        h = 4 * g + q
                        last = mm(BANKS[n % 2][(c % 2) * GC:(c % 2) * GC + GC, q * GD:q * GD + GD],
                                  conv1[:, 12 + h, c * GC:c * GC + GC], state[:, h])
                    last.then_inc(c_ks_mm, 1)

                def tr(n):
                    c, g = SCAN[n]
                    b, r = c // 2, slice((c % 2) * GC, (c % 2) * GC + GC)
                    if c:
                        pe.wait_ge(c_resid, n - 2)
                    if n >= 2:
                        pe.wait_ge(c_vnew, n - 1)
                    for q in range(4):
                        h = 4 * g + q
                        rhs = resid[r, n % 2, q] if c else v_tok[r, b, h]
                        last = mm(BANKS[2 + n % 2][r, q * GD:q * GD + GD], inv_t[r, b * GH + h], rhs)
                    last.then_inc(c_tr_mm, 1)

                def ou(n):
                    c, g = SCAN[n]
                    b, r = c // 2, slice((c % 2) * GC, (c % 2) * GC + GC)
                    pe.wait_ge(c_vnew, n + 1)
                    if n >= 2:
                        pe.wait_ge(c_o, n - 1)
                    for q in range(4):
                        h = 4 * g + q
                        o = BANKS[4 + n % 2][:, q * GC:q * GC + GC]
                        if c:
                            mm(o, state[:, h], conv1[:, h, c * GC:c * GC + GC], True, False)
                        last = mm(o, v_new[r, g, q], attn_t[r, b * GH + h], not c, True)
                    last.then_inc(c_o_mm, 1)
                    if c == 3:
                        return
                    if n >= 2:
                        pe.wait_ge(c_state, n - 1)
                    for q in range(4):
                        last = mm(BANKS[6 + n % 2][:, q * GD:q * GD + GD], k_tok[r, b, 4 * g + q], v_new[r, g, q])
                    last.then_inc(c_u_mm, 1)

                for n in range(len(SCAN) + 2):
                    if n < len(SCAN):
                        ks(n)
                    if 0 <= n - 1 < len(SCAN):
                        tr(n - 1)
                    if n >= 2:
                        ou(n - 2)
                pe.wait_ge(c_vnew, 12)
                for n in range(6):
                    pe.wait_ge(o_sqd, n + 1)
                    if n >= 4:
                        pe.wait_ge(o_root, n - 3)
                    mm(PB[n % 4][:, :], C("ones"), o_sq[:, n % 2]).then_inc(o_sum, 1)

            pe.wait_ge(in_landed[0], 16)
            pe.wait_ge(in_landed[1], 16)
            for g in range(PRM_G):
                last = pe.transpose(PB[g // 4][:, (g % 4) * P:(g % 4 + 1) * P], prm_rows[:, g, :], C("ident"))
            last.then_inc(prm_turned, 1)
            pe.wait_ge(in_landed[4], 32)
            pe.wait_ge(rel_ones, 1)
            for v in range(2):
                last = mm(AB[v][0:AH, 0:384], rel[0:33, :], bucket[0:33, v, :])
            last.then_inc(vec_mm, 1)
            pe.wait_ge(c_ready, 1)
            for m in range(16):
                ada_unit(m)
            pe.wait_ge(prm_ready, 1)
            sum_squares(0)
            pe.wait_ge(mods_read, 1)
            project("dt0", token=True, norm=0)
            project("conv0", ada0=16)
            pe.wait_ge(mods_read, 2)
            pe.wait_ge(vec_copied, 1)
            bias_tiles(0)
            project("q0")
            project("k0")
            project("v0", token=True)
            attention(0)
            project("z0", ada0=36)
            ssd()
            for m in range(48, 52):
                if m == 48:
                    pe.wait_ge(d_y, 12)
                ada_unit(m)
            pe.wait_ge(mods_read, 4)
            accumulate("out0", mix_ready, 0, lambda k: k if not isinstance(k, int) or k < 12 else k + 6)
            sum_squares(1)
            sum_squares(2)
            project("up0", ada0=52, norm=1)
            pe.wait_ge(mods_read, 5)
            accumulate("down0", g_ready, 0, lambda k: k)
            sum_squares(3)
            sum_squares(4)
            project("dt1", token=True, norm=2)
            project("conv1")
            bias_tiles(1)
            project("q1")
            project("k1")
            project("v1", token=True)
            attention(1)
            project("z1")
            gdn()
            accumulate("out1", mix_ready, MIX_T, lambda k: k if not isinstance(k, int) or k < 12 else k + 6)
            sum_squares(5)
            sum_squares(6)
            project("up1", norm=3)
            accumulate("down1", g_ready, FT, lambda k: k)
            sum_squares(7)

        @block.scalar
        def _(act):
            chain = [0]

            def link(ins):
                chain[0] += 1
                ins.then_inc(act_step, 1)
                act.wait_ge(act_step, chain[0])

            def round_half(n, a, i=0):
                if n >= UNITS:
                    return
                if a == 0:
                    act.wait_ge(w_landed[n % 4], 16 * i + 16 * (n // 4 + 1))
                if 2 * n + a >= 4:
                    act.wait_ge(w_used, 8 * i + 2 * n + a - 3)
                hi, _, src = w_half(n, a)
                act.activation(hi, src, ACT.Copy).then_inc(w_rounded, 1)

            def stream(name, before=None, after=None):
                n0 = PARTS[name][0]

                def step(k, i, j):
                    n = n0 + j
                    round_half(n + 2, 0, i)
                    if before is not None:
                        act.wait_ge(w_used, 8 * i + 2 * n + 2)
                        act.nop(nofuse=True)
                        before(k, i, j, PB[n % 4][:, 0:SEQ])
                    round_half(n + 2, 1, i)
                    if after is not None:
                        after(k, i, j)

                units(act, name, step)

            def conv(layer):
                dst, base = convs[layer], layer * XBC_T
                cnt = (XBC_T, GQ_T)[layer]

                def first(k, i, j, ps):
                    w = prm[:, ds(PRM[f"conv{layer}_w"] + 3 * cnt + k, 1)]
                    b = prm[:, ds(PRM["conv0_b"] + k, 1)] if layer == 0 else 0.0
                    act.activation(dst[:, ds(k, 1), :], one(ps), ACT.Identity, bias=b, scale=w).then_inc(conv_first, 1)

                def silu(k, i, j):
                    act.wait_ge(conv_taps, 3 * (base + k) + 3)
                    act.nop(nofuse=True)
                    act.activation(dst[:, ds(k, 1), :], dst[:, ds(k, 1), :], ACT.Silu).then_inc(conv_done, 1)

                stream(f"conv{layer}", first, silu)

            def up(layer):
                base = 2 * FT * layer

                def first(k, i, j, ps):
                    half, s = j % 2, j // 2 % 2
                    col = half * FT + 2 * i + j // 2
                    w = prm[:, ds(PRM["up_w"] + (3 * layer + 2) * 2 * FT + col, 1)]
                    b = prm[:, ds(PRM["up_b"] + layer * 2 * FT + col, 1)]
                    act.activation((yv if half else yg)[:, s], ps, ACT.Identity, bias=b, scale=w).then_inc(up_first, 1)

                def finish(k, i, j):
                    s = j // 2 % 2
                    pair = 2 * i + j // 2
                    if j % 2 == 0:
                        act.wait_ge(up_taps, 2 * (base + k) + 2)
                        act.activation(yg[:, s], yg[:, s], ACT.Gelu_apprx_tanh).then_inc(gelu_done, 1)
                    else:
                        act.wait_ge(prod_done, FT * layer + pair + 1)
                        act.nop(nofuse=True)
                        act.activation(a_hi[:, ds(pair, 1), :], prod[:, s:s + 1], ACT.Copy).then_inc(g_rounded, 1)

                stream(f"up{layer}", first, finish)

            def copy_unit(fn, dst):
                return lambda k, i, j, ps: act.activation(dst(k), ps, fn).then_inc(copied, 1)

            def root(event, bank=None, scale=1.0 / D_MODEL):
                act.wait_ge(sums, event + 1)
                act.activation(rn[:, 0], PB[0][:, 0:SEQ], ACT.Sqrt, bias=EPS, scale=scale).then_inc(roots, 1)

            def pre_norm(event, layer, which, after):
                for k in range(DT):
                    if after is None:
                        if k == 0:
                            act.wait_ge(in_landed[2], 16)
                    else:
                        act.wait_ge(x_ready, 8 * after + k + 1)
                    act.activation(sq[:, k], x[:, k], ACT.Square).then_inc(squares, 1)
                if after is None:
                    round_half(0, 0)
                    round_half(0, 1)
                    round_half(1, 0)
                    round_half(1, 1)
                root(event)
                norm = 2 * layer + which
                for k in range(DT):
                    act.wait_ge(scaled, DT * norm + k + 1)
                    act.activation(h_hi[:, k], yr[:, k], ACT.Identity, bias=mods[:, layer, 3 * which, k:k + 1]).then_inc(h_rounded, 1)

            def post_norm(event, name):
                act.wait_ge(w_used, 2 * (PARTS[name][0] + PARTS[name][1]))
                for q in range(4):
                    act.activation(sq[:, 2 * q:2 * q + 2].rearrange("p a t -> p (a t)"), AB[q][:, :], ACT.Square).then_inc(squares, 2)
                root(event)

            def attention(layer):
                n8 = AH * layer
                act.wait_ge(s_max, layer + 1)
                for h in range(AH):
                    act.activation(scores[:, h, 0:SEQ], scores[:, h, 0:SEQ], ACT.Exp, bias=S("neg_max", h, 1),
                                   accum_out=S("prob_sum", h, 1)).then_inc(s_exp, 1)
                    act.activation(scores[:, h, SEQ:384], scores[:, h, SEQ:384], ACT.Exp, bias=S("neg_max", 8 + h, 1),
                                   accum_out=S("prob_sum", 8 + h, 1)).then_inc(s_exp, 1)
                if layer == 0:
                    act.activation(S("sink_exp", 0, 16), S("sink_exp", 0, 16), ACT.Exp).then_inc(s_exp, 1)
                for h in range(AH):
                    act.wait_ge(s_turned, n8 + h + 1)
                    if h >= 2:
                        act.wait_ge(s_out, n8 + h - 1)
                    act.activation(probs_t[:, h % 2], AB[h % 4][:, 0:384], ACT.Copy).then_inc(s_copied, 1)
                    if h % 2 == 1 and h >= 3:
                        attention_out(layer, h // 2 - 1)
                attention_out(layer, 3)

            def attention_out(layer, t):
                act.wait_ge(s_out, AH * layer + 2 * t + 2)
                act.activation(a_hi[:, 18 + t], PB[t][:, 0:SEQ], ACT.Copy).then_inc(s_rounded, 1)

            def gates(layer):
                n = 48 if layer == 0 else 24
                heads = (SSD_H, GH)[layer]
                act.wait_ge(gate_abs, layer + 1)
                act.activation(S("e", 0, n), S("abs", 0, n), ACT.Exp, scale=-1.0).then_inc(gate_exp, 1)
                act.activation(S("a", 0, heads), rows[:, ROW[f"a_log{layer}"]:ROW[f"a_log{layer}"] + heads], ACT.Exp).then_inc(gate_exp, 1)
                act.activation(S("be", 0, 24), S("bx", 0, 24), ACT.Exp, scale=-1.0).then_inc(gate_exp, 1)
                act.wait_ge(gate_ln, layer + 1)
                act.activation(S("ln", 0, n), S("u", 0, n), ACT.Ln).then_inc(gate_exp, 1)

            def ssd():
                for n in range(7):
                    act.wait_ge(d_turned, n + 1)
                    dst = xs_tok[:, n // 3, 512 * (n % 3):512 * (n % 3) + 512] if n < 6 else b_tok[:, :, :].rearrange("p a b -> p (a b)")
                    act.activation(dst, AB[n % 4][:, :], ACT.Copy).then_inc(d_tok, 1)
                for b in range(NB):
                    act.wait_ge(d_cb_mm, b + 1)
                    act.activation(cb[:, b].rearrange("p a b -> p (a b)"), PB[1 + b][:, :], ACT.Copy).then_inc(d_cb, 1)
                gates(0)
                act.wait_ge(d_cum, 1)
                act.activation(S("tail", 0, 24), S("tail", 0, 24), ACT.Exp).then_inc(d_tail, 1)
                for g in range(SSD_G):
                    act.wait_ge(d_state_mm, g + 1)
                    act.activation(h_in[:, 384 * g:384 * g + 384], AB[g][:, 0:384], ACT.Copy).then_inc(d_state, 1)
                for n in range(12):
                    act.wait_ge(d_diff, n + 1)
                    if n >= 6:
                        act.wait_ge(d_y_mm, n - 1)
                        act.activation(cexp[:, n % 2].rearrange("p a b -> p (a b)"), PB[n % 2][:, :], ACT.Exp)
                    l_ = lmat[:, n % 2].rearrange("p a b -> p (a b)")
                    act.activation(l_, l_, ACT.Exp).then_inc(d_decay, 1)
                for g in range(SSD_G):
                    act.wait_ge(d_gated, g + 1)
                    if g >= 2:
                        act.wait_ge(d_sum, g - 1)
                    act.activation(y_sq[:, g % 2], y_ssd[:, 3 * g:3 * g + 3], ACT.Square).then_inc(d_sq, 1)
                for g in range(SSD_G):
                    act.wait_ge(d_sum, g + 1)
                    act.activation(y_rn[:, g], PB[g][:, 0:SEQ], ACT.Sqrt, bias=EPS, scale=1.0 / 384).then_inc(d_root, 1)
                for g in range(SSD_G):
                    act.wait_ge(d_mix, g + 1)
                    act.activation(a_hi[:, 3 * g:3 * g + 3], y_mix[:, 3 * g:3 * g + 3], ACT.Copy).then_inc(d_rounded, 1)

            def gdn():
                def square(n):
                    if n >= 2:
                        act.wait_ge(n_sum, n - 1)
                    act.activation(g_sq[:, n % 2], conv1[:, 2 * n:2 * n + 2], ACT.Square).then_inc(n_sq, 1)

                def turn_v(m):
                    act.wait_ge(v_turned, m + 1)
                    b, h = 4 * m // GH, 4 * m % GH
                    act.activation(v_tok[:, b, h:h + 4].rearrange("p a b -> p (a b)"), AB[m % 4][:, :], ACT.Copy).then_inc(v_copied, 1)

                act.wait_ge(conv_done, XBC_T + GQ_T)
                gates(1)
                square(0)
                for n in range(12):
                    if n < 11:
                        square(n + 1)
                    act.wait_ge(n_sum, n + 1)
                    if n >= 2:
                        act.wait_ge(n_unit, n - 1)
                    act.activation(g_rn[:, n % 2].rearrange("p a b -> p (a b)"), PB[n % 4][:, :], ACT.Sqrt, bias=EPS).then_inc(n_root, 1)
                    if n % 2:
                        turn_v(n // 2)
                act.wait_ge(g_cum, 1)
                act.activation(S("tail", 0, 24), S("tail", 0, 24), ACT.Exp).then_inc(g_tail, 1)
                for j in range(2):
                    act.activation(S(f"tot{j}", 0, 24), S(f"tot{j}", 0, 24), ACT.Exp).then_inc(g_tot, 1)
                for n in range(6):
                    act.wait_ge(g_diff, n + 1)
                    act.activation(egc[:, 4 * n:4 * n + 4].rearrange("p a b -> p (a b)"), PB[n % 2][:, :], ACT.Exp)
                    d_ = dec[:, 4 * n:4 * n + 4].rearrange("p a b -> p (a b)")
                    act.activation(d_, d_, ACT.Exp).then_inc(g_decay, 1)
                for lv in range(1, LEVELS):
                    for m in range(3):
                        act.wait_ge(i_y_mm, 3 * lv + m + 1)
                        act.activation(step_y[:, 8 * m:8 * m + 8].rearrange("p a b -> p (a b)"), BANKS[m][:, :], ACT.Copy).then_inc(i_y, 1)
                for n, (c, g) in enumerate(SCAN):
                    act.wait_ge(c_o_mm, n + 1)
                    act.activation(conv1[:, 4 * g:4 * g + 4, c * GC:c * GC + GC],
                                   BANKS[4 + n % 2][:, 0:4 * GC].rearrange("p (a b) -> p a b", a=4), ACT.Copy).then_inc(c_o, 1)
                act.wait_ge(c_o, 12)

                def o_square(n):
                    if n >= 2:
                        act.wait_ge(o_sum, n - 1)
                    act.activation(o_sq[:, n % 2], conv1[:, 2 * n:2 * n + 2], ACT.Square).then_inc(o_sqd, 1)

                o_square(0)
                for n in range(6):
                    if n < 5:
                        o_square(n + 1)
                    act.wait_ge(o_sum, n + 1)
                    if n >= 2:
                        act.wait_ge(o_mixed, n - 1)
                    act.activation(o_rn[:, n % 2].rearrange("p a b -> p (a b)"), PB[n % 4][:, :], ACT.Sqrt, bias=EPS, scale=1.0 / GD).then_inc(o_root, 1)
                    if n:
                        o_round(n - 1)
                o_round(5)

            def o_round(n):
                act.wait_ge(o_mixed, n + 1)
                act.activation(a_hi[:, 2 * n:2 * n + 2], o_t[:, n % 2], ACT.Copy).then_inc(o_rounded, 1)

            def key0(k, i, j, ps):
                for kv in range(2):
                    for half in range(2):
                        last = act.activation(att_k[half * AD:half * AD + AD, kv], ps[kv * AD:kv * AD + AD], ACT.Copy)
                last.then_inc(copied, 1)

            def values(k, i, j, ps):
                act.activation(att_v[:, :, P * j:P * j + P], ps.rearrange("p (b c) -> p b c", b=NB), ACT.Copy).then_inc(copied, 1)

            def mixer(layer):
                stream(f"dt{layer}")
                conv(layer)
                for q in range(4):
                    if q == 0:
                        act.wait_ge(hankel_mm, layer + 1)
                        if layer == 0:
                            act.wait_ge(bias_vec_stored, 16)
                    last = act.activation(bias[:, 2 * q:2 * q + 2].rearrange("p a b -> p (a b)"), AB[q][:, :], ACT.Copy)
                last.then_inc(bias_ready, 1)
                stream(f"q{layer}", lambda k, i, j, ps: act.activation(att_q[:, j], ps, ACT.Copy, scale=AD ** -0.5).then_inc(copied, 1))
                stream(f"k{layer}", key0 if layer == 0 else copy_unit(ACT.Copy, lambda k: att_k[:, k]))
                stream(f"v{layer}", values)
                attention(layer)
                stream(f"z{layer}", lambda k, i, j, ps: act.activation(zs[:, ds(k, 1), :], one(ps), ACT.Silu).then_inc(copied, 1))
                (ssd, gdn)[layer]()
                stream(f"out{layer}")

            act.wait_ge(prm_ready, 1)
            act.activation(c_silu[:, :], prm[:, PRM["c"]:PRM["c"] + 8], ACT.Silu).then_inc(c_ready, 1)
            pre_norm(0, 0, 0, None)
            mixer(0)
            post_norm(1, "out0")
            pre_norm(2, 0, 1, 0)
            up(0)
            stream("down0")
            post_norm(3, "down0")
            pre_norm(4, 1, 0, 1)
            mixer(1)
            post_norm(5, "out1")
            pre_norm(6, 1, 1, 2)
            up(1)
            stream("down1")
            post_norm(7, "down1")

        @block.vector
        def _(dve):
            chain = [0]

            def link(ins):
                chain[0] += 1
                ins.then_inc(dve_step, 1)
                dve.wait_ge(dve_step, chain[0])

            def fl(ap):
                return ap.rearrange("p a b -> p (a b)")

            def split_half(n, a, i=0):
                if n >= UNITS:
                    return
                hi, lo, src = w_half(n, a)
                dve.wait_ge(w_rounded, 8 * i + 2 * n + a + 1)
                dve.tensor_tensor(lo, src, hi.bitcast(F32), ALU.subtract).then_inc(w_split, 1)

            def stream(name, work=None, after=None):
                n0 = PARTS[name][0]

                def step(k, i, j):
                    n = n0 + j
                    split_half(n + 2, 0, i)
                    if work is not None:
                        work(k, i, j, PB[n % 4][:, 0:SEQ])
                    split_half(n + 2, 1, i)
                    if after is not None:
                        after(k, i, j)

                units(dve, name, step)

            def taps(dst, w, ps, width, done, base):
                for s in range(1, width):
                    if s > 1:
                        dve.wait_ge(done, base + s - 1)
                    dve.scalar_tensor_tensor(dst(slice(s, SEQ)), ps(slice(0, SEQ - s)), w(width - 1 - s), dst(slice(s, SEQ)),
                                             ALU.mult, ALU.add).then_inc(done, 1)

            def conv(layer):
                dst, base, cnt = convs[layer], layer * XBC_T, (XBC_T, GQ_T)[layer]

                def work(k, i, j, ps):
                    dve.wait_ge(conv_first, base + k + 1)
                    taps(lambda t: dst[:, ds(k, 1), t], lambda tap: prm[:, ds(PRM[f"conv{layer}_w"] + tap * cnt + k, 1)],
                         lambda t: one(ps[:, t]), 4, conv_taps, 3 * (base + k))

                stream(f"conv{layer}", work)

            def up(layer):
                base = 2 * FT * layer

                def work(k, i, j, ps):
                    half, s = j % 2, j // 2 % 2
                    y = (yv if half else yg)[:, s]
                    col = half * FT + 2 * i + j // 2
                    dve.wait_ge(up_first, base + k + 1)
                    taps(lambda t: y[:, t], lambda tap: prm[:, ds(PRM["up_w"] + (3 * layer + tap) * 2 * FT + col, 1)],
                         lambda t: ps[:, t], 3, up_taps, 2 * (base + k))
                    if half:
                        dve.wait_ge(gelu_done, FT * layer + 2 * i + j // 2 + 1)
                        dve.wait_ge(up_taps, 2 * (base + k) + 2)
                        dve.tensor_tensor(prod[:, s], yg[:, s], y, ALU.mult).then_inc(prod_done, 1)

                def after(k, i, j):
                    if j % 2:
                        pair = 2 * i + j // 2
                        dve.wait_ge(g_rounded, FT * layer + pair + 1)
                        dve.tensor_tensor(a_lo[:, ds(pair, 1), :], prod[:, j // 2 % 2:j // 2 % 2 + 1],
                                          a_hi[:, ds(pair, 1), :].bitcast(F32), ALU.subtract).then_inc(g_ready, 1)

                stream(f"up{layer}", work, after)

            def read_mods(a, b, used):
                dve.wait_ge(ada_used, used)
                m = mods[:, :, :, :].rearrange("p l s k -> p (l s k)")
                dve.tensor_tensor(m[:, a:b], AB[3][:, a:b], prm[:, PRM["ada_b"] + a:PRM["ada_b"] + b], ALU.add).then_inc(mods_read, 1)

            def make_gain(layer, which, mods_at):
                dve.wait_ge(mods_read, mods_at)
                c = PRM["norm"] + (4 * layer + which) * 8
                w, g = prm[:, c:c + 8], gain[:, layer, which]
                section = {0: 1, 1: 2, 2: 4, 3: 5}[which]
                m = mods[:, layer, section]
                if which % 2 == 0:
                    link(dve.scalar_tensor_tensor(g, m, 1.0, w, ALU.add, ALU.mult))
                else:
                    link(dve.tensor_tensor(g, m, w, ALU.mult))

            def inverse_root(event):
                dve.wait_ge(roots, event + 1)
                link(dve.reciprocal(rn[:, 1], rn[:, 0]))

            def pre_norm(event, layer, which):
                inverse_root(event)
                norm = 2 * layer + which

                def rest(k):
                    dve.wait_ge(h_rounded, DT * norm + k + 1)
                    dve.scalar_tensor_tensor(h_lo[:, k], yr[:, k], mods[:, layer, 3 * which, k:k + 1], h_hi[:, k].bitcast(F32),
                                             ALU.add, ALU.subtract).then_inc(h_ready, 1)

                for k in range(DT):
                    dve.scalar_tensor_tensor(yr[:, k], x[:, k], gain[:, layer, 2 * which, k:k + 1], rn[:, 1],
                                             ALU.mult, ALU.mult).then_inc(scaled, 1)
                    if k >= 2:
                        rest(k - 2)
                rest(DT - 2)
                rest(DT - 1)

            def post_norm(event, layer, which):
                inverse_root(event)
                for q in range(4):
                    link(dve.tensor_tensor(yr[:, 2 * q:2 * q + 2], AB[q][:, :].rearrange("p (a t) -> p a t", a=2),
                                           bc(rn[:, 1:2], P, 2, SEQ), ALU.mult))
                    for k in (2 * q, 2 * q + 1):
                        dve.scalar_tensor_tensor(x[:, k], yr[:, k], gain[:, layer, 2 * which + 1, k:k + 1], x[:, k],
                                                 ALU.mult, ALU.add).then_inc(x_ready, 1)

            def attention(layer):
                n8 = AH * layer
                dve.wait_ge(bias_ready, layer + 1)
                for h in range(AH):
                    dve.wait_ge(s_scored, n8 + h + 1)
                    dve.tensor_tensor_reduce(scores[:, h, 0:SEQ], AB[h % 4][:, 0:SEQ], bias[:, h], 1.0, -3e38, ALU.add, ALU.max,
                                             S("max", h, 1)).then_inc(s_biased, 1)
                    dve.tensor_tensor_reduce(scores[:, h, SEQ:384], AB[h % 4][:, SEQ:384], bias[:, h, P:SEQ], 1.0, -3e38, ALU.add, ALU.max,
                                             S("max", 8 + h, 1)).then_inc(s_biased, 1)
                dve.wait_ge(s_biased, 2 * (n8 + AH))
                sink = bc(rows[:, ROW["sinks"]:ROW["sinks"] + 8].rearrange("p (a b) -> p a b", a=1), P, 2, 8)
                two = lambda t: S(t, 0, 16).rearrange("p (a b) -> p a b", a=2)
                if layer == 0:
                    link(dve.tensor_tensor(two("max"), two("max"), sink, ALU.max))
                    dve.tensor_tensor(two("sink_exp"), sink, two("max"), ALU.subtract)
                dve.tensor_scalar(S("neg_max", 0, 16), S("max", 0, 16), -1.0, None, ALU.mult).then_inc(s_max, 1)
                dve.wait_ge(s_exp, 17 if layer == 0 else 17 + 16)
                if layer == 0:
                    link(dve.tensor_tensor(S("prob_sum", 0, 16), S("prob_sum", 0, 16), S("sink_exp", 0, 16), ALU.add))
                link(dve.reciprocal(S("inv_sum", 0, 16), S("prob_sum", 0, 16)))
                for h in range(AH):
                    dve.tensor_scalar(scores[:, h, 0:SEQ], scores[:, h, 0:SEQ], S("inv_sum", h, 1), None, ALU.mult)
                    dve.tensor_scalar(scores[:, h, SEQ:384], scores[:, h, SEQ:384], S("inv_sum", 8 + h, 1), None, ALU.mult).then_inc(s_norm, 1)
                for t in range(4):
                    dve.wait_ge(s_rounded, 4 * layer + t + 1)
                    dve.tensor_tensor(a_lo[:, 18 + t], PB[t][:, 0:SEQ], a_hi[:, 18 + t].bitcast(F32), ALU.subtract).then_inc(s_ready, 1)

            def gates(layer):
                n, heads = (48, SSD_H) if layer == 0 else (24, GH)
                link(dve.scalar_tensor_tensor(S("abs", 0, n), S("dtx", 0, n), -1.0, S("dtx", 0, n), ALU.mult, ALU.max))
                if layer == 0:
                    link(dve.memset(S("bx", 0, 24), 0.0))
                dve.tensor_scalar(S("relu", 0, n), S("dtx", 0, n), 0.0, None, ALU.max).then_inc(gate_abs, 1)
                dve.wait_ge(gate_exp, 4 * layer + 3)
                link(dve.tensor_scalar(S("u", 0, n), S("e", 0, n), 1.0, None, ALU.add))
                link(dve.tensor_scalar(S("um", 0, n), S("u", 0, n), -1.0, None, ALU.add))
                dve.tensor_scalar(S("be1", 0, 24), S("be", 0, 24), 1.0, None, ALU.add).then_inc(gate_ln, 1)
                link(dve.tensor_tensor(S("um", 0, n), S("e", 0, n), S("um", 0, n), ALU.subtract))
                link(dve.reciprocal(S("ur", 0, n), S("u", 0, n)))
                dve.wait_ge(gate_ln, layer + 1)
                link(dve.reciprocal(S("beta", 0, 24), S("be1", 0, 24)))
                link(dve.tensor_tensor(S("um", 0, n), S("um", 0, n), S("ur", 0, n), ALU.mult))
                link(dve.tensor_tensor(S("um", 0, n), S("um", 0, n), S("relu", 0, n), ALU.add))
                dve.wait_ge(gate_exp, 4 * layer + 4)
                link(dve.tensor_tensor(S("dt", 0, n), S("um", 0, n), S("ln", 0, n), ALU.add))
                two = lambda t: S(t, 0, n).rearrange("p (a b) -> p a b", a=2)
                a_ = bc(S("a", 0, heads).rearrange("p (a b) -> p a b", a=1), P, 2, heads)
                dve.scalar_tensor_tensor(two("da"), two("dt"), -1.0, a_, ALU.mult, ALU.mult).then_inc(gate_ready, 1)

            def ssd():
                gates(0)
                dve.wait_ge(in_landed[3], 16)
                for half in range(2):
                    r = slice(half * 64, half * 64 + 64)
                    link(dve.tensor_copy(S("d", 0, 12, half * 64, half * 64 + 64), rows[r, ROW["d"] + half:ROW["d"] + 24:2]))
                dve.wait_ge(d_cum_mm, 1)
                link(dve.tensor_copy(S("cum", 0, 48), PB[0][:, 0:48]))
                dve.tensor_tensor(S("tail", 0, 24), PB[0][:, 48:72], S("cum", 0, 24), ALU.subtract).then_inc(d_cum, 1)
                dve.wait_ge(d_tail, 1)
                link(dve.tensor_tensor(S("tail", 0, 24), S("tail", 0, 24), S("dt", 0, 24), ALU.mult))
                dve.wait_ge(d_tok, 3)
                dve.tensor_tensor(xd[:, :].rearrange("p (h d) -> p h d", h=24), xs_tok[:, 0].rearrange("p (h d) -> p h d", h=24),
                                  bc(S("tail", 0, 24).rearrange("p (h d) -> p h d", d=1), P, 24, 64), ALU.mult).then_inc(d_xd, 1)
                dve.wait_ge(d_cb, 2)

                def diff(n):
                    b, h0 = n // 6, 4 * (n % 6)
                    dve.wait_ge(d_decay_mm, n + 1)
                    for q in range(4):
                        last = dve.scalar_tensor_tensor(lmat[:, n % 2, q], PB[n % 2][:, q * P:q * P + P], S("cum", 24 * b + h0 + q, 1),
                                                        C("keep"), ALU.subtract, ALU.min)
                    last.then_inc(d_diff, 1)

                def weights(n):
                    b, h0 = n // 6, 4 * (n % 6)
                    dve.wait_ge(d_decay, n + 1)
                    if n >= 2:
                        dve.wait_ge(d_y_mm, n - 1)
                    for q in range(4):
                        h = h0 + q
                        if b:
                            dve.tensor_tensor(cexp[:, n % 2, q], cexp[:, n % 2, q], conv0[:, 16 + h // HPG, P:2 * P], ALU.mult)
                        last = dve.scalar_tensor_tensor(mmat[:, n % 2, q], lmat[:, n % 2, q], S("dt", 24 * b + h, 1), cb[:, b, h // HPG],
                                                        ALU.mult, ALU.mult)
                    last.then_inc(d_mmat, 1)

                def outputs(n):
                    b, t0 = n // 6, 2 * (n % 6)
                    dve.wait_ge(d_y_mm, n + 1)
                    for q in range(2):
                        c = slice(b * P, b * P + P)
                        last = dve.scalar_tensor_tensor(y_ssd[:, t0 + q, c], conv0[:, t0 + q, c], S("d", t0 + q, 1),
                                                        AB[n % 4][:, q * P:q * P + P], ALU.mult, ALU.add)
                    last.then_inc(d_y, 1)

                diff(0)
                for n in range(12):
                    if n < 11:
                        diff(n + 1)
                    weights(n)
                    if n:
                        outputs(n - 1)
                outputs(11)
                dve.wait_ge(d_y, 12)
                for g in range(SSD_G):
                    t = slice(3 * g, 3 * g + 3)
                    dve.tensor_tensor(y_ssd[:, t], y_ssd[:, t], zs[:, t], ALU.mult).then_inc(d_gated, 1)
                read_mods(48, 52, 52)
                for g in range(SSD_G):
                    dve.wait_ge(d_root, g + 1)
                    link(dve.reciprocal(y_rn[:, g], y_rn[:, g]))
                    for k in range(3 * g, 3 * g + 3):
                        last = dve.scalar_tensor_tensor(y_mix[:, k], y_ssd[:, k], prm[:, PRM["ssd_norm"] + k:PRM["ssd_norm"] + k + 1],
                                                        y_rn[:, g], ALU.mult, ALU.mult)
                    last.then_inc(d_mix, 1)
                    if g:
                        mix_rest(g - 1)
                mix_rest(3)
                mark_attention(0)

            def mix_rest(g):
                dve.wait_ge(d_rounded, g + 1)
                for k in range(3 * g, 3 * g + 3):
                    dve.tensor_tensor(a_lo[:, k], y_mix[:, k], a_hi[:, k].bitcast(F32), ALU.subtract).then_inc(mix_ready, 1)

            def mark_attention(layer):
                dve.wait_ge(mix_ready, MIX_T * layer + 12)
                dve.sem_inc(mix_ready, 4)

            def gdn():
                stack = lambda ap, n: bc(ap.rearrange("p (s d) -> p s d", d=1), ap.shape[0], ap.shape[1], n)
                gates(1)
                for n in range(12):
                    dve.wait_ge(n_root, n + 1)
                    r = g_rn[:, n % 2]
                    link(dve.reciprocal(r, r))
                    t = conv1[:, 2 * n:2 * n + 2]
                    if n < 6:
                        dve.scalar_tensor_tensor(t, t, GD ** -0.5, r, ALU.mult, ALU.mult).then_inc(n_unit, 1)
                    else:
                        dve.tensor_tensor(t, t, r, ALU.mult).then_inc(n_unit, 1)
                dve.wait_ge(g_cum_mm, 1)
                link(dve.tensor_copy(S("cum", 0, 24), PB[0][:, 0:24]))
                for j in range(2):
                    dve.tensor_copy(S(f"tot{j}", 0, 24), PB[0][:, 48 + 24 * j:72 + 24 * j])
                dve.tensor_tensor(S("tail", 0, 24), PB[0][:, 24:48], S("cum", 0, 24), ALU.subtract).then_inc(g_cum, 1)
                dve.wait_ge(g_tail, 1)
                for n in range(6):
                    dve.wait_ge(k_turned, n + 1)
                    b, h = 4 * n // GH, 4 * n % GH
                    dve.tensor_tensor(k_tok[:, b, h:h + 4], AB[n % 4][:, :].rearrange("p (a d) -> p a d", a=4),
                                      stack(S("tail", 4 * n, 4), GD), ALU.mult).then_inc(k_copied, 1)
                for n in range(6):
                    dve.wait_ge(g_decay_mm, n + 1)
                    ps = PB[n % 2][:, :].rearrange("p (a d) -> p a d", a=4)
                    for j in range(2):
                        r = slice(j * GC, j * GC + GC)
                        last = dve.tensor_tensor(dec[r, 4 * n:4 * n + 4], ps[r, :, r], stack(S("cum", 4 * n, 4, r.start, r.stop), GC), ALU.subtract)
                    link(last)
                    keep = bc(C("keep_chunk", 0, GC).rearrange("p (a d) -> p a d", a=1), P, 4, GC)
                    dve.tensor_tensor(dec[:, 4 * n:4 * n + 4], dec[:, 4 * n:4 * n + 4], keep, ALU.min).then_inc(g_diff, 1)
                for m in range(3):
                    s8 = slice(8 * m, 8 * m + 8)
                    dve.wait_ge(g_gram_mm, 2 * m + 1)
                    dve.wait_ge(g_decay, min(6, 2 * m + 2))
                    link(dve.tensor_tensor(sys_t[:, s8], AB[2 * m % 4][:, :].rearrange("p (a d) -> p a d", a=8), dec[:, s8], ALU.mult))
                    dve.tensor_tensor(sys_t[:, s8], sys_t[:, s8], stack(S("beta", 8 * m, 8), GC), ALU.mult).then_inc(g_gram, 1)
                    dve.wait_ge(g_gram_mm, 2 * m + 2)
                    dve.tensor_tensor(attn_t[:, s8], AB[(2 * m + 1) % 4][:, :].rearrange("p (a d) -> p a d", a=8), dec[:, s8], ALU.mult).then_inc(g_gram, 1)
                ident = bc(C("ident_chunk", 0, GC).rearrange("p (a d) -> p a d", a=1), P, 8, GC)
                three = lambda bank: bank[:, :].rearrange("p (a d) -> p a d", a=8)
                for lv in range(LEVELS):
                    for m in range(3):
                        s8 = slice(8 * m, 8 * m + 8)
                        if lv == 0:
                            dve.wait_ge(i_off, m + 1)
                            dve.tensor_tensor(inv_t[:, s8], ident, off_t[:, s8], ALU.subtract)
                            dve.wait_ge(i_y_mm, m + 1)
                            dve.tensor_tensor(inv[:, s8], ident, three(BANKS[m]), ALU.subtract).then_inc(i_inv, 1)
                            continue
                        dve.wait_ge(i_inv, 3 * (lv - 1) + m + 1)
                        if lv < LEVELS - 1:
                            dve.wait_ge(i_z_mm, 3 * (lv - 1) + m + 1)
                            dve.tensor_tensor(inv[:, s8], inv[:, s8], three(BANKS[3 + m]), ALU.subtract)
                        dve.wait_ge(i_zt_mm, 3 * (lv - 1) + m + 1)
                        dve.tensor_tensor(inv_t[:, s8], inv_t[:, s8], three(BANKS[m]), ALU.subtract).then_inc(i_inv, 1)

                def residual(n):
                    c, g = SCAN[n]
                    if c:
                        b, r = c // 2, slice((c % 2) * GC, (c % 2) * GC + GC)
                        dve.wait_ge(c_ks_mm, n - 2)
                        dve.tensor_tensor(resid[r, n % 2], v_tok[r, b, 4 * g:4 * g + 4],
                                          BANKS[n % 2][r, :].rearrange("p (a d) -> p a d", a=4), ALU.subtract).then_inc(c_resid, 1)

                def values(n):
                    c, g = SCAN[n]
                    b, r = c // 2, slice((c % 2) * GC, (c % 2) * GC + GC)
                    dve.wait_ge(c_tr_mm, n + 1)
                    dve.tensor_tensor(v_new[r, g], BANKS[2 + n % 2][r, :].rearrange("p (a d) -> p a d", a=4),
                                      stack(S("beta", b * GH + 4 * g, 4, r.start, r.stop), GD), ALU.mult).then_inc(c_vnew, 1)

                def states(n):
                    c, g = SCAN[n]
                    if c == 3:
                        return
                    b, j = c // 2, c % 2
                    dve.wait_ge(c_u_mm, n + 1)
                    if c == 0:
                        dve.tensor_copy(state[:, 4 * g:4 * g + 4], BANKS[6 + n % 2][:, :].rearrange("p (a d) -> p a d", a=4)).then_inc(c_state, 1)
                        return
                    for q in range(4):
                        h = 4 * g + q
                        last = dve.scalar_tensor_tensor(state[:, h], state[:, h], S(f"tot{j}", b * GH + h, 1),
                                                        BANKS[6 + n % 2][:, q * GD:q * GD + GD], ALU.mult, ALU.add)
                    last.then_inc(c_state, 1)

                dve.wait_ge(g_tot, 2)
                dve.wait_ge(i_inv, 3 * LEVELS)
                for n in range(len(SCAN) + 2):
                    if n < len(SCAN):
                        residual(n)
                    if 0 <= n - 1 < len(SCAN):
                        values(n - 1)
                    if n >= 2:
                        states(n - 2)

                def o_rest(n):
                    dve.wait_ge(o_rounded, n + 1)
                    for q in range(2):
                        dve.tensor_tensor(a_lo[:, 2 * n + q], o_t[:, n % 2, q], a_hi[:, 2 * n + q].bitcast(F32), ALU.subtract).then_inc(mix_ready, 1)

                for n in range(6):
                    dve.wait_ge(o_root, n + 1)
                    link(dve.reciprocal(o_rn[:, n % 2], o_rn[:, n % 2]))
                    link(dve.scalar_tensor_tensor(o_t[:, n % 2], conv1[:, 2 * n:2 * n + 2], prm[:, PRM["gdn_norm"]:PRM["gdn_norm"] + 1],
                                                  o_rn[:, n % 2], ALU.mult, ALU.mult))
                    dve.tensor_tensor(o_t[:, n % 2], o_t[:, n % 2], zs[:, 2 * n:2 * n + 2], ALU.mult).then_inc(o_mixed, 1)
                    if n:
                        o_rest(n - 1)
                o_rest(5)
                mark_attention(1)

            def read_dt(layer):
                def work(k, i, j, ps):
                    heads = (SSD_H, GH)[layer]
                    n = PARTS[f"dt{layer}"][0]
                    dve.wait_ge(w_used, 2 * n + 2)
                    dve.wait_ge(in_landed[3], 16)
                    v = ps.rearrange("p (b c) -> p b c", b=NB)
                    two = lambda t: S(t, 0, 2 * heads).rearrange("p (a b) -> p a b", a=2)
                    r0 = ROW[f"dt_bias{layer}"]
                    b_ = bc(rows[:, r0:r0 + heads].rearrange("p (a b) -> p a b", a=1), P, 2, heads)
                    if layer:
                        link(dve.tensor_copy(two("bx"), v[:, :, 0:heads]))
                    dve.tensor_tensor(two("dtx"), v[:, :, layer * heads:(layer + 1) * heads], b_, ALU.add).then_inc(dt_read, 1)

                stream(f"dt{layer}", work)
                dve.wait_ge(dt_read, layer + 1)

            def mixer(layer):
                read_dt(layer)
                conv(layer)
                if layer == 0:
                    read_mods(16, 36, 36)
                for q in "qkv":
                    stream(f"{q}{layer}")
                attention(layer)
                stream(f"z{layer}")
                if layer == 0:
                    read_mods(36, 48, 48)
                    for which in (1, 2, 3):
                        make_gain(0, which, 3)
                (ssd, gdn)[layer]()
                stream(f"out{layer}")

            dve.memset(rel[32:33, :], 1.0).then_inc(rel_ones, 1)
            dve.wait_ge(prm_turned, 1)
            dve.tensor_copy(prm[:, 0:512], PB[0][:, :])
            dve.tensor_copy(prm[:, 512:PRM_G * P], PB[1][:, 0:PRM_G * P - 512]).then_inc(prm_ready, 1)
            dve.wait_ge(vec_mm, 1)
            for v in range(2):
                last = dve.tensor_copy(bias_vec[0:AH, v], AB[v][0:AH, 0:384])
            last.then_inc(vec_copied, 1)
            for n in range(2):
                split_half(n, 0)
                split_half(n, 1)
            dve.wait_ge(prm_ready, 1)
            read_mods(0, 16, 16)
            make_gain(0, 0, 1)
            pre_norm(0, 0, 0)
            mixer(0)
            post_norm(1, 0, 0)
            pre_norm(2, 0, 1)
            up(0)
            read_mods(52, 96, 96)
            for which in range(4):
                make_gain(1, which, 5)
            stream("down0")
            post_norm(3, 0, 1)
            pre_norm(4, 1, 0)
            mixer(1)
            post_norm(5, 1, 0)
            pre_norm(6, 1, 1)
            up(1)
            stream("down1")
            post_norm(7, 1, 1)

        @block.gpsimd
        def _(pool):
            def scale(n):
                b, t0 = n // 2, (12, 0)[n % 2]
                t = conv1[:, t0:t0 + GH, b * P:b * P + P]
                pool.tensor_tensor(t, t, egc[:, b * GH:b * GH + GH], ALU.mult).then_inc(g_scaled, 1)

            for lv in range(LEVELS):
                for m in range(3):
                    if lv == 0:
                        pool.wait_ge(g_gram, 2 * m + 1)
                    else:
                        pool.wait_ge(i_y_mm, 3 * (lv - 1) + m + 1)
                        if lv == 1:
                            pool.wait_ge(i_inv, m + 1)
                    s8 = slice(8 * m, 8 * m + 8)
                    mask = bc(C("level", lv * GC, GC).rearrange("p (a d) -> p a d", a=1), P, 8, GC)
                    pool.tensor_tensor(off_t[:, s8], sys_t[:, s8], mask, ALU.mult).then_inc(i_off, 1)
                if 1 <= lv <= 4:
                    if lv == 1:
                        pool.wait_ge(g_gram_mm, 6)
                        pool.wait_ge(g_decay, 6)
                    scale(lv - 1)


def unit_columns(w, first, count, width=P):
    v = w[:, first:first + count * width].reshape(8, P, count, width)
    return v.transpose(1, 2, 0, 3).reshape(P, count, 8 * P)


def unit_rows(w):
    return w.reshape(-1, P, D_MODEL).transpose(1, 0, 2)


def kernel(**inputs):
    import concourse.bacc as bacc
    from concourse.bass_utils import run_bass_kernel_spmd

    v = {k: np.asarray(a) for k, a in inputs.items()}
    zeros = np.zeros((D_MODEL, P - 24), np.float32)

    def mixer_units(w, n_z, n_conv, n_att, gates_at, z_at, conv_at, att_at):
        gates = np.concatenate([w[:, gates_at:gates_at + 24], zeros], axis=1)
        return [unit_columns(gates, 0, 1), unit_columns(w, conv_at, n_conv), unit_columns(w, att_at, n_att),
                unit_columns(w, z_at, n_z)]

    def ffn_units(layer):
        w = v["ffn_w_up"][layer]
        both = np.stack([unit_columns(w, 0, FT), unit_columns(w, FT * P, FT)], axis=2)
        return [both.reshape(P, 2 * FT, 8 * P), unit_rows(v["ffn_w_down"][layer])]

    ab, cd = v["ab_w_in"][0], v["cd_w_in"][0]
    w_stream = np.ascontiguousarray(np.concatenate(
        mixer_units(ab, ZT, XBC_T, 6, 4096, 0, 1536, 4120) + [unit_rows(v["ab_w_out"][0])] + ffn_units(0)
        + mixer_units(cd, ZT, GQ_T, 12, 6144, 4608, 0, 6168) + [unit_rows(v["cd_w_out"][0])] + ffn_units(1), axis=1))
    ada_stream = np.ascontiguousarray(np.concatenate([unit_columns(v["ada_w"][layer], 0, 48) for layer in range(2)], axis=1))
    prm = np.concatenate([v[k].reshape(-1, P) for k in ("c", "ada_b", "norm_w", "ssd_conv_w", "ssd_conv_b", "ssd_norm_w",
                                                        "gdn_conv_w", "gdn_norm_w", "ffn_conv_w", "ffn_conv_b")])
    prm = np.concatenate([prm, np.zeros((PRM_G * P - PRM_COLS, P), np.float32)]).reshape(PRM_G, P, P).transpose(1, 0, 2)
    rows = np.concatenate([v[k].reshape(1, -1) for k in ("ssd_dt_bias", "ssd_a_log", "ssd_d", "swa_sinks", "gdn_dt_bias",
                                                         "gdn_a_log")], axis=1)
    arrays = {
        "w_stream": w_stream, "ada_stream": ada_stream,
        "x_tiles": np.ascontiguousarray(v["x"][0].T.reshape(DT, P, SEQ).transpose(1, 0, 2)),
        "prm": np.ascontiguousarray(prm), "rows": np.ascontiguousarray(rows),
        "constants": constants(), "buckets": bucket_rows(), "rel_bias": np.ascontiguousarray(v["rel_bias"]),
    }
    nc = bacc.Bacc("TRN2", target_bir_lowering=False, num_devices=1)
    aps = [nc.dram_tensor(f"in_{k}", a.shape, mybir.dt.from_np(a.dtype), kind="ExternalInput").ap() for k, a in arrays.items()]
    scratch = nc.dram_tensor("bias_scratch", (AH, 2, 384), F32).ap()
    out = nc.dram_tensor("out_tiles", (P, DT, SEQ), F32, kind="ExternalOutput").ap()
    build(nc, *aps, scratch, out)
    r = run_bass_kernel_spmd(nc, [{f"in_{k}": a for k, a in arrays.items()}], core_ids=[0])
    got = r.results[0]["out_tiles"]
    return np.ascontiguousarray(got.transpose(1, 0, 2).reshape(D_MODEL, SEQ).T).reshape(1, SEQ, D_MODEL)
```

```python
from contextlib import ExitStack

import numpy as np

import concourse.bass as bass
from concourse import mybir

F32 = mybir.dt.float32
F32R = mybir.dt.float32r
ACT = mybir.ActivationFunctionType
ALU = mybir.AluOpType
AX = mybir.AxisListType
ds = bass.ds

P = 128
D_MODEL, SEQ = 1024, 256
DT = D_MODEL // P
NB = SEQ // P
AH, AD = 8, 64
SSD_H, SSD_P, SSD_G = 24, 64, 4
HPG = SSD_H // SSD_G
GH, GD, GC = 12, 128, 64
FT = 2816 // P
NEG = -1e30
EPS_COL = 1e-6

XBC_T, ZT, GQ_T, MIX_T = 20, 12, 36, 16


def layout():
    parts, n = {}, 0
    for name, count in (("dt0", 1), ("conv0", XBC_T), ("q0", 4), ("k0", 1), ("v0", 1), ("z0", ZT), ("out0", MIX_T),
                        ("up0", 2 * FT), ("down0", FT), ("dt1", 1), ("conv1", GQ_T), ("q1", 4), ("k1", 4), ("v1", 4),
                        ("z1", ZT), ("out1", MIX_T), ("up1", 2 * FT), ("down1", FT)):
        parts[name] = (n, count)
        n += count
    return parts, n


PARTS, UNITS = layout()
ADA_UNITS = 2 * 6 * DT
ADA_WITH = {"q0": 16, "k0": 20, "out0": 40, "down0": 52, "q1": 72, "k1": 76, "out1": 80, "down1": 92}
ADA_SUMMED = list(range(16, 22)) + list(range(40, ADA_UNITS))
ADA_SSD = range(28, 40)
C_COL = 39

PRM, PRM_COLS = {}, 0
for _name, _rows in (("c", 8), ("ada_b", 96), ("norm", 64), ("conv0_w", 80), ("conv0_b", 20), ("ssd_norm", 12),
                     ("conv1_w", 144), ("gdn_norm", 1), ("up_w", 264), ("up_b", 88)):
    PRM[_name] = PRM_COLS
    PRM_COLS += _rows
PRM_G = -(-PRM_COLS // P)

ROW = {"dt_bias0": 0, "a_log0": 24, "d": 48, "sinks": 72, "dt_bias1": 80, "a_log1": 92}
ROW_COLS = 104

LEVELS = 6
CST, CST_COLS = {}, 0
for _name, _n in (("ident", 128), ("ones", 128), ("triu", 128), ("triu_chunk", 128), ("same_chunk", 128), 
                  ("reverse", 128), ("keep", 128), ("keep_chunk", 64), ("level", LEVELS * 64),
                  ("ident_chunk", 64), ("pick", 255), ("eps", 1)):
    CST[_name] = CST_COLS
    CST_COLS += _n


def constants():
    c = np.zeros((P, CST_COLS), np.float32)
    p, f = np.arange(P)[:, None], np.arange(P)[None, :]
    put = lambda name, v: c.__setitem__((slice(None), slice(CST[name], CST[name] + v.shape[1])), v)
    put("ident", np.eye(P))
    put("ones", np.ones((P, P)))
    put("triu", p <= f)
    put("triu_chunk", (p <= f) & (p // GC == f // GC))
    put("same_chunk", p // GC == f // GC)
    put("reverse", p + f == P - 1)
    put("keep", np.where(f >= p, -NEG, NEG))
    s, t = p % GC, np.arange(GC)[None, :]
    put("keep_chunk", np.where(t >= s, -NEG, NEG))
    for lv in range(LEVELS):
        b = 1 << lv
        m = (s // (2 * b) == t // (2 * b)) & (s // b % 2 == 0) & (t // b % 2 == 1)
        c[:, CST["level"] + lv * GC:CST["level"] + (lv + 1) * GC] = m
    put("ident_chunk", s == t)
    put("pick", np.broadcast_to(np.arange(255) == 127, (P, 255)))
    put("eps", np.full((P, 1), EPS_COL))
    return c


def bucket_rows():
    starts = [0, 1, 2, 3, 4, 5, 6, 7, 8, 9, 10, 11, 12, 13, 14, 15, 16, 21, 27, 35, 46, 59, 77, 99, 128, 166, 216]
    r = np.zeros((33, 2, 384), np.float32)
    for v in range(2):
        for i in range(384):
            dist = 255 - i
            if dist < 0 or (v == 0 and dist >= 128):
                r[32, v, i] = NEG
            else:
                r[sum(dist >= s for s in starts) - 1, v, i] = 1
    return r


def build(nc, w_dram, ada_dram, x_dram, prm_dram, row_dram, cst_dram, bucket_dram, rel_dram, scratch, out_dram):
    with ExitStack() as ctx:
        sem = lambda name: ctx.enter_context(nc.semaphore(name))
        cursor = [-(-nc.sbuf_base // 32) * 32]

        def sb(name, shape, dt=F32, at=None):
            size = int(np.prod(shape[1:])) * 4
            off = cursor[0] if at is None else at
            t = nc.alloc_sbuf_tensor_at(name, [P] + list(shape[1:]), dt, offset=off)
            if at is None:
                cursor[0] += -(-size // 32) * 32
            return t

        def region(size):
            at = -(-cursor[0] // 32) * 32
            cursor[0] = at + size
            return at

        KB = 1024
        x = sb("x", [P, DT, SEQ])
        h_hi = sb("h_hi", [P, DT, SEQ], F32R)
        h_lo = sb("h_lo", [P, DT, SEQ], F32R)
        raw = sb("raw", [P, 4, 8, P])
        w_hi = sb("w_hi", [P, 4, 4, P], F32R)
        w_lo = sb("w_lo", [P, 4, 4, P], F32R)
        cst = sb("cst", [P, CST_COLS])
        prm = sb("prm", [P, PRM_G * P])
        rows = sb("rows", [P, ROW_COLS])
        mods = sb("mods", [P, 2, 6, DT])
        gain = sb("gain", [P, 2, 4, DT])
        c_cols = sb("c_cols", [P, DT])
        small = sb("small", [P, 36, 48])
        at_hi, at_lo = region(22 * KB), region(22 * KB)
        a_hi = sb("a_hi", [P, 22, SEQ], F32R, at=at_hi)
        a_lo = sb("a_lo", [P, 22, SEQ], F32R, at=at_lo)
        arena = region(78 * KB)
        extra = region(12 * KB)
        c_silu = sb("c_silu", [P, DT, P + C_COL], at=extra)
        ada_first = sb("ada_first", [P, 4, 8, P], at=arena + 62 * KB)
        ada_ssd = sb("ada_ssd", [P, 4, 8, P], at=at_hi)
        ada_long = sb("ada_long", [P, 8, 8, P], at=arena + 30 * KB)
        ada_sum = sb("ada_sum", [P, 2, 2, P], at=extra + 10 * KB)
        assert cursor[0] <= nc.sbuf_usable_end, (cursor[0], nc.sbuf_usable_end)
        conv0 = sb("conv0", [P, XBC_T, SEQ], at=arena)
        conv1 = sb("conv1", [P, GQ_T, SEQ], at=arena)
        convs = (conv0, conv1)
        zs = sb("zs", [P, ZT, SEQ], at=arena + 36 * KB)
        sq = sb("sq", [P, DT, SEQ], at=arena)
        yr = sb("yr", [P, DT, SEQ], at=arena + 8 * KB)
        yg = sb("yg", [P, 2, SEQ], at=arena + 24 * KB)
        yv = sb("yv", [P, 2, SEQ], at=arena + 26 * KB)
        prod = sb("prod", [P, 2, SEQ], at=arena + 28 * KB)
        prm_rows = sb("prm_rows", [P, PRM_G, P], at=arena + 30 * KB)
        bucket = sb("bucket", [P, 2, 384], at=arena + 34 * KB)
        rel = sb("rel", [P, 8], at=arena + 37 * KB)
        bias_vec = sb("bias_vec", [P, 2, 384], at=arena + 38 * KB)
        scores = sb("scores", [P, AH, 384], at=at_hi)
        probs_t = sb("probs_t", [P, 2, 384], at=at_hi + 12 * KB)
        att_q = sb("att_q", [P, 4, SEQ], at=at_lo)
        att_k = sb("att_k", [P, 4, SEQ], at=at_lo + 4 * KB)
        att_v = sb("att_v", [P, NB, 512], at=at_lo + 8 * KB)
        bias = sb("bias", [P, AH, SEQ], at=arena + 48 * KB)
        hankels = (sb("hankel0", [P, AH, SEQ], at=arena + 20 * KB), sb("hankel1", [P, AH, SEQ], at=at_hi))
        xs_tok = sb("xs_tok", [P, NB, 1536], at=arena + 20 * KB)
        b_tok = sb("b_tok", [P, SSD_G, P], at=arena + 32 * KB)
        cb = sb("cb", [P, NB, SSD_G, P], at=arena + 48 * KB)
        h_in = sb("h_in", [P, 1536], at=arena + 52 * KB)
        xd = sb("xd", [P, 1536], at=arena + 58 * KB)
        lmat = sb("lmat", [P, 2, 4, P], at=arena + 64 * KB)
        mmat = sb("mmat", [P, 2, 4, P], at=arena + 68 * KB)
        cexp = sb("cexp", [P, 2, 4, P], at=arena + 72 * KB)
        y_ssd = sb("y_ssd", [P, ZT, SEQ], at=at_lo)
        y_sq = sb("y_sq", [P, 2, 3, SEQ], at=arena + 64 * KB)
        y_mix = sb("y_mix", [P, ZT, SEQ], at=arena)
        NS = NB * GH
        v_tok = sb("v_tok", [P, NB, GH, GD], at=arena + 48 * KB)
        k_tok = sb("k_tok", [P, NB, GH, GD], at=arena + 24 * KB)
        attn_t = sb("attn_t", [P, NS, GC], at=arena + 60 * KB)
        state = sb("state", [P, GH, GD], at=arena + 72 * KB)
        dec = sb("dec", [P, NS, GC], at=at_hi)
        sys_t = sb("sys_t", [P, NS, GC], at=at_hi + 6 * KB)
        inv = sb("inv", [P, NS, GC], at=at_hi + 12 * KB)
        step_y = sb("step_y", [P, NS, GC], at=at_hi)
        inv_t = sb("inv_t", [P, NS, GC], at=at_lo + 12 * KB)
        inv_t_bd = sb("inv_t_bd", [P, NS, P], at=at_lo)
        off_bd = sb("off_bd", [P, NS, P], at=arena + 66 * KB)
        egc = sb("egc", [P, NS, P], at=extra)
        step_y_bd = sb("step_y_bd", [P, NS, P], at=extra)
        g_sq = sb("g_sq", [P, 3, 2, SEQ], at=at_hi)
        resid = sb("resid", [P, 2, 4, GD], at=at_hi + 8 * KB)
        v_new = sb("v_new", [P, 3, 4, GD], at=at_hi + 12 * KB)
        o_sq = sb("o_sq", [P, 3, 2, SEQ], at=arena + 48 * KB)
        o_t = sb("o_t", [P, 3, 2, SEQ], at=arena + 54 * KB)

        PB = [ctx.enter_context(nc.psum_tensor(f"proj{i}", [P, 512], F32)) for i in range(4)]
        AB = [ctx.enter_context(nc.psum_tensor(f"acc{i}", [P, 512], F32)) for i in range(4)]
        BANKS = PB + AB
        ada_ps = AB[3]

        def C(name, a=0, n=None, p0=0, p1=P):
            n = n or 128
            return cst[p0:p1, CST[name] + a:CST[name] + a + n]

        EPS = cst[:, CST["eps"]:CST["eps"] + 1]
        acc = lambda k: AB[k // 2][:, (k % 2) * SEQ:(k % 2 + 1) * SEQ]
        tile_at = lambda k: k if k < 12 else k + 6

        in_landed = [sem(f"in_landed{i}") for i in range(5)]
        bias_vec_stored, hankel_landed, out_stored = sem("bias_vec_stored"), sem("hankel_landed"), sem("out_stored")
        w_landed = [sem(f"w_landed{i}") for i in range(4)]
        ada_landed = [sem(f"ada_landed{i}") for i in range(8)]
        w_rounded, w_split, w_used = sem("w_rounded"), sem("w_split"), sem("w_used")
        ada_terms, ada_added, mods_read = sem("ada_terms"), sem("ada_added"), sem("mods_read")
        act_step, dve_step = sem("act_step"), sem("dve_step")
        rel_ones, prm_turned, prm_ready, c_ready = (sem(n) for n in ("rel_ones", "prm_turned", "prm_ready", "c_ready"))
        vec_mm, vec_copied, hankel_mm, bias_ready = (sem(n) for n in ("vec_mm", "vec_copied", "hankel_mm", "bias_ready"))
        squares, sums, roots, scaled, h_rounded, h_ready, x_ready = (
            sem(n) for n in ("squares", "sums", "roots", "scaled", "h_rounded", "h_ready", "x_ready"))
        inv_rms, spread, y_scaled = sem("inv_rms"), sem("spread"), sem("y_scaled")
        z_silu, zeroed, c_zeroed = sem("z_silu"), sem("zeroed"), sem("c_zeroed")
        dt_read, conv_first, conv_taps, conv_done = (sem(n) for n in ("dt_read", "conv_first", "conv_taps", "conv_done"))
        copied = sem("copied")
        up_first, up_taps, gelu_done, prod_done, g_rounded, g_ready = (
            sem(n) for n in ("up_first", "up_taps", "gelu_done", "prod_done", "g_rounded", "g_ready"))
        s_scored, s_biased, s_max, s_exp, s_norm = (sem(n) for n in ("s_scored", "s_biased", "s_max", "s_exp", "s_norm"))
        s_turned, s_copied, s_out, s_rounded, s_ready = (
            sem(n) for n in ("s_turned", "s_copied", "s_out", "s_rounded", "s_ready"))
        gate_abs, gate_exp, gate_ln, gate_ready = (sem(n) for n in ("gate_abs", "gate_exp", "gate_ln", "gate_ready"))
        d_item_mm, d_item, d_cum_mm, d_cum, d_tail, d_xd = (sem(n) for n in ("ssd_item_mm", "ssd_item", "ssd_cum_mm", "ssd_cum", "ssd_tail", "ssd_xd"))
        d_decay_mm, d_diff, d_decay, d_mmat, d_y_mm, d_y = (
            sem(n) for n in ("ssd_decay_mm", "ssd_diff", "ssd_decay", "ssd_mmat", "ssd_y_mm", "ssd_y"))
        d_gated, d_sq, d_sum, d_root, d_inv, d_spread, d_mix, d_rounded, mix_ready = (
            sem(n) for n in ("ssd_gated", "ssd_sq", "ssd_sum", "ssd_root", "ssd_inv", "ssd_spread", "ssd_mix", "ssd_rounded", "mix_ready"))
        n_sq, n_sum, n_root, n_inv, n_spread, n_unit = (
            sem(n) for n in ("l2_sq", "l2_sum", "l2_root", "l2_inv", "l2_spread", "l2_unit"))
        v_turned, v_copied, k_turned, k_copied = (sem(n) for n in ("v_turned", "v_copied", "k_turned", "k_copied"))
        g_cum_mm, g_cum, g_tail, g_tot = (sem(n) for n in ("gdn_cum_mm", "gdn_cum", "gdn_tail", "gdn_total"))
        g_decay_mm, g_diff, g_decay, g_gram_mm, g_gram = (
            sem(n) for n in ("gdn_decay_mm", "gdn_diff", "gdn_decay", "gdn_gram_mm", "gdn_gram"))
        i_off, i_y_mm, i_y, i_y_bd, i_z_mm, i_zt_mm, i_inv, i_bd = (
            sem(n) for n in ("inv_off", "inv_y_mm", "inv_y", "inv_y_bd", "inv_z_mm", "inv_zt_mm", "inv_done", "inv_bd"))
        g_scaled = sem("gdn_scaled")
        c_ks_mm, c_resid, c_tr_mm, c_vnew, c_o_mm, c_o, c_u_mm, c_state = (
            sem(n) for n in ("scan_ks_mm", "scan_resid", "scan_tr_mm", "scan_vnew", "scan_o_mm", "scan_o", "scan_u_mm", "scan_state"))
        o_sqd, o_sum, o_root, o_inv, o_spread, o_mixed, o_rounded = (
            sem(n) for n in ("o_sqd", "o_sum", "o_root", "o_inv", "o_spread", "o_mixed", "o_rounded"))

        freed = {}
        totals = {}
        for name, (n0, cnt) in PARTS.items():
            key = {"dt": (dt_read, 1), "conv": (conv_taps, 3), "up": (up_taps, 2)}.get(name[:-1], (copied, 1))
            if name[:-1] in ("out", "down"):
                continue
            for n in range(n0, n0 + cnt):
                at = totals.get(name[:-1] if key[1] > 1 else str(key[0]), 0) + key[1]
                totals[name[:-1] if key[1] > 1 else str(key[0])] = at
                freed[n] = (key[0], at, key[1])

        def bank_id(n):
            name = next(q for q, (n0, cnt) in PARTS.items() if n0 <= n < n0 + cnt)
            return n % 4 if name[:-1] in ("dt", "conv", "up") else n % 2

        banks = {n: PB[bank_id(n)] for n in freed}
        before = {n: max((m for m in freed if m < n and bank_id(m) == bank_id(n)), default=None) for n in freed}

        def units(e, name, step):
            cnt = PARTS[name][1]
            for k in range(min(4, cnt)):
                step(k, 0, k)
            span = 8 if name[:-1] == "down" else 4
            groups = 0 if name[:-1] == "out" else max(cnt - 4, 0) // span
            if groups > 0:
                with e.Fori(0, groups) as g:
                    i = g * (span // 4)
                    for j in range(4, 4 + span):
                        step(4 * i + j, i, j)
            for k in range(min(4, cnt) + span * groups, cnt):
                step(k, 0, k)

        def w_half(n, a):
            s = (2 * n + a) % 4
            return w_hi[:, s], w_lo[:, s], raw[:, n % 4, 4 * a:4 * a + 4]

        def ada_slots(m, count=1):
            ring, size = (ada_ssd, 4) if m in ADA_SSD else (ada_long, 8) if 40 <= m < 72 or m >= 80 else (ada_first, 4)
            return ring[:, m % size:m % size + count], size

        ada_pair = lambda m: ADA_SUMMED.index(m) // 2

        names = {}

        def S(name, a=0, n=48, p0=0, p1=P):
            names.setdefault(name, len(names))
            assert len(names) <= 36
            return small[p0:p1, names[name], a:a + n]

        def bc(ap, *shape):
            return ap.broadcast_to(list(shape))

        def one(ap):
            return ap.rearrange("p (a t) -> p a t", a=1)

        last_copy = {q: freed[PARTS[q][0] + PARTS[q][1] - 1][1] for q in ("k0", "v0", "z0", "k1", "v1", "z1")}
        O_BANK = (AB[3], PB[2])
        Y_BANK = (AB[2], AB[3], PB[2])
        FIRST_AFTER = [PARTS[q][0] % 4 for q in ("dt0", "up0", "up0", "dt1", "dt1", "up1", "up1", "up1")]
        SUM_BANK = [PB[(f + 2) % 4] for f in FIRST_AFTER]
        ROW_BANK = [PB[(f + 1) % 4] for f in FIRST_AFTER]
        ADA_BANK = {"q0": PB[3], "k0": PB[3], "v0": PB[3], "out0": PB[2], "down0": PB[0], "q1": PB[3], "k1": PB[3], "v1": PB[3],
                    "out1": PB[1], "down1": PB[2]}
        ADA_AFTER = {("q0", 3): 16, ("k0", 0): 18, ("v0", 0): 20, ("down0", 3): 52, ("down0", 21): 70, ("q1", 3): 72,
                     ("k1", 1): 74, ("k1", 3): 76, ("v1", 1): 78, ("down1", 3): 92, ("down1", 21): 94}
        for k in range(3, 15, 2):
            ADA_AFTER["out0", k], ADA_AFTER["out1", k] = 40 + k - 3, 80 + k - 3

        def k_tail(name, k):
            count = {"k0": 0, "out0": 12, "down0": 20, "out1": 12}.get(name, 4)
            return k >= count if isinstance(k, int) else count <= 4

        SCAN = [(c, g) for c in range(SEQ // GC) for g in range(GH // 4)]
        block = ctx.enter_context(nc.Block())

        @block.sync
        def _(sp):
            def load_w(n, i=0):
                if n >= 4:
                    sp.wait_ge(w_split, 8 * i + 2 * n - 6)
                sp.dma_start(raw[:, n % 4].rearrange("p (o a) b -> p o (a b)", o=1),
                             w_dram[:, ds(4 * i + n, 1), :]).then_inc(w_landed[n % 4], 16)

            def load_ada(m, i=0):
                slot, size = ada_slots(m)
                if m not in (40, 41, 42, 43, 44, 45, 46, 47, 72, 73, 74, 75, 80, 81, 82, 83, 84, 85, 86, 87):
                    if m - size in ADA_SUMMED:
                        sp.wait_ge(ada_terms, 8 * ada_pair((m - size) // 2 * 2) + 8 + 16 * i)
                    elif m >= size:
                        sp.wait_ge(ada_added, m - size + 1)
                sp.dma_start(slot.rearrange("p o a b -> p o (a b)"), ada_dram[:, ds(4 * i + m, 1), :]).then_inc(ada_landed[m % 8], 16)

            def stream(n0, end, ada0=None, count=0):
                with sp.Fori(0, (count or end - n0) // 4) as i:
                    for j in range(4):
                        load_w(n0 + j, i)
                        if count:
                            load_ada(ada0 + j, i)
                for n in range(n0 + (count or end - n0) // 4 * 4, end):
                    load_w(n)

            def hankel_load(v):
                src = bass.AP(tensor=scratch.tensor, offset=v * 384, ap=[[1, P], [768, AH], [1, SEQ]])
                sp.dma_start(hankels[v][:, :, :], src).then_inc(hankel_landed, 16)

            sp.dma_start(prm_rows[:, :, :], prm_dram).then_inc(in_landed[0], 16)
            sp.dma_start(cst[:, :], cst_dram).then_inc(in_landed[1], 16)
            load_ada(0)
            load_ada(1)
            load_ada(2)
            load_ada(3)
            sp.dma_start(x[:, :, :], x_dram).then_inc(in_landed[2], 16)
            sp.dma_start(rows[:, :], row_dram.broadcast_to([P, ROW_COLS])).then_inc(in_landed[3], 16)
            sp.dma_start(bucket[0:33, :, :], bucket_dram).then_inc(in_landed[4], 16)
            sp.dma_start(rel[0:32, :], rel_dram).then_inc(in_landed[4], 16)
            for n in range(4):
                load_w(n)
            for m in range(4, 16):
                load_ada(m)
            sp.wait_ge(vec_copied, 1)
            sp.dma_start(scratch, bias_vec[0:AH, :, :]).then_inc(bias_vec_stored, 16)
            sp.wait_ge(bias_vec_stored, 16)
            hankel_load(0)
            n_q0, n_z0, n_out0, n_up0, n_down0, n_q1, n_out1, n_up1 = (
                PARTS[q][0] for q in ("q0", "z0", "out0", "up0", "down0", "q1", "out1", "up1"))
            stream(4, n_q0 + 2)
            for k in range(6):
                load_w(n_q0 + 2 + k)
                load_ada(16 + k)
            for k in range(6):
                load_ada(22 + k)
                if k % 2:
                    load_w(n_z0 + 2 + k // 2)
            sp.wait_ge(s_ready, 4)
            for m in range(28, 32):
                load_ada(m)
            stream(n_z0 + 5, n_out0 + 2)
            for m in range(32, 40):
                load_ada(m)
            sp.wait_ge(d_sum, SSD_G)
            for k in range(12):
                load_ada(40 + k)
                load_w(n_out0 + 2 + k)
            stream(n_out0 + 14, n_up0 + 4)
            for m in range(52, 60):
                load_ada(m)
            stream(n_up0 + 4, n_down0 + 4)
            for k in range(12):
                load_w(n_down0 + 4 + k)
                load_ada(60 + k)
            stream(n_down0 + 16, n_q1 - 2)
            sp.wait_ge(x_ready, 2 * DT)
            hankel_load(1)
            for m in range(72, 76):
                load_ada(m)
            stream(n_q1 - 2, n_q1 + 4)
            for k in range(4, 8):
                load_w(n_q1 + k)
                load_ada(72 + k)
            stream(n_q1 + 8, n_out1 + 4)
            sp.wait_ge(mix_ready, MIX_T + 12)
            for k in range(12):
                load_ada(80 + k)
                load_w(n_out1 + 4 + k)
            stream(n_out1 + 16, n_up1 + 4)
            for m in range(92, 96):
                load_ada(m)
            stream(n_up1 + 4, UNITS)
            sp.wait_ge(x_ready, 4 * DT)
            sp.dma_start(out_dram, x[:, :, :]).then_inc(out_stored, 16)
            sp.wait_ge(out_stored, 16)

        @block.tensor
        def _(pe):
            def mm(out, a, b, start=True, stop=True):
                return pe.matmul(out, a, b, start=start, stop=stop, skip_group_check=True)

            def ada_unit(m, bank, first=False):
                pe.wait_ge(ada_landed[m % 8], 16 * (m // 8 + 1))
                for k in range(8):
                    last = mm(bank[:, 0:P], ada_slots(m)[0][:, 0, k], c_silu[:, k, C_COL - m:C_COL - m + P], first and k == 0, k == 7)
                last.then_inc(ada_added, 1)

            def ada_sums(m, i, bank, first=False):
                p = ada_pair(m)
                pe.wait_ge(ada_terms, 8 * p + 8 + 16 * i)
                if not isinstance(i, int):
                    pe.nop(nofuse=True)
                for q in range(2):
                    last = mm(bank[:, 0:P], ada_sum[:, p % 2, q], C("pick", P - 1 - m - q) if isinstance(i, int) else
                              cst[:, ds(CST["pick"] + P - 1 - m - q - 4 * i, P)], first and q == 0, True)
                last.then_inc(ada_added, 2)

            def ada_with(name, k, i, j):
                if isinstance(k, int) and (name, k) in ADA_AFTER:
                    m = ADA_AFTER[name, k]
                    ada_sums(m, 0, ADA_BANK[name], m in (16, 40, 52, 72, 80, 92))
                elif name in ADA_WITH and not k_tail(name, k) and not isinstance(k, int) and j % 2:
                    ada_sums(ADA_WITH[name] + j - 3, i, ADA_BANK[name])

            def project(name, token=False, norm=None, some=None):
                n0 = PARTS[name][0]

                def step(k, i, j):
                    n = n0 + j
                    if before[n] is not None:
                        s, at, per = freed[before[n]]
                        pe.wait_ge(s, 4 * per * i + at)
                    for a in range(2):
                        if norm is not None and j == 0:
                            pe.wait_ge(h_ready, 8 * norm + 4 * a + 4)
                        pe.wait_ge(w_split, 8 * i + 2 * n + a + 1)
                        hi, lo, _ = w_half(n, a)
                        for q in range(4):
                            t = 4 * a + q
                            for p_, (u, v) in enumerate(((hi, h_hi), (hi, h_lo), (lo, h_hi))):
                                st, en = t == 0 and p_ == 0, t == 7 and p_ == 2
                                if token:
                                    for b in range(NB):
                                        c = slice(b * P, b * P + P)
                                        last = mm(banks[n][:, c], v[:, t, c], u[:, q], st and b == 0, en)
                                else:
                                    last = mm(banks[n][:, 0:SEQ], u[:, q], v[:, t], st, en)
                        last.then_inc(w_used, 1)
                    ada_with(name, k, i, j)

                if some is None:
                    units(pe, name, step)
                else:
                    for k in some:
                        step(k, 0, k)

            def accumulate(name, ready, first_ready, at):
                n0, cnt = PARTS[name]

                def step(k, i, j):
                    n = n0 + j
                    if ready is not None:
                        pe.wait_ge(ready, first_ready + k + 1)
                    for a in range(2):
                        pe.wait_ge(w_split, 8 * i + 2 * n + a + 1)
                        hi, lo, _ = w_half(n, a)
                        for q in range(4):
                            t = 4 * a + q
                            s = at(k)
                            for p_, (u, v) in enumerate(((hi, a_hi), (hi, a_lo), (lo, a_hi))):
                                last = mm(acc(t), u[:, q], v[:, ds(s, 1), :], j == 0 and p_ == 0 and t % 2 == 0,
                                          j == cnt - 1 and p_ == 2)
                        last.then_inc(w_used, 1)
                    ada_with(name, k, i, j)

                units(pe, name, step)

            def column_sums(out, tile, col, start, stop):
                for b in range(NB):
                    last = mm(out[:, 0:P], tile[:, b * P:b * P + P], C("pick", P - 1 - col - b), start and b == 0, stop)
                return last

            def spread_rows(out, cols):
                for b in range(NB):
                    last = mm(out[:, b * P:b * P + P], bc(cols[:, b:b + 1], P, P), C("ident"))
                return last

            def root_mean_square(event):
                for k in range(DT):
                    pe.wait_ge(squares, event * DT + k + 1)
                    last = column_sums(SUM_BANK[event], sq[:, k], 0, k == 0, k == DT - 1)
                last.then_inc(sums, 1)
                pe.wait_ge(inv_rms, event + 1)
                spread_rows(ROW_BANK[event], S("inv_rms", 0, 2)).then_inc(spread, 1)

            def bias_tiles(layer):
                pe.wait_ge(hankel_landed, 16 * (layer + 1))
                for q in range(4):
                    last = mm(AB[q][:, :], C("reverse"), hankels[layer][:, 2 * q:2 * q + 2, :])
                last.then_inc(hankel_mm, 1)

            def attention(layer):
                n8 = AH * layer
                pe.wait_ge(bias_ready, layer + 1)
                pe.wait_ge(conv_taps, 3 * (XBC_T + layer * GQ_T))
                pe.wait_ge(copied, last_copy[f"k{layer}"])
                for h in range(AH):
                    p0, t = AD * (h % 2), h // 2
                    q_, k_ = att_q[p0:p0 + AD, t], att_k[p0:p0 + AD, t if layer else h // 4]
                    if h >= 3:
                        pe.wait_ge(s_biased, 2 * (n8 + h - 2))
                    mm(AB[h % 3][:, 0:SEQ], q_[:, P:2 * P], k_[:, 0:SEQ])
                    mm(AB[h % 3][:, SEQ:SEQ + P], q_[:, 0:P], k_[:, 0:P]).then_inc(s_scored, 1)
                if layer == 0:
                    project("z0", some=(0,))
                    for m in range(3):
                        ada_unit(22 + 2 * m, PB[3])
                        ada_unit(23 + 2 * m, PB[3])
                        if m < 2:
                            project("z0", some=(m + 1,))
                else:
                    project("v1", token=True)
                pe.wait_ge(copied, last_copy[f"v{layer}"])

                def values(h):
                    p0, t = AD * (h % 2), h // 2
                    c0 = AD * (h if layer else h // 4)
                    o, pt = O_BANK[t % 2][p0:p0 + AD], probs_t[:, h % 2]
                    pe.wait_ge(s_copied, n8 + h + 1)
                    if t >= 2:
                        pe.wait_ge(s_ready, 4 * layer + t - 1)
                    mm(o[:, 0:P], att_v[:, 0, c0:c0 + AD], pt[:, 2 * P:3 * P])
                    mm(o[:, P:2 * P], att_v[:, 0, c0:c0 + AD], pt[:, 0:P], True, False)
                    mm(o[:, P:2 * P], att_v[:, 1, c0:c0 + AD], pt[:, P:2 * P], False, True).then_inc(s_out, 1)

                for h in range(AH):
                    pe.wait_ge(s_norm, n8 + h + 1)
                    if h >= 3:
                        pe.wait_ge(s_copied, n8 + h - 2)
                    for b in range(3):
                        last = pe.transpose(AB[h % 3][:, b * P:b * P + P], scores[:, h, b * P:b * P + P], C("ident"))
                    last.then_inc(s_turned, 1)
                    if h:
                        values(h - 1)
                values(AH - 1)
                pe.wait_ge(s_ready, 4 * (layer + 1))

            def ssd_outputs(n):
                b, h0 = n // 6, 4 * (n % 6)
                pe.wait_ge(d_mmat, n + 1)
                if n >= 3:
                    pe.wait_ge(d_y, n - 2)
                for q in range(4):
                    h = h0 + q
                    p0 = SSD_P * (h % 2)
                    o, f = Y_BANK[n % 3][p0:p0 + SSD_P, (q // 2) * P:(q // 2 + 1) * P], slice(SSD_P * h, SSD_P * h + SSD_P)
                    last = mm(o, xs_tok[:, b, f], mmat[:, n % 2, q], True, b == 0)
                    if b:
                        last = mm(o, h_in[:, f], cexp[:, n % 2, q], False, True)
                last.then_inc(d_y_mm, 1)

            def ssd():
                pe.wait_ge(conv_done, XBC_T)

                def item(m):
                    if m >= 4:
                        pe.wait_ge(d_item, m - 3)
                    return AB[m % 4]

                for m in range(7):
                    bank = item(m)
                    for q in range(4):
                        t, b = 4 * (m % 3) + q, m // 3
                        src = conv0[:, t, b * P:b * P + P] if m < 6 else conv0[:, 12 + q, 0:P]
                        last = pe.transpose(bank[:, q * P:q * P + P], src, C("ident"))
                    last.then_inc(d_item_mm, 1)
                ada_unit(28, PB[3])
                for b in range(NB):
                    bank = item(7 + b)
                    for g in range(SSD_G):
                        t = slice(b * P, b * P + P)
                        last = mm(bank[:, g * P:g * P + P], conv0[:, 12 + g, t], conv0[:, 16 + g, t])
                    last.then_inc(d_item_mm, 1)
                pe.wait_ge(gate_ready, 1)
                for b in range(NB):
                    mm(PB[2][:, 24 * b:24 * b + 24], C("triu"), S("da", 24 * b, 24))
                mm(PB[2][:, 48:72], C("ones"), S("da", 0, 24)).then_inc(d_cum_mm, 1)
                project("z0", some=(3,))
                ada_unit(29, PB[3])
                pe.wait_ge(d_xd, 1)
                for g in range(SSD_G):
                    mm(item(9 + g)[:, 0:384], b_tok[:, g], xd[:, 384 * g:384 * g + 384]).then_inc(d_item_mm, 1)
                pe.wait_ge(d_cum, 1)
                pe.wait_ge(d_item, 13)
                for n in range(12):
                    b, h0 = n // 6, 4 * (n % 6)
                    if n >= 2:
                        pe.wait_ge(d_decay, n - 1)
                    for q in range(4):
                        col = S("da", 24 * b + h0 + q, 1)
                        last = mm(AB[n % 2][:, q * P:q * P + P], bc(col, P, P), C("triu"))
                    last.then_inc(d_decay_mm, 1)
                    if n < 8:
                        project("z0", some=(4 + n,))
                    for m in ((24 + n,) if n in (6, 7) else (16 + 2 * n, 17 + 2 * n) if n >= 8 else ()):
                        ada_unit(m, PB[3])
                    if n:
                        ssd_outputs(n - 1)
                ssd_outputs(11)
                for g in range(SSD_G):
                    pe.wait_ge(d_sq, g + 1)
                    for k in range(3):
                        last = column_sums(AB[0], y_sq[:, g % 2, k], 2 * g, g == 0 and k == 0, g == 3 and k == 2)
                    last.then_inc(d_sum, 1)
                pe.wait_ge(d_inv, 1)
                for g in range(SSD_G):
                    last = spread_rows(PB[g // 2][:, (g % 2) * SEQ:(g % 2 + 1) * SEQ], S("group_inv", 2 * g, 2))
                    if g % 2:
                        last.then_inc(d_spread, 1)

            def stacks(out, a, b, m):
                for q in range(8):
                    for j in range(2):
                        last = mm(out[j * GC:j * GC + GC, q * GC:q * GC + GC], a(8 * m + q)[:, j * GC:j * GC + GC], b(8 * m + q))
                return last

            def gdn():
                pe.wait_ge(conv_done, XBC_T + GQ_T)
                for n in range(12):
                    pe.wait_ge(n_sq, n + 1)
                    for q in range(2):
                        last = column_sums(PB[2], g_sq[:, n % 3, q], 4 * n + 2 * q, n == 0 and q == 0, n == 11 and q == 1)
                    last.then_inc(n_sum, 1)
                    project("z1", some=(n,))
                    if n % 2 == 0:
                        m = n // 2
                        if m >= 4:
                            pe.wait_ge(v_copied, m - 3)
                        for q in range(4):
                            b, h = (4 * m + q) // GH, (4 * m + q) % GH
                            last = pe.transpose(AB[m % 4][:, q * P:q * P + P], conv1[:, 24 + h, b * P:b * P + P], C("ident"))
                        last.then_inc(v_turned, 1)
                pe.wait_ge(gate_ready, 2)
                either = [bc(C("same_chunk", j * GC, 1), P, P) for j in range(2)]
                for q, summed in enumerate([C("triu_chunk"), C("same_chunk")] + either):
                    last = mm(PB[3][:, 24 * q:24 * q + 24], summed, S("da", 0, 24))
                last.then_inc(g_cum_mm, 1)
                pe.wait_ge(v_copied, 6)
                pe.wait_ge(n_inv, 1)
                for n in range(12):
                    if n >= 4:
                        pe.wait_ge(n_unit, n - 3)
                    for q in range(2):
                        last = spread_rows(AB[n % 4][:, q * SEQ:q * SEQ + SEQ], S("l2_inv", 4 * n + 2 * q, 2))
                    last.then_inc(n_spread, 1)
                pe.wait_ge(copied, last_copy["z1"])
                pe.wait_ge(g_cum, 1)
                for n in range(6):
                    if n >= 2:
                        pe.wait_ge(g_decay, n - 1)
                    for q in range(4):
                        last = mm(PB[n % 2][:, q * P:q * P + P], bc(S("da", 4 * n + q, 1), P, P), C("triu_chunk"))
                    last.then_inc(g_decay_mm, 1)
                pe.wait_ge(n_unit, 12)
                for n in range(6):
                    if n >= 4:
                        pe.wait_ge(k_copied, n - 3)
                    for q in range(4):
                        b, h = (4 * n + q) // GH, (4 * n + q) % GH
                        last = pe.transpose(AB[n % 4][:, q * P:q * P + P], conv1[:, 12 + h, b * P:b * P + P], C("ident"))
                    last.then_inc(k_turned, 1)
                pe.wait_ge(k_copied, 6)
                for m in range(3):
                    for w, rhs in ((0, 12), (1, 0)):
                        bank = 2 * m + w
                        if bank >= 4:
                            pe.wait_ge(g_gram, bank - 3)
                        for q in range(8):
                            b, h = (8 * m + q) // GH, (8 * m + q) % GH
                            for j in range(2):
                                t = slice(b * P + j * GC, b * P + j * GC + GC)
                                last = mm(AB[bank % 4][j * GC:j * GC + GC, q * GC:q * GC + GC], conv1[:, 12 + h, t],
                                          conv1[:, rhs + h, t])
                        last.then_inc(g_gram_mm, 1)
                of, iv, it = (lambda s: off_bd[:, s]), (lambda s: inv[:, s]), (lambda s: inv_t[:, s])
                it_bd, sy, sy_bd = (lambda s: inv_t_bd[:, s]), (lambda s: step_y[:, s]), (lambda s: step_y_bd[:, s])
                pe.wait_ge(g_gram, 6)
                pe.wait_ge(g_decay, 6)
                for lv in range(LEVELS):
                    for m in range(3):
                        pe.wait_ge(i_off, 3 * lv + m + 1)
                        if lv:
                            pe.wait_ge(i_inv, 3 * (lv - 1) + m + 1)
                        stacks(BANKS[m], of, iv if lv else (lambda s: C("ident_chunk", 0, GC)), m).then_inc(i_y_mm, 1)
                    if not lv:
                        continue
                    for m in range(3):
                        at = 3 * (lv - 1) + m + 1
                        if lv < LEVELS - 1:
                            pe.wait_ge(i_y, at)
                            pe.wait_ge(i_bd, at)
                            stacks(BANKS[3 + m], it_bd, sy, m).then_inc(i_z_mm, 1)
                        pe.wait_ge(i_y_bd, at)
                        stacks(BANKS[m], sy_bd, it, m).then_inc(i_zt_mm, 1)
                pe.wait_ge(i_inv, 3 * LEVELS)
                pe.wait_ge(g_scaled, 4)

                def ks(n):
                    c, g = SCAN[n]
                    if not c:
                        return
                    pe.wait_ge(c_state, 3 * (c - 1) + g + 1)
                    for q in range(4):
                        h = 4 * g + q
                        last = mm(BANKS[n % 2][(c % 2) * GC:(c % 2) * GC + GC, q * GD:q * GD + GD],
                                  conv1[:, 12 + h, c * GC:c * GC + GC], state[:, h])
                    last.then_inc(c_ks_mm, 1)

                def tr(n):
                    c, g = SCAN[n]
                    b, r = c // 2, slice((c % 2) * GC, (c % 2) * GC + GC)
                    if c:
                        pe.wait_ge(c_resid, n - 2)
                    if n >= 2:
                        pe.wait_ge(c_vnew, n - 1)
                    for q in range(4):
                        h = 4 * g + q
                        rhs = resid[r, n % 2, q] if c else v_tok[r, b, h]
                        last = mm(BANKS[2 + n % 2][r, q * GD:q * GD + GD], inv_t[r, b * GH + h], rhs)
                    last.then_inc(c_tr_mm, 1)

                def ou(n):
                    c, g = SCAN[n]
                    b, r = c // 2, slice((c % 2) * GC, (c % 2) * GC + GC)
                    pe.wait_ge(c_vnew, n + 1)
                    if n >= 2:
                        pe.wait_ge(c_o, n - 1)
                    for q in range(4):
                        h = 4 * g + q
                        o = BANKS[4 + n % 2][:, q * GC:q * GC + GC]
                        if c:
                            mm(o, state[:, h], conv1[:, h, c * GC:c * GC + GC], True, False)
                        last = mm(o, v_new[r, g, q], attn_t[r, b * GH + h], not c, True)
                    last.then_inc(c_o_mm, 1)
                    if c == 3:
                        return
                    if n >= 2:
                        pe.wait_ge(c_state, n - 1)
                    for q in range(4):
                        last = mm(BANKS[6 + n % 2][:, q * GD:q * GD + GD], k_tok[r, b, 4 * g + q], v_new[r, g, q])
                    last.then_inc(c_u_mm, 1)

                for n in range(len(SCAN) + 2):
                    if n < len(SCAN):
                        ks(n)
                    if 0 <= n - 1 < len(SCAN):
                        tr(n - 1)
                    if n >= 2:
                        ou(n - 2)
                for n in range(6):
                    pe.wait_ge(o_sqd, n + 1)
                    for q in range(2):
                        last = column_sums(PB[0], o_sq[:, n % 3, q], 4 * n + 2 * q, n == 0 and q == 0, n == 5 and q == 1)
                    last.then_inc(o_sum, 1)
                pe.wait_ge(o_inv, 1)
                for n in range(6):
                    if n >= 3:
                        pe.wait_ge(o_mixed, n - 2)
                    for q in range(2):
                        last = spread_rows(PB[1 + n % 3][:, q * SEQ:q * SEQ + SEQ], S("o_inv", 4 * n + 2 * q, 2))
                    last.then_inc(o_spread, 1)

            pe.wait_ge(in_landed[0], 16)
            pe.wait_ge(in_landed[1], 16)
            for g in range(PRM_G):
                last = pe.transpose(PB[g // 4][:, (g % 4) * P:(g % 4 + 1) * P], prm_rows[:, g, :], C("ident"))
            last.then_inc(prm_turned, 1)
            pe.wait_ge(in_landed[4], 32)
            pe.wait_ge(rel_ones, 1)
            for v in range(2):
                last = mm(AB[v][0:AH, 0:384], rel[0:33, :], bucket[0:33, v, :])
            last.then_inc(vec_mm, 1)
            pe.wait_ge(c_ready, 1)
            for m in range(16):
                ada_unit(m, AB[3], first=m == 0)
            pe.wait_ge(prm_ready, 1)
            root_mean_square(0)
            pe.wait_ge(mods_read, 1)
            project("dt0", token=True, norm=0)
            project("conv0")
            pe.wait_ge(vec_copied, 1)
            bias_tiles(0)
            pe.wait_ge(conv_taps, 3 * XBC_T)
            project("q0")
            project("k0")
            project("v0", token=True)
            attention(0)
            ssd()
            accumulate("out0", mix_ready, 0, lambda k: k if not isinstance(k, int) or k < 12 else k + 6)
            root_mean_square(1)
            root_mean_square(2)
            project("up0", norm=1)
            accumulate("down0", g_ready, 0, lambda k: k)
            root_mean_square(3)
            root_mean_square(4)
            project("dt1", token=True, norm=2)
            project("conv1")
            bias_tiles(1)
            pe.wait_ge(conv_taps, 3 * (XBC_T + GQ_T))
            project("q1")
            project("k1")
            attention(1)
            gdn()
            accumulate("out1", mix_ready, MIX_T, lambda k: k if not isinstance(k, int) or k < 12 else k + 6)
            root_mean_square(5)
            root_mean_square(6)
            project("up1", norm=3)
            accumulate("down1", g_ready, FT, lambda k: k)
            root_mean_square(7)

        @block.scalar
        def _(act):
            chain = [0]

            def link(ins):
                chain[0] += 1
                ins.then_inc(act_step, 1)
                act.wait_ge(act_step, chain[0])

            def round_half(n, a, i=0):
                if n >= UNITS:
                    return
                if a == 0:
                    act.wait_ge(w_landed[n % 4], 16 * i + 16 * (n // 4 + 1))
                if 2 * n + a >= 4:
                    act.wait_ge(w_used, 8 * i + 2 * n + a - 3)
                hi, _, src = w_half(n, a)
                act.activation(hi, src, ACT.Copy).then_inc(w_rounded, 1)

            def stream(name, before=None, after=None, some=None):
                n0, cnt = PARTS[name]

                def step(k, i, j):
                    n = n0 + j
                    round_half(n + 2, 0, i)
                    if before is not None:
                        act.wait_ge(w_used, 8 * i + 2 * n + 2)
                        act.nop(nofuse=True)
                        before(k, i, j, banks[n][:, 0:SEQ])
                    round_half(n + 2, 1, i)
                    if after is not None and j:
                        after(k - 1, i, j - 1)

                if some is None:
                    units(act, name, step)
                else:
                    for k in some:
                        step(k, 0, k)
                if after is not None:
                    after(cnt - 1, 0, cnt - 1)

            def conv(layer):
                dst, base = convs[layer], layer * XBC_T
                cnt = (XBC_T, GQ_T)[layer]

                def first(k, i, j, ps):
                    w = prm[:, ds(PRM[f"conv{layer}_w"] + 3 * cnt + k, 1)]
                    b = prm[:, ds(PRM["conv0_b"] + k, 1)] if layer == 0 else 0.0
                    act.activation(dst[:, ds(k, 1), :], one(ps), ACT.Identity, bias=b, scale=w).then_inc(conv_first, 1)

                def silu(k, i, j):
                    act.wait_ge(conv_taps, 3 * (base + k) + 3)
                    act.nop(nofuse=True)
                    act.activation(dst[:, ds(k, 1), :], dst[:, ds(k, 1), :], ACT.Silu).then_inc(conv_done, 1)

                stream(f"conv{layer}", first, silu)

            def up(layer):
                base = 2 * FT * layer

                def first(k, i, j, ps):
                    half, s = j % 2, j // 2 % 2
                    col = half * FT + 2 * i + j // 2
                    w = prm[:, ds(PRM["up_w"] + (3 * layer + 2) * 2 * FT + col, 1)]
                    b = prm[:, ds(PRM["up_b"] + layer * 2 * FT + col, 1)]
                    act.activation((yv if half else yg)[:, s], ps, ACT.Identity, bias=b, scale=w).then_inc(up_first, 1)

                def finish(k, i, j):
                    s = j // 2 % 2
                    pair = 2 * i + j // 2
                    if j % 2 == 0:
                        act.wait_ge(up_taps, 2 * (base + k) + 2)
                        act.activation(yg[:, s], yg[:, s], ACT.Gelu_apprx_tanh).then_inc(gelu_done, 1)
                    else:
                        act.wait_ge(prod_done, FT * layer + pair + 1)
                        act.nop(nofuse=True)
                        act.activation(a_hi[:, ds(pair, 1), :], prod[:, s:s + 1], ACT.Copy).then_inc(g_rounded, 1)

                stream(f"up{layer}", first, finish)

            def copy_unit(fn, dst):
                return lambda k, i, j, ps: act.activation(dst(k), ps, fn).then_inc(copied, 1)

            def root(event, scale=1.0 / D_MODEL):
                act.wait_ge(sums, event + 1)
                act.activation(S("rms", 0, 2), SUM_BANK[event][:, 0:2], ACT.Sqrt, bias=EPS, scale=scale).then_inc(roots, 1)

            def pre_norm(event, layer, which, after):
                for q in range(4):
                    if after is None:
                        if q == 0:
                            act.wait_ge(in_landed[2], 16)
                    else:
                        act.wait_ge(x_ready, 8 * after + 2 * q + 2)
                    act.activation(sq[:, 2 * q:2 * q + 2], x[:, 2 * q:2 * q + 2], ACT.Square).then_inc(squares, 2)
                if after is None:
                    round_half(0, 0)
                    round_half(0, 1)
                    round_half(1, 0)
                    round_half(1, 1)
                root(event)
                norm = 2 * layer + which
                for k in range(DT):
                    act.wait_ge(scaled, DT * norm + k + 1)
                    act.activation(h_hi[:, k], yr[:, k], ACT.Identity, bias=mods[:, layer, 3 * which, k:k + 1]).then_inc(h_rounded, 1)

            def post_norm(event, name):
                act.wait_ge(w_used, 2 * (PARTS[name][0] + PARTS[name][1]))
                for q in range(4):
                    act.activation(sq[:, 2 * q:2 * q + 2].rearrange("p a t -> p (a t)"), AB[q][:, :], ACT.Square).then_inc(squares, 2)
                root(event)

            def attention(layer):
                n8 = AH * layer
                act.wait_ge(s_max, layer + 1)
                for h in range(AH):
                    act.activation(scores[:, h, 0:SEQ], scores[:, h, 0:SEQ], ACT.Exp, bias=S("neg_max", h, 1),
                                   accum_out=S("prob_sum", h, 1)).then_inc(s_exp, 1)
                    act.activation(scores[:, h, SEQ:384], scores[:, h, SEQ:384], ACT.Exp, bias=S("neg_max", 8 + h, 1),
                                   accum_out=S("prob_sum", 8 + h, 1)).then_inc(s_exp, 1)
                if layer == 0:
                    act.activation(S("sink_exp", 0, 16), S("sink_exp", 0, 16), ACT.Exp).then_inc(s_exp, 1)
                if layer == 0:
                    stream("z0", copy_z, some=(0, 1, 2))
                else:
                    stream("v1", values)
                for h in range(AH):
                    act.wait_ge(s_turned, n8 + h + 1)
                    if h >= 2:
                        act.wait_ge(s_out, n8 + h - 1)
                    act.activation(probs_t[:, h % 2], AB[h % 3][:, 0:384], ACT.Copy).then_inc(s_copied, 1)
                    if h % 2 == 1 and h >= 3:
                        attention_out(layer, h // 2 - 1)
                attention_out(layer, 3)

            def attention_out(layer, t):
                act.wait_ge(s_out, AH * layer + 2 * t + 2)
                act.activation(a_hi[:, 18 + t], O_BANK[t % 2][:, 0:SEQ], ACT.Copy).then_inc(s_rounded, 1)

            def gates(layer):
                n = 48 if layer == 0 else 24
                heads = (SSD_H, GH)[layer]
                act.wait_ge(gate_abs, layer + 1)
                act.activation(S("e", 0, n), S("abs", 0, n), ACT.Exp, scale=-1.0).then_inc(gate_exp, 1)
                act.activation(S("a", 0, heads), rows[:, ROW[f"a_log{layer}"]:ROW[f"a_log{layer}"] + heads], ACT.Exp).then_inc(gate_exp, 1)
                act.activation(S("be", 0, 24), S("bx", 0, 24), ACT.Exp, scale=-1.0).then_inc(gate_exp, 1)
                act.wait_ge(gate_ln, layer + 1)
                act.activation(S("ln", 0, n), S("u", 0, n), ACT.Ln).then_inc(gate_exp, 1)

            def copy_z(k, i, j, ps):
                act.activation(zs[:, k], ps, ACT.Copy).then_inc(copied, 1)

            def silu_z(layer):
                act.wait_ge(copied, last_copy[f"z{layer}"])
                for g in range(4):
                    act.activation(zs[:, 3 * g:3 * g + 3], zs[:, 3 * g:3 * g + 3], ACT.Silu).then_inc(z_silu, 1)

            def ssd():
                flat = lambda ap: ap.rearrange("p a b -> p (a b)")

                def item(m, dst, width=512):
                    act.wait_ge(d_item_mm, m + 1)
                    act.activation(dst, AB[m % 4][:, 0:width], ACT.Copy).then_inc(d_item, 1)

                gates(0)
                for m in range(6):
                    item(m, xs_tok[:, m // 3, 512 * (m % 3):512 * (m % 3) + 512])
                item(6, flat(b_tok[:, :, :]))
                for b in range(NB):
                    item(7 + b, flat(cb[:, b]))
                act.wait_ge(d_cum, 1)
                act.activation(S("tail", 0, 24), S("tail", 0, 24), ACT.Exp).then_inc(d_tail, 1)
                stream("z0", copy_z, some=(3,))
                for g in range(SSD_G):
                    item(9 + g, h_in[:, 384 * g:384 * g + 384], 384)
                for n in range(12):
                    act.wait_ge(d_diff, n + 1)
                    if n >= 6:
                        act.wait_ge(d_y_mm, n - 1)
                        act.activation(flat(cexp[:, n % 2]), AB[n % 2][:, :], ACT.Exp)
                    act.activation(flat(lmat[:, n % 2]), flat(lmat[:, n % 2]), ACT.Exp).then_inc(d_decay, 1)
                    if n < 8:
                        stream("z0", copy_z, some=(4 + n,))
                silu_z(0)
                for g in range(SSD_G):
                    act.wait_ge(d_gated, g + 1)
                    if g >= 2:
                        act.wait_ge(d_sum, g - 1)
                    act.activation(y_sq[:, g % 2], y_ssd[:, 3 * g:3 * g + 3], ACT.Square).then_inc(d_sq, 1)
                act.wait_ge(d_sum, SSD_G)
                act.activation(S("group_rms", 0, 8), AB[0][:, 0:8], ACT.Sqrt, bias=EPS, scale=1.0 / 384).then_inc(d_root, 1)
                act.wait_ge(ada_added, 40)
                for g in range(SSD_G):
                    act.wait_ge(d_mix, g + 1)
                    act.activation(a_hi[:, 3 * g:3 * g + 3], y_mix[:, 3 * g:3 * g + 3], ACT.Copy).then_inc(d_rounded, 1)

            def gdn():
                flat = lambda ap: ap.rearrange("p a b -> p (a b)")

                def square(n):
                    if n >= 3:
                        act.wait_ge(n_sum, n - 2)
                    act.activation(g_sq[:, n % 3], conv1[:, 2 * n:2 * n + 2], ACT.Square).then_inc(n_sq, 1)

                act.wait_ge(conv_done, XBC_T + GQ_T)
                square(0)
                square(1)
                for n in range(12):
                    stream("z1", copy_z, some=(n,))
                    if n < 10:
                        square(n + 2)
                    if n % 2:
                        m = n // 2
                        act.wait_ge(v_turned, m + 1)
                        b, h = 4 * m // GH, 4 * m % GH
                        act.activation(flat(v_tok[:, b, h:h + 4]), AB[m % 4][:, :], ACT.Copy).then_inc(v_copied, 1)
                act.wait_ge(n_sum, 12)
                act.activation(S("l2", 0, 48), PB[2][:, 0:48], ACT.Sqrt, bias=EPS).then_inc(n_root, 1)
                gates(1)
                act.wait_ge(g_cum, 1)
                act.activation(S("tail", 0, 24), S("tail", 0, 24), ACT.Exp).then_inc(g_tail, 1)
                for j in range(2):
                    act.activation(S(f"tot{j}", 0, 24), S(f"tot{j}", 0, 24), ACT.Exp).then_inc(g_tot, 1)
                for n in range(6):
                    act.wait_ge(g_diff, n + 1)
                    act.activation(flat(egc[:, 4 * n:4 * n + 4]), PB[n % 2][:, :], ACT.Exp)
                    d_ = flat(dec[:, 4 * n:4 * n + 4])
                    act.activation(d_, d_, ACT.Exp).then_inc(g_decay, 1)
                halves = (slice(0, GC), slice(GC, P))

                def transposed_bd(at, m):
                    act.wait_ge(i_inv, at)
                    for r in halves:
                        last = act.activation(inv_t_bd[r, 8 * m:8 * m + 8, r], inv_t[r, 8 * m:8 * m + 8], ACT.Copy)
                    last.then_inc(i_bd, 1)

                act.wait_ge(zeroed, 2)
                for m in range(3):
                    transposed_bd(m + 1, m)
                for lv in range(1, LEVELS):
                    for m in range(3):
                        s8 = slice(8 * m, 8 * m + 8)
                        act.wait_ge(i_y_mm, 3 * lv + m + 1)
                        if lv < LEVELS - 1:
                            act.activation(flat(step_y[:, s8]), BANKS[m][:, :], ACT.Copy).then_inc(i_y, 1)
                        if lv == 1 and m == 0:
                            act.wait_ge(zeroed, 3)
                        for r in halves:
                            last = act.activation(step_y_bd[r, s8, r], BANKS[m][r, :].rearrange("p (a d) -> p a d", a=8), ACT.Copy)
                        last.then_inc(i_y_bd, 1)
                    if lv < LEVELS - 2:
                        for m in range(3):
                            transposed_bd(3 * lv + m + 1, m)
                silu_z(1)
                for n, (c, g) in enumerate(SCAN):
                    act.wait_ge(c_o_mm, n + 1)
                    act.activation(conv1[:, 4 * g:4 * g + 4, c * GC:c * GC + GC],
                                   BANKS[4 + n % 2][:, 0:4 * GC].rearrange("p (a b) -> p a b", a=4), ACT.Copy).then_inc(c_o, 1)
                act.wait_ge(c_o, 12)
                for n in range(6):
                    if n >= 3:
                        act.wait_ge(o_sum, n - 2)
                    act.activation(o_sq[:, n % 3], conv1[:, 2 * n:2 * n + 2], ACT.Square).then_inc(o_sqd, 1)
                act.wait_ge(o_sum, 6)
                act.activation(S("o_rms", 0, 24), PB[0][:, 0:24], ACT.Sqrt, bias=EPS, scale=1.0 / GD).then_inc(o_root, 1)
                for n in range(6):
                    o_round(n)

            def o_round(n):
                act.wait_ge(o_mixed, n + 1)
                act.activation(a_hi[:, 2 * n:2 * n + 2], o_t[:, n % 3], ACT.Copy).then_inc(o_rounded, 1)

            def key0(k, i, j, ps):
                for kv in range(2):
                    for half in range(2):
                        last = act.activation(att_k[half * AD:half * AD + AD, kv], ps[kv * AD:kv * AD + AD], ACT.Copy)
                last.then_inc(copied, 1)

            def values(k, i, j, ps):
                act.activation(att_v[:, :, P * j:P * j + P], ps.rearrange("p (b c) -> p b c", b=NB), ACT.Copy).then_inc(copied, 1)

            def mixer(layer):
                stream(f"dt{layer}")
                conv(layer)
                for q in range(4):
                    if q == 0:
                        act.wait_ge(hankel_mm, layer + 1)
                        if layer == 0:
                            act.wait_ge(bias_vec_stored, 16)
                    last = act.activation(bias[:, 2 * q:2 * q + 2].rearrange("p a b -> p (a b)"), AB[q][:, :], ACT.Copy)
                last.then_inc(bias_ready, 1)
                stream(f"q{layer}", lambda k, i, j, ps: act.activation(att_q[:, j], ps, ACT.Copy, scale=AD ** -0.5).then_inc(copied, 1))
                stream(f"k{layer}", key0 if layer == 0 else copy_unit(ACT.Copy, lambda k: att_k[:, k]))
                if layer == 0:
                    stream("v0", values)
                attention(layer)
                (ssd, gdn)[layer]()
                stream(f"out{layer}")

            act.wait_ge(prm_ready, 1)
            act.wait_ge(c_zeroed, 1)
            act.activation(c_cols[:, :], prm[:, PRM["c"]:PRM["c"] + 8], ACT.Silu)
            act.activation(c_silu[:, :, C_COL], prm[:, PRM["c"]:PRM["c"] + 8], ACT.Silu).then_inc(c_ready, 1)
            pre_norm(0, 0, 0, None)
            mixer(0)
            post_norm(1, "out0")
            pre_norm(2, 0, 1, 0)
            up(0)
            stream("down0")
            post_norm(3, "down0")
            pre_norm(4, 1, 0, 1)
            mixer(1)
            post_norm(5, "out1")
            pre_norm(6, 1, 1, 2)
            up(1)
            stream("down1")
            post_norm(7, "down1")

        @block.vector
        def _(dve):
            chain = [0]

            def link(ins):
                chain[0] += 1
                ins.then_inc(dve_step, 1)
                dve.wait_ge(dve_step, chain[0])

            def fl(ap):
                return ap.rearrange("p a b -> p (a b)")

            def split_half(n, a, i=0):
                if n >= UNITS:
                    return
                hi, lo, src = w_half(n, a)
                dve.wait_ge(w_rounded, 8 * i + 2 * n + a + 1)
                dve.tensor_tensor(lo, src, hi.bitcast(F32), ALU.subtract).then_inc(w_split, 1)

            def ada_term(m, k, i=0):
                p = ada_pair(m)
                dst, w, c_ = ada_sum[:, p % 2], ada_slots(m, 2)[0][:, :, k], c_cols[:, k:k + 1]
                if k == 0:
                    for q in range(2):
                        dve.wait_ge(ada_landed[(m + q) % 8], 16 * (m // 8 + 1) + 8 * i)
                    if p >= 2:
                        dve.wait_ge(ada_added, ADA_SUMMED[2 * p - 3] + 1 + 4 * i)
                    dve.tensor_scalar(dst, w, c_, None, ALU.mult).then_inc(ada_terms, 1)
                else:
                    dve.wait_ge(ada_terms, 8 * p + k + 16 * i)
                    dve.scalar_tensor_tensor(dst, w, c_, dst, ALU.mult, ALU.add).then_inc(ada_terms, 1)

            def stream(name, work=None, after=None, some=None):
                n0, cnt = PARTS[name]

                def step(k, i, j):
                    n = n0 + j
                    halves = [lambda a=a: split_half(n + 2, a, i) for a in range(2)]
                    if name in ADA_WITH and not k_tail(name, k):
                        m, t = ADA_WITH[name] + j // 2 * 2, 4 * (j % 2)
                        ada_term(m, t, i)
                        halves.pop(0)()
                        ada_term(m, t + 1, i)
                        halves.pop(0)()
                        ada_term(m, t + 2, i)
                        ada_term(m, t + 3, i)
                    if work is not None:
                        work(k, i, j, banks[n][:, 0:SEQ], halves)
                    for half in halves:
                        half()
                    if after is not None and j:
                        after(k - 1, i, j - 1)

                if some is None:
                    units(dve, name, step)
                else:
                    for k in some:
                        step(k, 0, k)
                if after is not None:
                    after(cnt - 1, 0, cnt - 1)

            def taps(dst, w, ps, width, done, base, between):
                for s in range(1, width):
                    if s > 1 and between:
                        between.pop(0)()
                    if s > 1:
                        dve.wait_ge(done, base + s - 1)
                    dve.scalar_tensor_tensor(dst(slice(s, SEQ)), ps(slice(0, SEQ - s)), w(width - 1 - s), dst(slice(s, SEQ)),
                                             ALU.mult, ALU.add).then_inc(done, 1)

            def conv(layer):
                dst, base, cnt = convs[layer], layer * XBC_T, (XBC_T, GQ_T)[layer]

                def work(k, i, j, ps, halves):
                    dve.wait_ge(conv_first, base + k + 1)
                    taps(lambda t: dst[:, ds(k, 1), t], lambda tap: prm[:, ds(PRM[f"conv{layer}_w"] + tap * cnt + k, 1)],
                         lambda t: one(ps[:, t]), 4, conv_taps, 3 * (base + k), halves)

                stream(f"conv{layer}", work)

            def up(layer):
                base = 2 * FT * layer

                def work(k, i, j, ps, halves):
                    half, s = j % 2, j // 2 % 2
                    y = (yv if half else yg)[:, s]
                    col = half * FT + 2 * i + j // 2
                    dve.wait_ge(up_first, base + k + 1)
                    taps(lambda t: y[:, t], lambda tap: prm[:, ds(PRM["up_w"] + (3 * layer + tap) * 2 * FT + col, 1)],
                         lambda t: ps[:, t], 3, up_taps, 2 * (base + k), halves)
                    if half:
                        halves.pop(0)()
                        dve.wait_ge(gelu_done, FT * layer + 2 * i + j // 2 + 1)
                        dve.wait_ge(up_taps, 2 * (base + k) + 2)
                        dve.tensor_tensor(prod[:, s], yg[:, s], y, ALU.mult).then_inc(prod_done, 1)

                def after(k, i, j):
                    if j % 2:
                        pair = 2 * i + j // 2
                        dve.wait_ge(g_rounded, FT * layer + pair + 1)
                        dve.tensor_tensor(a_lo[:, ds(pair, 1), :], prod[:, j // 2 % 2:j // 2 % 2 + 1],
                                          a_hi[:, ds(pair, 1), :].bitcast(F32), ALU.subtract).then_inc(g_ready, 1)

                stream(f"up{layer}", work, after)

            def read_mods(a, b, bank):
                dve.wait_ge(ada_added, b)
                m = mods[:, :, :, :].rearrange("p l s k -> p (l s k)")
                dve.tensor_tensor(m[:, a:b], bank[:, a:b], prm[:, PRM["ada_b"] + a:PRM["ada_b"] + b], ALU.add).then_inc(mods_read, 1)

            def make_gain(layer, which, mods_at):
                dve.wait_ge(mods_read, mods_at)
                c = PRM["norm"] + (4 * layer + which) * 8
                w, g = prm[:, c:c + 8], gain[:, layer, which]
                section = {0: 1, 1: 2, 2: 4, 3: 5}[which]
                m = mods[:, layer, section]
                if which % 2 == 0:
                    link(dve.scalar_tensor_tensor(g, m, 1.0, w, ALU.add, ALU.mult))
                else:
                    link(dve.tensor_tensor(g, m, w, ALU.mult))

            def inverse_root(event):
                dve.wait_ge(roots, event + 1)
                dve.reciprocal(S("inv_rms", 0, 2), S("rms", 0, 2)).then_inc(inv_rms, 1)
                dve.wait_ge(spread, event + 1)

            def pre_norm(event, layer, which):
                inverse_root(event)
                norm = 2 * layer + which

                def rest(k):
                    dve.wait_ge(h_rounded, DT * norm + k + 1)
                    dve.scalar_tensor_tensor(h_lo[:, k], yr[:, k], mods[:, layer, 3 * which, k:k + 1], h_hi[:, k].bitcast(F32),
                                             ALU.add, ALU.subtract).then_inc(h_ready, 1)

                for k in range(DT):
                    dve.scalar_tensor_tensor(yr[:, k], x[:, k], gain[:, layer, 2 * which, k:k + 1], ROW_BANK[event][:, 0:SEQ],
                                             ALU.mult, ALU.mult).then_inc(scaled, 1)
                    if k >= 2:
                        rest(k - 2)
                rest(DT - 2)
                rest(DT - 1)

            def post_norm(event, layer, which):
                done = 8 * (2 * layer + which)
                for q in range(4):
                    dve.wait_ge(squares, DT * event + 2 * q + 2)
                    for k in (2 * q, 2 * q + 1):
                        last = dve.tensor_scalar(yr[:, k], acc(k), gain[:, layer, 2 * which + 1, k:k + 1], None, ALU.mult)
                last.then_inc(y_scaled, 4)
                inverse_root(event)
                rows_ = bc(one(ROW_BANK[event][:, 0:SEQ]), P, 2, SEQ)
                dve.wait_ge(y_scaled, done + 4)

                def add(q):
                    dve.wait_ge(y_scaled, done + 5 + q)
                    dve.tensor_tensor(x[:, 2 * q:2 * q + 2], x[:, 2 * q:2 * q + 2], yr[:, 2 * q:2 * q + 2], ALU.add).then_inc(x_ready, 2)

                for q in range(4):
                    dve.tensor_tensor(yr[:, 2 * q:2 * q + 2], yr[:, 2 * q:2 * q + 2], rows_, ALU.mult).then_inc(y_scaled, 1)
                    if q:
                        add(q - 1)
                add(3)

            def attention(layer):
                n8 = AH * layer
                dve.wait_ge(bias_ready, layer + 1)
                for h in range(AH):
                    dve.wait_ge(s_scored, n8 + h + 1)
                    dve.tensor_tensor_reduce(scores[:, h, 0:SEQ], AB[h % 3][:, 0:SEQ], bias[:, h], 1.0, -3e38, ALU.add, ALU.max,
                                             S("max", h, 1)).then_inc(s_biased, 1)
                    dve.tensor_tensor_reduce(scores[:, h, SEQ:384], AB[h % 3][:, SEQ:384], bias[:, h, P:SEQ], 1.0, -3e38, ALU.add, ALU.max,
                                             S("max", 8 + h, 1)).then_inc(s_biased, 1)
                dve.wait_ge(s_biased, 2 * (n8 + AH))
                sink = bc(rows[:, ROW["sinks"]:ROW["sinks"] + 8].rearrange("p (a b) -> p a b", a=1), P, 2, 8)
                two = lambda t: S(t, 0, 16).rearrange("p (a b) -> p a b", a=2)
                if layer == 0:
                    link(dve.tensor_tensor(two("max"), two("max"), sink, ALU.max))
                    dve.tensor_tensor(two("sink_exp"), sink, two("max"), ALU.subtract)
                dve.tensor_scalar(S("neg_max", 0, 16), S("max", 0, 16), -1.0, None, ALU.mult).then_inc(s_max, 1)
                if layer == 0:
                    stream("z0", some=(0, 1, 2))
                else:
                    stream("v1")
                dve.wait_ge(s_exp, 17 if layer == 0 else 17 + 16)
                if layer == 0:
                    link(dve.tensor_tensor(S("prob_sum", 0, 16), S("prob_sum", 0, 16), S("sink_exp", 0, 16), ALU.add))
                link(dve.reciprocal(S("inv_sum", 0, 16), S("prob_sum", 0, 16)))
                for h in range(AH):
                    dve.tensor_scalar(scores[:, h, 0:SEQ], scores[:, h, 0:SEQ], S("inv_sum", h, 1), None, ALU.mult)
                    dve.tensor_scalar(scores[:, h, SEQ:384], scores[:, h, SEQ:384], S("inv_sum", 8 + h, 1), None, ALU.mult).then_inc(s_norm, 1)
                for t in range(4):
                    dve.wait_ge(s_rounded, 4 * layer + t + 1)
                    dve.tensor_tensor(a_lo[:, 18 + t], O_BANK[t % 2][:, 0:SEQ], a_hi[:, 18 + t].bitcast(F32), ALU.subtract).then_inc(s_ready, 1)

            def gates(layer):
                n, heads = (48, SSD_H) if layer == 0 else (24, GH)
                link(dve.scalar_tensor_tensor(S("abs", 0, n), S("dtx", 0, n), -1.0, S("dtx", 0, n), ALU.mult, ALU.max))
                if layer == 0:
                    link(dve.memset(S("bx", 0, 24), 0.0))
                dve.tensor_scalar(S("relu", 0, n), S("dtx", 0, n), 0.0, None, ALU.max).then_inc(gate_abs, 1)
                dve.wait_ge(gate_exp, 4 * layer + 3)
                link(dve.tensor_scalar(S("u", 0, n), S("e", 0, n), 1.0, None, ALU.add))
                link(dve.tensor_scalar(S("um", 0, n), S("u", 0, n), -1.0, None, ALU.add))
                dve.tensor_scalar(S("be1", 0, 24), S("be", 0, 24), 1.0, None, ALU.add).then_inc(gate_ln, 1)
                link(dve.tensor_tensor(S("um", 0, n), S("e", 0, n), S("um", 0, n), ALU.subtract))
                link(dve.reciprocal(S("ur", 0, n), S("u", 0, n)))
                dve.wait_ge(gate_ln, layer + 1)
                link(dve.reciprocal(S("beta", 0, 24), S("be1", 0, 24)))
                link(dve.tensor_tensor(S("um", 0, n), S("um", 0, n), S("ur", 0, n), ALU.mult))
                link(dve.tensor_tensor(S("um", 0, n), S("um", 0, n), S("relu", 0, n), ALU.add))
                dve.wait_ge(gate_exp, 4 * layer + 4)
                link(dve.tensor_tensor(S("dt", 0, n), S("um", 0, n), S("ln", 0, n), ALU.add))
                two = lambda t: S(t, 0, n).rearrange("p (a b) -> p a b", a=2)
                a_ = bc(S("a", 0, heads).rearrange("p (a b) -> p a b", a=1), P, 2, heads)
                dve.scalar_tensor_tensor(two("da"), two("dt"), -1.0, a_, ALU.mult, ALU.mult).then_inc(gate_ready, 1)

            def ssd():
                gates(0)
                dve.wait_ge(in_landed[3], 16)
                for half in range(2):
                    r = slice(half * 64, half * 64 + 64)
                    link(dve.tensor_copy(S("d", 0, 12, half * 64, half * 64 + 64), rows[r, ROW["d"] + half:ROW["d"] + 24:2]))
                dve.wait_ge(d_cum_mm, 1)
                link(dve.tensor_copy(S("cum", 0, 48), PB[2][:, 0:48]))
                dve.tensor_tensor(S("tail", 0, 24), PB[2][:, 48:72], S("cum", 0, 24), ALU.subtract).then_inc(d_cum, 1)
                dve.wait_ge(d_tail, 1)
                link(dve.tensor_tensor(S("tail", 0, 24), S("tail", 0, 24), S("dt", 0, 24), ALU.mult))
                dve.wait_ge(d_item, 3)
                dve.tensor_tensor(xd[:, :].rearrange("p (h d) -> p h d", h=24), xs_tok[:, 0].rearrange("p (h d) -> p h d", h=24),
                                  bc(S("tail", 0, 24).rearrange("p (h d) -> p h d", d=1), P, 24, 64), ALU.mult).then_inc(d_xd, 1)
                dve.wait_ge(d_item, 9)
                stream("z0", some=(3,))

                def diff(n):
                    b, h0 = n // 6, 4 * (n % 6)
                    dve.wait_ge(d_decay_mm, n + 1)
                    for q in range(4):
                        last = dve.scalar_tensor_tensor(lmat[:, n % 2, q], AB[n % 2][:, q * P:q * P + P], S("cum", 24 * b + h0 + q, 1),
                                                        C("keep"), ALU.subtract, ALU.min)
                    last.then_inc(d_diff, 1)

                def weights(n):
                    b, h0 = n // 6, 4 * (n % 6)
                    dve.wait_ge(d_decay, n + 1)
                    if n >= 2:
                        dve.wait_ge(d_y_mm, n - 1)
                    for q in range(4):
                        h = h0 + q
                        if b:
                            dve.tensor_tensor(cexp[:, n % 2, q], cexp[:, n % 2, q], conv0[:, 16 + h // HPG, P:2 * P], ALU.mult)
                        last = dve.scalar_tensor_tensor(mmat[:, n % 2, q], lmat[:, n % 2, q], S("dt", 24 * b + h, 1), cb[:, b, h // HPG],
                                                        ALU.mult, ALU.mult)
                    last.then_inc(d_mmat, 1)

                def outputs(n):
                    b, t0 = n // 6, 2 * (n % 6)
                    dve.wait_ge(d_y_mm, n + 1)
                    for q in range(2):
                        c = slice(b * P, b * P + P)
                        last = dve.scalar_tensor_tensor(y_ssd[:, t0 + q, c], conv0[:, t0 + q, c], S("d", t0 + q, 1),
                                                        Y_BANK[n % 3][:, q * P:q * P + P], ALU.mult, ALU.add)
                    last.then_inc(d_y, 1)

                diff(0)
                for n in range(12):
                    if n < 8:
                        stream("z0", some=(4 + n,))
                    if n < 11:
                        diff(n + 1)
                    weights(n)
                    if n:
                        outputs(n - 1)
                outputs(11)
                dve.wait_ge(d_y, 12)
                for g in range(SSD_G):
                    t = slice(3 * g, 3 * g + 3)
                    dve.wait_ge(z_silu, g + 1)
                    dve.tensor_tensor(y_ssd[:, t], y_ssd[:, t], zs[:, t], ALU.mult).then_inc(d_gated, 1)
                dve.wait_ge(d_root, 1)
                dve.reciprocal(S("group_inv", 0, 8), S("group_rms", 0, 8)).then_inc(d_inv, 1)
                for g in range(SSD_G):
                    dve.wait_ge(d_spread, g // 2 + 1)
                    for k in range(3 * g, 3 * g + 3):
                        last = dve.scalar_tensor_tensor(y_mix[:, k], y_ssd[:, k], prm[:, PRM["ssd_norm"] + k:PRM["ssd_norm"] + k + 1],
                                                        PB[g // 2][:, (g % 2) * SEQ:(g % 2 + 1) * SEQ], ALU.mult, ALU.mult)
                    last.then_inc(d_mix, 1)
                    if g:
                        mix_rest(g - 1)
                mix_rest(3)
                mark_attention(0)

            def mix_rest(g):
                dve.wait_ge(d_rounded, g + 1)
                for k in range(3 * g, 3 * g + 3):
                    dve.tensor_tensor(a_lo[:, k], y_mix[:, k], a_hi[:, k].bitcast(F32), ALU.subtract).then_inc(mix_ready, 1)

            def mark_attention(layer):
                dve.wait_ge(mix_ready, MIX_T * layer + 12)
                dve.sem_inc(mix_ready, 4)

            def gdn():
                stack = lambda ap, n: bc(ap.rearrange("p (s d) -> p s d", d=1), ap.shape[0], ap.shape[1], n)
                for n in range(12):
                    stream("z1", some=(n,))
                dve.wait_ge(n_root, 1)
                link(dve.reciprocal(S("l2_inv", 0, 48), S("l2", 0, 48)))
                dve.tensor_scalar(S("l2_inv", 0, 24), S("l2_inv", 0, 24), GD ** -0.5, None, ALU.mult).then_inc(n_inv, 1)
                gates(1)
                for n in range(12):
                    dve.wait_ge(n_spread, n + 1)
                    t = conv1[:, 2 * n:2 * n + 2]
                    dve.tensor_tensor(t, t, AB[n % 4][:, :].rearrange("p (a t) -> p a t", a=2), ALU.mult).then_inc(n_unit, 1)
                    if n == 3:
                        dve.wait_ge(g_cum_mm, 1)
                        link(dve.tensor_copy(S("cum", 0, 24), PB[3][:, 0:24]))
                        for j in range(2):
                            dve.tensor_copy(S(f"tot{j}", 0, 24), PB[3][:, 48 + 24 * j:72 + 24 * j])
                        dve.tensor_tensor(S("tail", 0, 24), PB[3][:, 24:48], S("cum", 0, 24), ALU.subtract).then_inc(g_cum, 1)
                keep = bc(C("keep_chunk", 0, GC).rearrange("p (a d) -> p a d", a=1), P, 4, GC)
                for n in range(6):
                    dve.wait_ge(g_decay_mm, n + 1)
                    ps = PB[n % 2][:, :].rearrange("p (a d) -> p a d", a=4)
                    for j in range(2):
                        r = slice(j * GC, j * GC + GC)
                        last = dve.tensor_tensor(dec[r, 4 * n:4 * n + 4], ps[r, :, r], stack(S("cum", 4 * n, 4, r.start, r.stop), GC), ALU.subtract)
                    link(last)
                    dve.tensor_tensor(dec[:, 4 * n:4 * n + 4], dec[:, 4 * n:4 * n + 4], keep, ALU.min).then_inc(g_diff, 1)
                dve.wait_ge(g_tail, 1)
                for n in range(6):
                    dve.wait_ge(k_turned, n + 1)
                    b, h = 4 * n // GH, 4 * n % GH
                    dve.tensor_tensor(k_tok[:, b, h:h + 4], AB[n % 4][:, :].rearrange("p (a d) -> p a d", a=4),
                                      stack(S("tail", 4 * n, 4), GD), ALU.mult).then_inc(k_copied, 1)
                ident = bc(C("ident_chunk", 0, GC).rearrange("p (a d) -> p a d", a=1), P, 8, GC)
                three = lambda bank: bank[:, :].rearrange("p (a d) -> p a d", a=8)

                def off_blocks(lv, m):
                    s8 = slice(8 * m, 8 * m + 8)
                    for r in (slice(0, GC), slice(GC, P)):
                        mask = bc(C("level", lv * GC, GC, r.start, r.stop).rearrange("p (a d) -> p a d", a=1), GC, 8, GC)
                        last = dve.tensor_tensor(off_bd[r, s8, r], sys_t[r, s8], mask, ALU.mult)
                    last.then_inc(i_off, 1)

                for m in range(3):
                    s8 = slice(8 * m, 8 * m + 8)
                    dve.wait_ge(g_gram_mm, 2 * m + 1)
                    dve.wait_ge(g_decay, min(6, 2 * m + 2))
                    link(dve.tensor_tensor(sys_t[:, s8], three(AB[2 * m % 4]), dec[:, s8], ALU.mult))
                    link(dve.tensor_tensor(sys_t[:, s8], sys_t[:, s8], stack(S("beta", 8 * m, 8), GC), ALU.mult))
                    dve.sem_inc(g_gram, 1)
                    dve.wait_ge(g_gram_mm, 2 * m + 2)
                    dve.tensor_tensor(attn_t[:, s8], three(AB[(2 * m + 1) % 4]), dec[:, s8], ALU.mult).then_inc(g_gram, 1)
                    if m == 0:
                        dve.wait_ge(zeroed, 2)
                    off_blocks(0, m)
                    mask = bc(C("level", 0, GC).rearrange("p (a d) -> p a d", a=1), P, 8, GC)
                    link(dve.tensor_tensor(inv_t[:, s8], sys_t[:, s8], mask, ALU.mult))
                    dve.tensor_tensor(inv_t[:, s8], ident, inv_t[:, s8], ALU.subtract)
                dve.wait_ge(g_gram_mm, 6)
                for b in range(NB):
                    t = conv1[:, 12:12 + GH, b * P:b * P + P]
                    dve.tensor_tensor(t, t, egc[:, b * GH:b * GH + GH], ALU.mult).then_inc(g_scaled, 1)
                for lv in range(LEVELS):
                    if lv == 0:
                        for m in range(3):
                            s8 = slice(8 * m, 8 * m + 8)
                            dve.wait_ge(i_y_mm, m + 1)
                            dve.tensor_tensor(inv[:, s8], ident, three(BANKS[m]), ALU.subtract).then_inc(i_inv, 1)
                    if lv < LEVELS - 1:
                        for m in range(3):
                            dve.wait_ge(i_y_mm, 3 * lv + m + 1)
                            off_blocks(lv + 1, m)
                    if lv:
                        for m in range(3):
                            s8 = slice(8 * m, 8 * m + 8)
                            dve.wait_ge(i_inv, 3 * (lv - 1) + m + 1)
                            if lv < LEVELS - 1:
                                dve.wait_ge(i_z_mm, 3 * (lv - 1) + m + 1)
                                dve.tensor_tensor(inv[:, s8], inv[:, s8], three(BANKS[3 + m]), ALU.subtract)
                            dve.wait_ge(i_zt_mm, 3 * (lv - 1) + m + 1)
                            dve.tensor_tensor(inv_t[:, s8], inv_t[:, s8], three(BANKS[m]), ALU.subtract).then_inc(i_inv, 1)

                def residual(n):
                    c, g = SCAN[n]
                    if c:
                        b, r = c // 2, slice((c % 2) * GC, (c % 2) * GC + GC)
                        dve.wait_ge(c_ks_mm, n - 2)
                        dve.tensor_tensor(resid[r, n % 2], v_tok[r, b, 4 * g:4 * g + 4],
                                          BANKS[n % 2][r, :].rearrange("p (a d) -> p a d", a=4), ALU.subtract).then_inc(c_resid, 1)

                def values(n):
                    c, g = SCAN[n]
                    b, r = c // 2, slice((c % 2) * GC, (c % 2) * GC + GC)
                    dve.wait_ge(c_tr_mm, n + 1)
                    dve.tensor_tensor(v_new[r, g], BANKS[2 + n % 2][r, :].rearrange("p (a d) -> p a d", a=4),
                                      stack(S("beta", b * GH + 4 * g, 4, r.start, r.stop), GD), ALU.mult).then_inc(c_vnew, 1)

                def states(n):
                    c, g = SCAN[n]
                    if c == 3:
                        return
                    b, j = c // 2, c % 2
                    dve.wait_ge(c_u_mm, n + 1)
                    if c == 0:
                        dve.tensor_copy(state[:, 4 * g:4 * g + 4], BANKS[6 + n % 2][:, :].rearrange("p (a d) -> p a d", a=4)).then_inc(c_state, 1)
                        return
                    for q in range(4):
                        h = 4 * g + q
                        last = dve.scalar_tensor_tensor(state[:, h], state[:, h], S(f"tot{j}", b * GH + h, 1),
                                                        BANKS[6 + n % 2][:, q * GD:q * GD + GD], ALU.mult, ALU.add)
                    last.then_inc(c_state, 1)

                dve.wait_ge(g_tot, 2)
                dve.wait_ge(i_inv, 3 * LEVELS)
                for n in range(len(SCAN) + 2):
                    if n < len(SCAN):
                        residual(n)
                    if 0 <= n - 1 < len(SCAN):
                        values(n - 1)
                    if n >= 2:
                        states(n - 2)

                def o_rest(n):
                    dve.wait_ge(o_rounded, n + 1)
                    for q in range(2):
                        dve.tensor_tensor(a_lo[:, 2 * n + q], o_t[:, n % 3, q], a_hi[:, 2 * n + q].bitcast(F32), ALU.subtract).then_inc(mix_ready, 1)

                dve.wait_ge(o_root, 1)
                dve.reciprocal(S("o_inv", 0, 24), S("o_rms", 0, 24)).then_inc(o_inv, 1)
                dve.wait_ge(z_silu, 8)
                for n in range(6):
                    dve.wait_ge(o_spread, n + 1)
                    if n >= 3:
                        dve.wait_ge(mix_ready, MIX_T + 2 * (n - 2))
                    link(dve.scalar_tensor_tensor(o_t[:, n % 3], conv1[:, 2 * n:2 * n + 2], prm[:, PRM["gdn_norm"]:PRM["gdn_norm"] + 1],
                                                  PB[1 + n % 3][:, :].rearrange("p (a t) -> p a t", a=2), ALU.mult, ALU.mult))
                    dve.tensor_tensor(o_t[:, n % 3], o_t[:, n % 3], zs[:, 2 * n:2 * n + 2], ALU.mult).then_inc(o_mixed, 1)
                    if n:
                        o_rest(n - 1)
                o_rest(5)
                mark_attention(1)

            def read_dt(layer):
                def work(k, i, j, ps, halves):
                    heads = (SSD_H, GH)[layer]
                    n = PARTS[f"dt{layer}"][0]
                    dve.wait_ge(w_used, 2 * n + 2)
                    dve.wait_ge(in_landed[3], 16)
                    v = ps.rearrange("p (b c) -> p b c", b=NB)
                    two = lambda t: S(t, 0, 2 * heads).rearrange("p (a b) -> p a b", a=2)
                    r0 = ROW[f"dt_bias{layer}"]
                    b_ = bc(rows[:, r0:r0 + heads].rearrange("p (a b) -> p a b", a=1), P, 2, heads)
                    if layer:
                        link(dve.tensor_copy(two("bx"), v[:, :, 0:heads]))
                    dve.tensor_tensor(two("dtx"), v[:, :, layer * heads:(layer + 1) * heads], b_, ALU.add).then_inc(dt_read, 1)

                stream(f"dt{layer}", work)
                dve.wait_ge(dt_read, layer + 1)

            def mixer(layer):
                read_dt(layer)
                conv(layer)
                stream(f"q{layer}")
                stream(f"k{layer}")
                if layer == 0:
                    for k in range(8):
                        ada_term(20, k)
                    stream("v0")
                    attention(0)
                    ssd()
                    read_mods(16, 40, PB[3])
                    make_gain(0, 1, 2)
                    make_gain(0, 2, 2)
                else:
                    attention(1)
                    read_mods(72, 80, PB[3])
                    gdn()
                stream(f"out{layer}")

            dve.memset(rel[32:33, :], 1.0).then_inc(rel_ones, 1)
            dve.wait_ge(prm_turned, 1)
            dve.tensor_copy(prm[:, 0:512], PB[0][:, :])
            dve.tensor_copy(prm[:, 512:PRM_G * P], PB[1][:, 0:PRM_G * P - 512]).then_inc(prm_ready, 1)
            dve.wait_ge(vec_mm, 1)
            for v in range(2):
                last = dve.tensor_copy(bias_vec[0:AH, v], AB[v][0:AH, 0:384])
            last.then_inc(vec_copied, 1)
            for n in range(2):
                split_half(n, 0)
                split_half(n, 1)
            dve.wait_ge(prm_ready, 1)
            dve.wait_ge(c_ready, 1)
            read_mods(0, 16, AB[3])
            make_gain(0, 0, 1)
            pre_norm(0, 0, 0)
            mixer(0)
            read_mods(40, 52, PB[2])
            make_gain(0, 3, 3)
            post_norm(1, 0, 0)
            pre_norm(2, 0, 1)
            up(0)
            stream("down0")
            read_mods(52, 72, PB[0])
            make_gain(1, 0, 4)
            make_gain(1, 1, 4)
            post_norm(3, 0, 1)
            pre_norm(4, 1, 0)
            mixer(1)
            read_mods(80, 92, PB[1])
            make_gain(1, 2, 6)
            post_norm(5, 1, 0)
            pre_norm(6, 1, 1)
            up(1)
            stream("down1")
            read_mods(92, 96, PB[2])
            make_gain(1, 3, 7)
            post_norm(7, 1, 1)

        @block.gpsimd
        def _(pool):
            pool.memset(c_silu[:, :, :], 0.0).then_inc(c_zeroed, 1)
            pool.wait_ge(s_ready, 8)
            pool.memset(inv_t_bd[:, :, :], 0.0).then_inc(zeroed, 1)
            pool.memset(off_bd[:, :, :], 0.0).then_inc(zeroed, 1)
            pool.wait_ge(g_gram_mm, 6)
            pool.wait_ge(g_decay, 6)
            for b in range(NB):
                t = conv1[:, 0:GH, b * P:b * P + P]
                pool.tensor_tensor(t, t, egc[:, b * GH:b * GH + GH], ALU.mult).then_inc(g_scaled, 1)
            pool.wait_ge(g_scaled, 4)
            pool.memset(step_y_bd[:, :, :], 0.0).then_inc(zeroed, 1)


def unit_columns(w, first, count, width=P):
    v = w[:, first:first + count * width].reshape(8, P, count, width)
    return v.transpose(1, 2, 0, 3).reshape(P, count, 8 * P)


def unit_rows(w):
    return w.reshape(-1, P, D_MODEL).transpose(1, 0, 2)


def kernel(**inputs):
    import concourse.bacc as bacc
    from concourse.bass_utils import run_bass_kernel_spmd

    v = {k: np.asarray(a) for k, a in inputs.items()}
    zeros = np.zeros((D_MODEL, P - 24), np.float32)

    def mixer_units(w, n_z, n_conv, n_att, gates_at, z_at, conv_at, att_at):
        gates = np.concatenate([w[:, gates_at:gates_at + 24], zeros], axis=1)
        return [unit_columns(gates, 0, 1), unit_columns(w, conv_at, n_conv), unit_columns(w, att_at, n_att),
                unit_columns(w, z_at, n_z)]

    def ffn_units(layer):
        w = v["ffn_w_up"][layer]
        both = np.stack([unit_columns(w, 0, FT), unit_columns(w, FT * P, FT)], axis=2)
        return [both.reshape(P, 2 * FT, 8 * P), unit_rows(v["ffn_w_down"][layer])]

    ab, cd = v["ab_w_in"][0], v["cd_w_in"][0]
    w_stream = np.ascontiguousarray(np.concatenate(
        mixer_units(ab, ZT, XBC_T, 6, 4096, 0, 1536, 4120) + [unit_rows(v["ab_w_out"][0])] + ffn_units(0)
        + mixer_units(cd, ZT, GQ_T, 12, 6144, 4608, 0, 6168) + [unit_rows(v["cd_w_out"][0])] + ffn_units(1), axis=1))
    ada_stream = np.ascontiguousarray(np.concatenate([unit_columns(v["ada_w"][layer], 0, 48) for layer in range(2)], axis=1))
    prm = np.concatenate([v[k].reshape(-1, P) for k in ("c", "ada_b", "norm_w", "ssd_conv_w", "ssd_conv_b", "ssd_norm_w",
                                                        "gdn_conv_w", "gdn_norm_w", "ffn_conv_w", "ffn_conv_b")])
    prm = np.concatenate([prm, np.zeros((PRM_G * P - PRM_COLS, P), np.float32)]).reshape(PRM_G, P, P).transpose(1, 0, 2)
    rows = np.concatenate([v[k].reshape(1, -1) for k in ("ssd_dt_bias", "ssd_a_log", "ssd_d", "swa_sinks", "gdn_dt_bias",
                                                         "gdn_a_log")], axis=1)
    arrays = {
        "w_stream": w_stream, "ada_stream": ada_stream,
        "x_tiles": np.ascontiguousarray(v["x"][0].T.reshape(DT, P, SEQ).transpose(1, 0, 2)),
        "prm": np.ascontiguousarray(prm), "rows": np.ascontiguousarray(rows),
        "constants": constants(), "buckets": bucket_rows(), "rel_bias": np.ascontiguousarray(v["rel_bias"]),
    }
    nc = bacc.Bacc("TRN2", target_bir_lowering=False, num_devices=1)
    aps = [nc.dram_tensor(f"in_{k}", a.shape, mybir.dt.from_np(a.dtype), kind="ExternalInput").ap() for k, a in arrays.items()]
    scratch = nc.dram_tensor("bias_scratch", (AH, 2, 384), F32).ap()
    out = nc.dram_tensor("out_tiles", (P, DT, SEQ), F32, kind="ExternalOutput").ap()
    build(nc, *aps, scratch, out)
    r = run_bass_kernel_spmd(nc, [{f"in_{k}": a for k, a in arrays.items()}], core_ids=[0])
    got = r.results[0]["out_tiles"]
    return np.ascontiguousarray(got.transpose(1, 0, 2).reshape(D_MODEL, SEQ).T).reshape(1, SEQ, D_MODEL)
```

```python
from contextlib import ExitStack

import numpy as np

import concourse.bass as bass
from concourse import mybir

F32 = mybir.dt.float32
F32R = mybir.dt.float32r
ACT = mybir.ActivationFunctionType
ALU = mybir.AluOpType
AX = mybir.AxisListType
ds = bass.ds

P = 128
D_MODEL, SEQ = 1024, 256
DT = D_MODEL // P
NB = SEQ // P
AH, AD = 8, 64
SSD_H, SSD_P, SSD_G = 24, 64, 4
HPG = SSD_H // SSD_G
GH, GD, GC = 12, 128, 64
FT = 2816 // P
NEG = -1e30
EPS_COL = 1e-6

XBC_T, ZT, GQ_T, MIX_T = 20, 12, 36, 16


def layout():
    parts, n = {}, 0
    for name, count in (("dt0", 1), ("conv0", XBC_T), ("q0", 4), ("k0", 1), ("v0", 1), ("z0", ZT), ("out0", MIX_T),
                        ("up0", 2 * FT), ("down0", FT), ("dt1", 1), ("conv1", GQ_T), ("q1", 4), ("k1", 4), ("v1", 4),
                        ("z1", ZT), ("out1", MIX_T), ("up1", 2 * FT), ("down1", FT)):
        parts[name] = (n, count)
        n += count
    return parts, n


PARTS, UNITS = layout()
ADA_UNITS = 2 * 6 * DT
ADA_WITH = {"q0": 16, "out0": 40, "down0": 52, "q1": 72, "k1": 76, "out1": 80, "down1": 92}
ADA_SUMMED = [2, 3, 6, 7, 10, 11, 14, 15] + list(range(16, 22)) + list(range(40, ADA_UNITS))
ADA_RINGS = {range(0, 16): 8,
             range(16, 28): 4,
             range(28, 40): 4,
             range(40, 72): 8,
             range(72, 80): 4,
             range(80, 92): 6,
             range(92, 96): 8}
C_COL = 39

PRM, PRM_COLS = {}, 0
for _name, _rows in (("c", 8), ("ada_b", 96), ("norm", 64), ("conv0_w", 80), ("conv0_b", 20), ("ssd_norm", 12),
                     ("conv1_w", 144), ("gdn_norm", 1), ("up_w", 264), ("up_b", 88)):
    PRM[_name] = PRM_COLS
    PRM_COLS += _rows
PRM_G = -(-PRM_COLS // P)

ROW = {"dt_bias0": 0, "a_log0": 24, "d": 48, "sinks": 72, "dt_bias1": 80, "a_log1": 92}
ROW_COLS = 104

LEVELS = 6
CST, CST_COLS = {}, 0
for _name, _n in (("ident", 128), ("ones", 128), ("triu", 128), ("triu_chunk", 128), ("same_chunk", 128),
                  ("reverse", 128), ("keep", 128), ("keep_chunk", 64), ("level", LEVELS * 64),
                  ("ident_chunk", 64), ("pick", 255), ("eps", 1)):
    CST[_name] = CST_COLS
    CST_COLS += _n


def constants():
    c = np.zeros((P, CST_COLS), np.float32)
    p, f = np.arange(P)[:, None], np.arange(P)[None, :]
    put = lambda name, v: c.__setitem__((slice(None), slice(CST[name], CST[name] + v.shape[1])), v)
    put("ident", np.eye(P))
    put("ones", np.ones((P, P)))
    put("triu", p <= f)
    put("triu_chunk", (p <= f) & (p // GC == f // GC))
    put("same_chunk", p // GC == f // GC)
    put("reverse", p + f == P - 1)
    put("keep", np.where(f >= p, -NEG, NEG))
    s, t = p % GC, np.arange(GC)[None, :]
    put("keep_chunk", np.where(t >= s, -NEG, NEG))
    for lv in range(LEVELS):
        b = 1 << lv
        m = (s // (2 * b) == t // (2 * b)) & (s // b % 2 == 0) & (t // b % 2 == 1)
        c[:, CST["level"] + lv * GC:CST["level"] + (lv + 1) * GC] = m
    put("ident_chunk", s == t)
    put("pick", np.broadcast_to(np.arange(255) == 127, (P, 255)))
    put("eps", np.full((P, 1), EPS_COL))
    return c


def bucket_rows():
    starts = [0, 1, 2, 3, 4, 5, 6, 7, 8, 9, 10, 11, 12, 13, 14, 15, 16, 21, 27, 35, 46, 59, 77, 99, 128, 166, 216]
    r = np.zeros((33, 2, 384), np.float32)
    for v in range(2):
        for i in range(384):
            dist = 255 - i
            if dist < 0 or (v == 0 and dist >= 128):
                r[32, v, i] = NEG
            else:
                r[sum(dist >= s for s in starts) - 1, v, i] = 1
    return r


def build(nc, w_dram, ada_dram, x_dram, prm_dram, row_dram, cst_dram, bucket_dram, rel_dram, scratch, out_dram):
    with ExitStack() as ctx:
        sem = lambda name: ctx.enter_context(nc.semaphore(name))
        cursor = [-(-nc.sbuf_base // 32) * 32]

        def sb(name, shape, dt=F32, at=None):
            size = int(np.prod(shape[1:])) * 4
            off = cursor[0] if at is None else at
            t = nc.alloc_sbuf_tensor_at(name, [P] + list(shape[1:]), dt, offset=off)
            if at is None:
                cursor[0] += -(-size // 32) * 32
            return t

        def region(size):
            at = -(-cursor[0] // 32) * 32
            cursor[0] = at + size
            return at

        KB = 1024
        x = sb("x", [P, DT, SEQ])
        h_hi = sb("h_hi", [P, DT, SEQ], F32R)
        h_lo = sb("h_lo", [P, DT, SEQ], F32R)
        raw = sb("raw", [P, 4, 8, P])
        w_hi = sb("w_hi", [P, 4, 4, P], F32R)
        w_lo = sb("w_lo", [P, 4, 4, P], F32R)
        cst = sb("cst", [P, CST_COLS])
        prm = sb("prm", [P, PRM_G * P])
        rows = sb("rows", [P, ROW_COLS])
        mods = sb("mods", [P, 2, 6, DT])
        gain = sb("gain", [P, 2, 4, DT])
        c_cols = sb("c_cols", [P, DT])
        small = sb("small", [P, 36, 48])
        at_hi, at_lo = region(22 * KB), region(22 * KB)
        a_hi = sb("a_hi", [P, 22, SEQ], F32R, at=at_hi)
        a_lo = sb("a_lo", [P, 22, SEQ], F32R, at=at_lo)
        arena = region(78 * KB)
        extra = region(12 * KB)
        c_silu = sb("c_silu", [P, DT, P + C_COL], at=extra)
        ada_first = sb("ada_first", [P, 4, 8, P], at=arena + 62 * KB)
        ada_ssd = sb("ada_ssd", [P, 4, 8, P], at=at_hi)
        ada_long = sb("ada_long", [P, 8, 8, P], at=arena + 30 * KB)
        ada_out1 = sb("ada_out1", [P, 6, 8, P], at=arena + 12 * KB)
        ada_sum = sb("ada_sum", [P, 2, 2, P], at=extra + 10 * KB)
        assert cursor[0] <= nc.sbuf_usable_end, (cursor[0], nc.sbuf_usable_end)
        conv0 = sb("conv0", [P, XBC_T, SEQ], at=arena)
        conv1 = sb("conv1", [P, GQ_T, SEQ], at=arena)
        convs = (conv0, conv1)
        zs = sb("zs", [P, ZT, SEQ], at=arena + 36 * KB)
        sq = sb("sq", [P, DT, SEQ], at=arena)
        yr = sb("yr", [P, DT, SEQ], at=arena + 8 * KB)
        yg = sb("yg", [P, 2, SEQ], at=arena + 24 * KB)
        yv = sb("yv", [P, 2, SEQ], at=arena + 26 * KB)
        prod = sb("prod", [P, 2, SEQ], at=arena + 28 * KB)
        prm_rows = sb("prm_rows", [P, PRM_G, P], at=arena + 20 * KB)
        bucket = sb("bucket", [P, 2, 384], at=arena + 24 * KB)
        rel = sb("rel", [P, 8], at=arena + 20 * KB + PRM_G * 512)
        bias_vec = sb("bias_vec", [P, 2, 384], at=arena + 27 * KB)
        scores = sb("scores", [P, AH, 384], at=at_hi)
        probs_t = sb("probs_t", [P, 2, 384], at=at_hi + 12 * KB)
        att_q = sb("att_q", [P, 4, SEQ], at=at_lo)
        att_k = sb("att_k", [P, 4, SEQ], at=at_lo + 4 * KB)
        att_v = sb("att_v", [P, NB, 512], at=at_lo + 8 * KB)
        bias = sb("bias", [P, AH, SEQ], at=arena + 48 * KB)
        hankels = (sb("hankel0", [P, AH, SEQ], at=arena + 20 * KB), sb("hankel1", [P, AH, SEQ], at=at_hi))
        xs_tok = sb("xs_tok", [P, NB, 1536], at=arena + 20 * KB)
        b_tok = sb("b_tok", [P, SSD_G, P], at=arena + 32 * KB)
        cb = sb("cb", [P, NB, SSD_G, P], at=arena + 48 * KB)
        h_in = sb("h_in", [P, 1536], at=arena + 52 * KB)
        xd = sb("xd", [P, 1536], at=arena + 58 * KB)
        lmat = sb("lmat", [P, 2, 4, P], at=arena + 64 * KB)
        mmat = sb("mmat", [P, 2, 4, P], at=arena + 68 * KB)
        cexp = sb("cexp", [P, 2, 4, P], at=arena + 72 * KB)
        y_ssd = sb("y_ssd", [P, ZT, SEQ], at=at_lo)
        y_sq = sb("y_sq", [P, 2, 3, SEQ], at=arena + 64 * KB)
        y_mix = sb("y_mix", [P, ZT, SEQ], at=arena)
        NS = NB * GH
        v_tok = sb("v_tok", [P, NB, GH, GD], at=arena + 48 * KB)
        k_tok = sb("k_tok", [P, NB, GH, GD], at=arena + 24 * KB)
        attn_t = sb("attn_t", [P, NS, GC], at=arena + 60 * KB)
        state = sb("state", [P, GH, GD], at=arena + 72 * KB)
        dec = sb("dec", [P, NS, GC], at=at_hi)
        sys_t = sb("sys_t", [P, NS, GC], at=at_hi + 6 * KB)
        inv = sb("inv", [P, NS, GC], at=at_hi + 12 * KB)
        step_y = sb("step_y", [P, NS, GC], at=at_hi)
        inv_t = sb("inv_t", [P, NS, GC], at=at_lo + 12 * KB)
        inv_t_bd = sb("inv_t_bd", [P, NS, P], at=at_lo)
        off_bd = sb("off_bd", [P, NS, P], at=arena + 66 * KB)
        egc = sb("egc", [P, NS, P], at=extra)
        step_y_bd = sb("step_y_bd", [P, NS, P], at=extra)
        g_sq = sb("g_sq", [P, 3, 2, SEQ], at=extra)
        resid = sb("resid", [P, 2, 2, 4, GD], at=at_hi)
        v_new = sb("v_new", [P, 2, 3, 4, GD], at=at_lo)
        o_tok = sb("o_tok", [P, NB, GH, GD], at=arena + 48 * KB)
        o_sq = sb("o_sq", [P, NB, GH, GD], at=extra)
        o_t = sb("o_t", [P, 3, 4, P], at=arena)

        PB = [ctx.enter_context(nc.psum_tensor(f"proj{i}", [P, 512], F32)) for i in range(4)]
        AB = [ctx.enter_context(nc.psum_tensor(f"acc{i}", [P, 512], F32)) for i in range(4)]
        BANKS = PB + AB
        ada_ps = AB[3]

        def C(name, a=0, n=None, p0=0, p1=P):
            n = n or 128
            return cst[p0:p1, CST[name] + a:CST[name] + a + n]

        EPS = cst[:, CST["eps"]:CST["eps"] + 1]
        acc = lambda k: AB[k // 2][:, (k % 2) * SEQ:(k % 2 + 1) * SEQ]
        tile_at = lambda k: k if k < 12 else k + 6

        in_landed = [sem(f"in_landed{i}") for i in range(5)]
        bias_vec_stored, hankel_landed, out_stored = sem("bias_vec_stored"), sem("hankel_landed"), sem("out_stored")
        w_landed = [sem(f"w_landed{i}") for i in range(4)]
        ada_landed = [sem(f"ada_landed{i}") for i in range(8)]
        w_rounded, w_split, w_used = sem("w_rounded"), sem("w_split"), sem("w_used")
        ada_terms, ada_added, mods_read = sem("ada_terms"), sem("ada_added"), sem("mods_read")
        act_step, dve_step = sem("act_step"), sem("dve_step")
        rel_ones, prm_turned, prm_ready, c_ready = (sem(n) for n in ("rel_ones", "prm_turned", "prm_ready", "c_ready"))
        vec_mm, vec_copied, hankel_mm, bias_ready = (sem(n) for n in ("vec_mm", "vec_copied", "hankel_mm", "bias_ready"))
        squares, sums, roots, scaled, h_rounded, h_ready, x_ready = (
            sem(n) for n in ("squares", "sums", "roots", "scaled", "h_rounded", "h_ready", "x_ready"))
        inv_rms, spread, y_scaled = sem("inv_rms"), sem("spread"), sem("y_scaled")
        z_silu, zeroed, c_zeroed = sem("z_silu"), sem("zeroed"), sem("c_zeroed")
        dt_read, conv_first, conv_taps, conv_done = (sem(n) for n in ("dt_read", "conv_first", "conv_taps", "conv_done"))
        copied = sem("copied")
        up_first, up_taps, gelu_done, prod_done, g_rounded, g_ready = (
            sem(n) for n in ("up_first", "up_taps", "gelu_done", "prod_done", "g_rounded", "g_ready"))
        s_scored, s_biased, s_max, s_exp, s_norm = (sem(n) for n in ("s_scored", "s_biased", "s_max", "s_exp", "s_norm"))
        s_turned, s_copied, s_out, s_rounded, s_ready = (
            sem(n) for n in ("s_turned", "s_copied", "s_out", "s_rounded", "s_ready"))
        gate_abs, gate_exp, gate_ln, gate_ready = (sem(n) for n in ("gate_abs", "gate_exp", "gate_ln", "gate_ready"))
        d_item_mm, d_item, d_cum_mm, d_cum, d_tail, d_xd = (
            sem(n) for n in ("ssd_item_mm", "ssd_item", "ssd_cum_mm", "ssd_cum", "ssd_tail", "ssd_xd"))
        d_decay_mm, d_diff, d_decay, d_mmat, d_y_mm, d_y = (
            sem(n) for n in ("ssd_decay_mm", "ssd_diff", "ssd_decay", "ssd_mmat", "ssd_y_mm", "ssd_y"))
        d_gated, d_sq, d_sum, d_root, d_inv, d_spread, d_mix, d_rounded, mix_ready = (
            sem(n) for n in ("ssd_gated", "ssd_sq", "ssd_sum", "ssd_root", "ssd_inv", "ssd_spread", "ssd_mix", "ssd_rounded", "mix_ready"))
        n_sq, n_sum, n_root, n_inv, n_spread, n_unit = (
            sem(n) for n in ("l2_sq", "l2_sum", "l2_root", "l2_inv", "l2_spread", "l2_unit"))
        v_turned, v_copied, k_turned, k_copied = (sem(n) for n in ("v_turned", "v_copied", "k_turned", "k_copied"))
        g_cum_mm, g_cum, g_tail, g_tot = (sem(n) for n in ("gdn_cum_mm", "gdn_cum", "gdn_tail", "gdn_total"))
        g_decay_mm, g_diff, g_decay, g_gram_mm, g_gram = (
            sem(n) for n in ("gdn_decay_mm", "gdn_diff", "gdn_decay", "gdn_gram_mm", "gdn_gram"))
        i_off, i_y_mm, i_y, i_y_bd, i_z_mm, i_zt_mm, i_inv, i_bd = (
            sem(n) for n in ("inv_off", "inv_y_mm", "inv_y", "inv_y_bd", "inv_z_mm", "inv_zt_mm", "inv_done", "inv_bd"))
        g_scaled = sem("gdn_scaled")
        c_ks_mm, c_resid, c_tr_mm, c_vnew, c_o_mm, c_o, c_u_mm, c_state = (
            sem(n) for n in ("scan_ks_mm", "scan_resid", "scan_tr_mm", "scan_vnew", "scan_o_mm", "scan_o", "scan_u_mm", "scan_state"))
        o_sqd, o_root, o_scaled, o_turned, o_mixed, o_rounded = (
            sem(n) for n in ("o_sqd", "o_root", "o_scaled", "o_turned", "o_mixed", "o_rounded"))
        o_split = sem("o_split")

        freed = {}
        totals = {}
        for name, (n0, cnt) in PARTS.items():
            key = {"dt": (dt_read, 1), "conv": (conv_taps, 3), "up": (up_taps, 2)}.get(name[:-1], (copied, 1))
            if name[:-1] in ("out", "down"):
                continue
            for n in range(n0, n0 + cnt):
                at = totals.get(name[:-1] if key[1] > 1 else str(key[0]), 0) + key[1]
                totals[name[:-1] if key[1] > 1 else str(key[0])] = at
                freed[n] = (key[0], at, key[1])

        def bank_id(n):
            name = next(q for q, (n0, cnt) in PARTS.items() if n0 <= n < n0 + cnt)
            if name == "z1":
                return 6
            return n % 4 if name[:-1] in ("dt", "conv", "up") else n % 2

        banks = {n: BANKS[bank_id(n)] for n in freed}
        before = {n: max((m for m in freed if m < n and bank_id(m) == bank_id(n)), default=None) for n in freed}

        def units(e, name, step):
            cnt = PARTS[name][1]
            for k in range(min(4, cnt)):
                step(k, 0, k)
            span = 8 if name[:-1] == "down" else 4
            groups = 0 if name[:-1] == "out" else max(cnt - 4, 0) // span
            if groups > 0:
                with e.Fori(0, groups) as g:
                    i = g * (span // 4)
                    for j in range(4, 4 + span):
                        step(4 * i + j, i, j)
            for k in range(min(4, cnt) + span * groups, cnt):
                step(k, 0, k)

        def w_half(n, a):
            s = (2 * n + a) % 4
            return w_hi[:, s], w_lo[:, s], raw[:, n % 4, 4 * a:4 * a + 4]

        def ada_slots(m, count=1):
            units_ = next(q for q in ADA_RINGS if m in q)
            size = ADA_RINGS[units_]
            ring = ada_long if size == 8 else ada_out1 if size == 6 else ada_ssd if units_[0] == 28 else ada_first
            return ring[:, m % size:m % size + count], size

        ada_pair = lambda m: ADA_SUMMED.index(m) // 2

        names = {}

        def S(name, a=0, n=48, p0=0, p1=P):
            names.setdefault(name, len(names))
            assert len(names) <= 36
            return small[p0:p1, names[name], a:a + n]

        def bc(ap, *shape):
            return ap.broadcast_to(list(shape))

        def one(ap):
            return ap.rearrange("p (a t) -> p a t", a=1)

        last_copy = {q: freed[PARTS[q][0] + PARTS[q][1] - 1][1] for q in ("k0", "v0", "z0", "k1", "v1", "z1")}
        O_BANK = (AB[3], PB[2])
        Y_BANK = (AB[2], AB[3], PB[2])
        FIRST_AFTER = [PARTS[q][0] % 4 for q in ("dt0", "up0", "up0", "dt1", "dt1", "up1", "up1", "up1")]
        SUM_BANK = [PB[(f + 2) % 4] for f in FIRST_AFTER]
        ROW_BANK = [PB[(f + 1) % 4] for f in FIRST_AFTER]
        ADA_BANK = {"q0": PB[3], "k0": PB[3], "v0": PB[3], "out0": PB[2], "down0": PB[0], "q1": PB[3], "k1": PB[3], "v1": PB[3],
                    "out1": PB[1], "down1": PB[2]}
        ADA_AFTER = {("q0", 3): 16, ("k0", 0): 18, ("v0", 0): 20, ("down0", 3): 52, ("down0", 21): 70, ("q1", 3): 72,
                     ("k1", 1): 74, ("k1", 3): 76, ("v1", 1): 78, ("down1", 3): 92, ("down1", 21): 94}
        for k in range(5, 17, 2):
            ADA_AFTER["out0", k], ADA_AFTER["out1", k] = 40 + k - 5, 80 + k - 5

        def has_ada(name, k):
            if name not in ADA_WITH:
                return False
            if name[:-1] == "out":
                return 2 <= k < 14
            count = 20 if name == "down0" else 4
            return k < count if isinstance(k, int) else count > 4

        V_BANK = (PB[0], PB[1])
        OUT_STEPS = [(g, b) for g in range(GH // 4) for b in range(NB)]
        SCAN = [(c, g) for c in range(SEQ // GC) for g in range(GH // 4)]
        block = ctx.enter_context(nc.Block())

        @block.sync
        def _(sp):
            def load_w(n, i=0):
                if n >= 4:
                    sp.wait_ge(w_split, 8 * i + 2 * n - 6)
                sp.dma_start(raw[:, n % 4].rearrange("p (o a) b -> p o (a b)", o=1),
                             w_dram[:, ds(4 * i + n, 1), :]).then_inc(w_landed[n % 4], 16)

            def load_ada(m):
                slot, size = ada_slots(m)
                if any(m in q and m - size in q for q in ADA_RINGS):
                    if m - size in ADA_SUMMED:
                        sp.wait_ge(ada_terms, 8 * ada_pair((m - size) // 2 * 2) + 8)
                    else:
                        sp.wait_ge(ada_added, m - size + 1)
                sp.dma_start(slot.rearrange("p o a b -> p o (a b)"), ada_dram[:, m:m + 1, :]).then_inc(ada_landed[m % 8], 16)

            def stream(n0, end):
                if end - n0 >= 4:
                    with sp.Fori(0, (end - n0) // 4) as i:
                        for j in range(4):
                            load_w(n0 + j, i)
                for n in range(n0 + (end - n0) // 4 * 4, end):
                    load_w(n)

            def hankel_load(v):
                src = bass.AP(tensor=scratch.tensor, offset=v * 384, ap=[[1, P], [768, AH], [1, SEQ]])
                sp.dma_start(hankels[v][:, :, :], src).then_inc(hankel_landed, 16)

            sp.dma_start(prm_rows[:, :, :], prm_dram).then_inc(in_landed[0], 16)
            sp.dma_start(cst[:, :], cst_dram).then_inc(in_landed[1], 16)
            for m in range(4):
                load_ada(m)
            sp.dma_start(x[:, :, :], x_dram).then_inc(in_landed[2], 16)
            for m in range(4, 8):
                load_ada(m)
            sp.dma_start(rows[:, :], row_dram.broadcast_to([P, ROW_COLS])).then_inc(in_landed[3], 16)
            sp.dma_start(bucket[0:33, :, :], bucket_dram).then_inc(in_landed[4], 16)
            sp.dma_start(rel[0:32, :], rel_dram).then_inc(in_landed[4], 16)
            for m in range(8, 16):
                load_ada(m)
            for n in range(4):
                load_w(n)
            sp.wait_ge(vec_copied, 1)
            sp.dma_start(scratch, bias_vec[0:AH, :, :]).then_inc(bias_vec_stored, 16)
            sp.wait_ge(bias_vec_stored, 16)
            hankel_load(0)
            n_q0, n_z0, n_out0, n_up0, n_down0, n_q1, n_out1, n_up1 = (
                PARTS[q][0] for q in ("q0", "z0", "out0", "up0", "down0", "q1", "out1", "up1"))
            stream(4, n_q0 + 2)
            for k in range(6):
                load_w(n_q0 + 2 + k)
                load_ada(16 + k)
            for k in range(6):
                load_ada(22 + k)
                if k % 2:
                    load_w(n_z0 + 2 + k // 2)
            sp.wait_ge(s_ready, 4)
            for m in range(28, 32):
                load_ada(m)
            stream(n_z0 + 5, n_out0 + 4)
            for m in range(32, 36):
                load_ada(m)
            stream(n_out0 + 4, n_out0 + 6)
            for m in range(36, 40):
                load_ada(m)
            sp.wait_ge(d_sum, SSD_G)
            for m in range(40, 44):
                load_ada(m)
            for k in range(4):
                load_w(n_out0 + 6 + k)
                load_ada(44 + k)
            for k in (0, 2):
                load_ada(48 + k)
                load_ada(49 + k)
                load_w(n_out0 + 10 + k)
                load_w(n_out0 + 11 + k)
            stream(n_out0 + 14, n_up0 + 4)
            for m in range(52, 60):
                load_ada(m)
            stream(n_up0 + 4, n_down0 + 4)
            for k in range(12):
                load_w(n_down0 + 4 + k)
                if k >= 4:
                    load_ada(56 + k)
            for k in range(8, 12):
                load_w(n_down0 + 8 + k)
                load_ada(60 + k)
            stream(n_down0 + 20, n_q1 - 20)
            sp.wait_ge(x_ready, 2 * DT)
            hankel_load(1)
            for m in range(72, 76):
                stream(n_q1 - 20 + 4 * (m - 72), n_q1 - 16 + 4 * (m - 72))
                load_ada(m)
            stream(n_q1 - 4, n_q1 + 4)
            for k in range(4, 8):
                load_w(n_q1 + k)
                load_ada(72 + k)
            stream(n_q1 + 8, n_out1 + 6)
            sp.wait_ge(c_o, 12)
            for m in range(80, 86):
                load_ada(m)
            stream(n_out1 + 6, n_out1 + 9)
            for k in (0, 2, 4):
                load_ada(86 + k)
                load_ada(87 + k)
                load_w(n_out1 + 9 + k)
                load_w(n_out1 + 10 + k)
            stream(n_out1 + 15, n_up1 + 4)
            for m in range(92, 96):
                load_ada(m)
            stream(n_up1 + 4, UNITS)
            sp.wait_ge(x_ready, 4 * DT)
            sp.dma_start(out_dram, x[:, :, :]).then_inc(out_stored, 16)
            sp.wait_ge(out_stored, 16)

        @block.tensor
        def _(pe):
            def mm(out, a, b, start=True, stop=True):
                return pe.matmul(out, a, b, start=start, stop=stop, skip_group_check=True)

            def ada_unit(m, bank, first=False):
                pe.wait_ge(ada_landed[m % 8], 16 * (m // 8 + 1))
                for k in range(8):
                    last = mm(bank[:, 0:P], ada_slots(m)[0][:, 0, k], c_silu[:, k, C_COL - m:C_COL - m + P], first and k == 0, k == 7)
                last.then_inc(ada_added, 1)

            def ada_sums(m, i, bank, first=False):
                p = ada_pair(m)
                pe.wait_ge(ada_terms, 8 * p + 8 + 16 * i)
                if not isinstance(i, int):
                    pe.nop(nofuse=True)
                for q in range(2):
                    last = mm(bank[:, 0:P], ada_sum[:, p % 2, q], C("pick", P - 1 - m - q) if isinstance(i, int) else
                              cst[:, ds(CST["pick"] + P - 1 - m - q - 4 * i, P)], first and q == 0, True)
                last.then_inc(ada_added, 2)

            def ada_with(name, k, i, j):
                if isinstance(k, int) and (name, k) in ADA_AFTER:
                    m = ADA_AFTER[name, k]
                    ada_sums(m, 0, ADA_BANK[name], m in (16, 40, 52, 72, 80, 92))
                elif has_ada(name, k) and not isinstance(k, int) and j % 2:
                    ada_sums(ADA_WITH[name] + j - 3, i, ADA_BANK[name])

            def project(name, token=False, norm=None, some=None):
                n0 = PARTS[name][0]

                def step(k, i, j):
                    n = n0 + j
                    if before[n] is not None:
                        s, at, per = freed[before[n]]
                        pe.wait_ge(s, 4 * per * i + at)
                    for a in range(2):
                        pe.wait_ge(w_split, 8 * i + 2 * n + a + 1)
                        hi, lo, _ = w_half(n, a)
                        for q in range(4):
                            t = 4 * a + q
                            if norm is not None and isinstance(k, int) and k == 0:
                                pe.wait_ge(h_ready, 8 * norm + t + 1)
                            for p_, (u, v) in enumerate(((hi, h_hi), (hi, h_lo), (lo, h_hi))):
                                st, en = t == 0 and p_ == 0, t == 7 and p_ == 2
                                if token:
                                    for b in range(NB):
                                        c = slice(b * P, b * P + P)
                                        last = mm(banks[n][:, c], v[:, t, c], u[:, q], st and b == 0, en)
                                else:
                                    last = mm(banks[n][:, 0:SEQ], u[:, q], v[:, t], st, en)
                        last.then_inc(w_used, 1)
                    ada_with(name, k, i, j)

                if some is None:
                    units(pe, name, step)
                else:
                    for k in some:
                        step(k, 0, k)

            def project_values(some):
                n0, cnt = PARTS["v1"]
                for k in some:
                    if k == 0:
                        for n in (n0, n0 + 1):
                            s, at, _ = freed[before[n]]
                            pe.wait_ge(s, at)
                    for a in range(2):
                        pe.wait_ge(w_split, 2 * (n0 + k) + a + 1)
                        hi, lo, _ = w_half(n0 + k, a)
                        t = 2 * k + a
                        for p_, (u, v) in enumerate(((hi, h_hi), (hi, h_lo), (lo, h_hi))):
                            for b in range(NB):
                                last = mm(V_BANK[b][:, :], v[:, t, b * P:b * P + P], u.rearrange("p a b -> p (a b)"),
                                          t == 0 and p_ == 0, t == 7 and p_ == 2)
                        last.then_inc(w_used, 1)
                    ada_with("v1", k, 0, k)

            def accumulate(name, ready, first_ready, at):
                n0, cnt = PARTS[name]

                def step(k, i, j):
                    n = n0 + j
                    if ready is not None:
                        pe.wait_ge(ready, first_ready + k + 1)
                    for a in range(2):
                        pe.wait_ge(w_split, 8 * i + 2 * n + a + 1)
                        hi, lo, _ = w_half(n, a)
                        for q in range(4):
                            t = 4 * a + q
                            s = at(k)
                            for p_, (u, v) in enumerate(((hi, a_hi), (hi, a_lo), (lo, a_hi))):
                                last = mm(acc(t), u[:, q], v[:, ds(s, 1), :], j == 0 and p_ == 0 and t % 2 == 0,
                                          j == cnt - 1 and p_ == 2)
                        last.then_inc(w_used, 1)
                    ada_with(name, k, i, j)

                units(pe, name, step)

            def column_sums(out, tile, col, start, stop):
                for b in range(NB):
                    last = mm(out[:, 0:P], tile[:, b * P:b * P + P], C("pick", P - 1 - col - b), start and b == 0, stop)
                return last

            def spread_rows(out, cols):
                for b in range(NB):
                    last = mm(out[:, b * P:b * P + P], bc(cols[:, b:b + 1], P, P), C("ident"))
                return last

            def root_mean_square(event):
                for k in range(DT):
                    pe.wait_ge(squares, event * DT + k + 1)
                    last = column_sums(SUM_BANK[event], sq[:, k], 0, k == 0, k == DT - 1)
                last.then_inc(sums, 1)
                pe.wait_ge(inv_rms, event + 1)
                spread_rows(ROW_BANK[event], S("inv_rms", 0, 2)).then_inc(spread, 1)

            def bias_tiles(layer):
                pe.wait_ge(hankel_landed, 16 * (layer + 1))
                for q in range(4):
                    last = mm(AB[q][:, :], C("reverse"), hankels[layer][:, 2 * q:2 * q + 2, :])
                last.then_inc(hankel_mm, 1)

            def attention(layer):
                n8 = AH * layer
                if layer:
                    project_values((0, 1))
                pe.wait_ge(bias_ready, layer + 1)
                pe.wait_ge(conv_taps, 3 * (XBC_T + layer * GQ_T))
                pe.wait_ge(copied, last_copy[f"k{layer}"])
                for h in range(AH):
                    p0, t = AD * (h % 2), h // 2
                    q_, k_ = att_q[p0:p0 + AD, t], att_k[p0:p0 + AD, t if layer else h // 4]
                    if h >= 3:
                        pe.wait_ge(s_biased, 2 * (n8 + h - 2))
                    mm(AB[h % 3][:, 0:SEQ], q_[:, P:2 * P], k_[:, 0:SEQ])
                    mm(AB[h % 3][:, SEQ:SEQ + P], q_[:, 0:P], k_[:, 0:P]).then_inc(s_scored, 1)
                if layer == 0:
                    project("z0", some=(0,))
                    for m in range(3):
                        ada_unit(22 + 2 * m, PB[3])
                        ada_unit(23 + 2 * m, PB[3])
                        if m < 2:
                            project("z0", some=(m + 1,))
                else:
                    project_values((2, 3))
                    pe.wait_ge(s_biased, 32)
                    for m in range(6):
                        if m >= 4:
                            pe.wait_ge(v_copied, m - 3)
                        for q in range(4):
                            b, h = (4 * m + q) // GH, (4 * m + q) % GH
                            last = pe.transpose(AB[m % 4][:, q * P:q * P + P], conv1[:, 24 + h, b * P:b * P + P], C("ident"))
                        last.then_inc(v_turned, 1)
                    pe.wait_ge(v_copied, 6)
                pe.wait_ge(copied, last_copy[f"v{layer}"])

                def values(h):
                    p0, t = AD * (h % 2), h // 2
                    c0 = AD * (h if layer else h // 4)
                    o, pt = O_BANK[t % 2][p0:p0 + AD], probs_t[:, h % 2]
                    pe.wait_ge(s_copied, n8 + h + 1)
                    if t >= 2:
                        pe.wait_ge(s_ready, 4 * layer + t - 1)
                    mm(o[:, 0:P], att_v[:, 0, c0:c0 + AD], pt[:, 2 * P:3 * P])
                    mm(o[:, P:2 * P], att_v[:, 0, c0:c0 + AD], pt[:, 0:P], True, False)
                    mm(o[:, P:2 * P], att_v[:, 1, c0:c0 + AD], pt[:, P:2 * P], False, True).then_inc(s_out, 1)

                for h in range(AH):
                    pe.wait_ge(s_norm, n8 + h + 1)
                    if h >= 3:
                        pe.wait_ge(s_copied, n8 + h - 2)
                    for b in range(3):
                        last = pe.transpose(AB[h % 3][:, b * P:b * P + P], scores[:, h, b * P:b * P + P], C("ident"))
                    last.then_inc(s_turned, 1)
                    if h:
                        values(h - 1)
                values(AH - 1)
                pe.wait_ge(s_ready, 4 * (layer + 1))

            def ssd_outputs(n):
                b, h0 = n // 6, 4 * (n % 6)
                pe.wait_ge(d_mmat, n + 1)
                if n >= 3:
                    pe.wait_ge(d_y, n - 2)
                for q in range(4):
                    h = h0 + q
                    p0 = SSD_P * (h % 2)
                    o, f = Y_BANK[n % 3][p0:p0 + SSD_P, (q // 2) * P:(q // 2 + 1) * P], slice(SSD_P * h, SSD_P * h + SSD_P)
                    last = mm(o, xs_tok[:, b, f], mmat[:, n % 2, q], True, b == 0)
                    if b:
                        last = mm(o, h_in[:, f], cexp[:, n % 2, q], False, True)
                last.then_inc(d_y_mm, 1)

            def ssd():
                pe.wait_ge(conv_done, XBC_T)

                def item(m):
                    if m >= 4:
                        pe.wait_ge(d_item, m - 3)
                    return AB[m % 4]

                for m in range(7):
                    bank = item(m)
                    for q in range(4):
                        t, b = 4 * (m % 3) + q, m // 3
                        src = conv0[:, t, b * P:b * P + P] if m < 6 else conv0[:, 12 + q, 0:P]
                        last = pe.transpose(bank[:, q * P:q * P + P], src, C("ident"))
                    last.then_inc(d_item_mm, 1)
                ada_unit(28, PB[3])
                for b in range(NB):
                    bank = item(7 + b)
                    for g in range(SSD_G):
                        t = slice(b * P, b * P + P)
                        last = mm(bank[:, g * P:g * P + P], conv0[:, 12 + g, t], conv0[:, 16 + g, t])
                    last.then_inc(d_item_mm, 1)
                pe.wait_ge(gate_ready, 1)
                for b in range(NB):
                    mm(PB[2][:, 24 * b:24 * b + 24], C("triu"), S("da", 24 * b, 24))
                mm(PB[2][:, 48:72], C("ones"), S("da", 0, 24)).then_inc(d_cum_mm, 1)
                project("z0", some=(3,))
                ada_unit(29, PB[3])
                pe.wait_ge(d_xd, 1)
                for g in range(SSD_G):
                    mm(item(9 + g)[:, 0:384], b_tok[:, g], xd[:, 384 * g:384 * g + 384]).then_inc(d_item_mm, 1)
                pe.wait_ge(d_cum, 1)
                pe.wait_ge(d_item, 13)
                for n in range(12):
                    b, h0 = n // 6, 4 * (n % 6)
                    if n >= 2:
                        pe.wait_ge(d_decay, n - 1)
                    for q in range(4):
                        col = S("da", 24 * b + h0 + q, 1)
                        last = mm(AB[n % 2][:, q * P:q * P + P], bc(col, P, P), C("triu"))
                    last.then_inc(d_decay_mm, 1)
                    if n < 8:
                        project("z0", some=(4 + n,))
                    for m in ((24 + n,) if n in (6, 7) else (16 + 2 * n, 17 + 2 * n) if n >= 8 else ()):
                        ada_unit(m, PB[3])
                    if n:
                        ssd_outputs(n - 1)
                ssd_outputs(11)
                for g in range(SSD_G):
                    pe.wait_ge(d_sq, g + 1)
                    for k in range(3):
                        last = column_sums(AB[0], y_sq[:, g % 2, k], 2 * g, g == 0 and k == 0, g == 3 and k == 2)
                    last.then_inc(d_sum, 1)
                pe.wait_ge(d_inv, 1)
                for g in range(SSD_G):
                    last = spread_rows(PB[g // 2][:, (g % 2) * SEQ:(g % 2 + 1) * SEQ], S("group_inv", 2 * g, 2))
                    if g % 2:
                        last.then_inc(d_spread, 1)

            def stacks(out, a, b, m):
                for j in range(2):
                    for q in range(8):
                        last = mm(out[j * GC:j * GC + GC, q * GC:q * GC + GC], a(8 * m + q)[:, j * GC:j * GC + GC], b(8 * m + q))
                return last

            def lengths(n):
                pe.wait_ge(n_sq, n + 1)
                for q in range(2):
                    last = column_sums(PB[2], g_sq[:, n % 3, q], 4 * n + 2 * q, n == 0 and q == 0, n == 11 and q == 1)
                last.then_inc(n_sum, 1)

            def unit_lengths():
                pe.wait_ge(n_inv, 1)
                pe.wait_ge(bias_ready, 2)
                for n in range(12):
                    if n >= 4:
                        pe.wait_ge(n_unit, n - 3)
                    for q in range(2):
                        last = spread_rows(AB[n % 4][:, q * SEQ:q * SEQ + SEQ], S("l2_inv", 4 * n + 2 * q, 2))
                    last.then_inc(n_spread, 1)
                pe.wait_ge(gate_ready, 2)
                either = [bc(C("same_chunk", j * GC, 1), P, P) for j in range(2)]
                for q, summed in enumerate([C("triu_chunk"), C("same_chunk")] + either):
                    last = mm(PB[2][:, 24 * q:24 * q + 24], summed, S("da", 0, 24))
                last.then_inc(g_cum_mm, 1)
                pe.wait_ge(n_unit, 12)

            def gdn():
                pe.wait_ge(g_cum, 1)
                for n in range(6):
                    if n >= 2:
                        pe.wait_ge(g_decay, n - 1)
                    for q in range(4):
                        last = mm(PB[n % 2][:, q * P:q * P + P], bc(S("da", 4 * n + q, 1), P, P), C("triu_chunk"))
                    last.then_inc(g_decay_mm, 1)
                pe.wait_ge(n_unit, 12)
                for n in range(6):
                    if n >= 4:
                        pe.wait_ge(k_copied, n - 3)
                    for q in range(4):
                        b, h = (4 * n + q) // GH, (4 * n + q) % GH
                        last = pe.transpose(AB[n % 4][:, q * P:q * P + P], conv1[:, 12 + h, b * P:b * P + P], C("ident"))
                    last.then_inc(k_turned, 1)
                pe.wait_ge(k_copied, 6)
                for m in range(3):
                    for w, rhs in ((0, 12), (1, 0)):
                        bank = 2 * m + w
                        if bank >= 4:
                            pe.wait_ge(g_gram, bank - 3)
                        for q in range(8):
                            b, h = (8 * m + q) // GH, (8 * m + q) % GH
                            for j in range(2):
                                t = slice(b * P + j * GC, b * P + j * GC + GC)
                                last = mm(AB[bank % 4][j * GC:j * GC + GC, q * GC:q * GC + GC], conv1[:, 12 + h, t],
                                          conv1[:, rhs + h, t])
                        last.then_inc(g_gram_mm, 1)
                of, iv, it = (lambda s: off_bd[:, s]), (lambda s: inv[:, s]), (lambda s: inv_t[:, s])
                it_bd, sy, sy_bd = (lambda s: inv_t_bd[:, s]), (lambda s: step_y[:, s]), (lambda s: step_y_bd[:, s])
                pe.wait_ge(g_decay, 6)
                for lv in range(LEVELS):
                    for m in range(3):
                        pe.wait_ge(i_off, 3 * lv + m + 1)
                        if lv:
                            pe.wait_ge(i_inv, 3 * (lv - 1) + m + 1)
                        stacks(BANKS[m], of, iv if lv else (lambda s: C("ident_chunk", 0, GC)), m).then_inc(i_y_mm, 1)
                    if not lv:
                        pe.wait_ge(g_gram, 6)
                        continue
                    for m in range(3):
                        at = 3 * (lv - 1) + m + 1
                        if at <= ZT:
                            project("z1", some=(at - 1,))
                        if lv < LEVELS - 1:
                            pe.wait_ge(i_y, at)
                            pe.wait_ge(i_bd, at)
                            stacks(BANKS[3 + m], it_bd, sy, m).then_inc(i_z_mm, 1)
                        pe.wait_ge(i_y_bd, at)
                        stacks(BANKS[m], sy_bd, it, m).then_inc(i_zt_mm, 1)
                pe.wait_ge(i_inv, 3 * LEVELS)
                pe.wait_ge(g_scaled, 4)

                def ks(n):
                    c, g = SCAN[n]
                    if not c:
                        return
                    pe.wait_ge(c_state, 3 * (c - 1) + g + 1)
                    if n >= 4:
                        pe.wait_ge(c_resid, n)
                    for q in range(4):
                        h = 4 * g + q
                        last = mm(BANKS[0][(c % 2) * GC:(c % 2) * GC + GC, q * GD:q * GD + GD],
                                  conv1[:, 12 + h, c * GC:c * GC + GC], state[:, h])
                    last.then_inc(c_ks_mm, 1)

                def tr(n):
                    c, g = SCAN[n]
                    b, r = c // 2, slice((c % 2) * GC, (c % 2) * GC + GC)
                    pe.wait_ge(c_resid, n + 1)
                    if n >= 2:
                        pe.wait_ge(c_vnew, n - 1)
                    for q in range(4):
                        h = 4 * g + q
                        last = mm(BANKS[2 + n % 2][r, q * GD:q * GD + GD], inv_t[:, b * GH + h], resid[:, c % 2, n % 2, q])
                    last.then_inc(c_tr_mm, 1)

                def ou(n):
                    c, g = SCAN[n]
                    b, r = c // 2, slice((c % 2) * GC, (c % 2) * GC + GC)
                    pe.wait_ge(c_vnew, n + 1)
                    if n >= 2:
                        pe.wait_ge(c_o, n - 1)
                    for q in range(4):
                        h = 4 * g + q
                        o = BANKS[4 + n % 2][r, q * GD:q * GD + GD]
                        if c:
                            mm(o, conv1[:, h, c * GC:c * GC + GC], state[:, h], True, False)
                        last = mm(o, attn_t[:, b * GH + h], v_new[:, c % 2, g, q], not c, True)
                    last.then_inc(c_o_mm, 1)
                    if c == 3:
                        return
                    if n >= 2:
                        pe.wait_ge(c_state, n - 1)
                    for q in range(4):
                        last = mm(BANKS[6 + n % 2][:, q * GD:q * GD + GD], k_tok[:, b, 4 * g + q], v_new[:, c % 2, g, q])
                    last.then_inc(c_u_mm, 1)

                for n in range(len(SCAN) + 2):
                    if n < len(SCAN):
                        ks(n)
                    if 0 <= n - 1 < len(SCAN):
                        tr(n - 1)
                    if n >= 2:
                        ou(n - 2)
                for n, (g, b) in enumerate(OUT_STEPS):
                    pe.wait_ge(o_scaled, n + 1)
                    if n >= 3:
                        pe.wait_ge(o_mixed, n - 2)
                    for q in range(4):
                        last = pe.transpose(PB[1 + n % 3][:, q * P:q * P + P], o_tok[:, b, 4 * g + q], C("ident"))
                    last.then_inc(o_turned, 1)

            pe.wait_ge(in_landed[0], 16)
            pe.wait_ge(in_landed[1], 16)
            for g in range(PRM_G):
                last = pe.transpose(PB[g // 4][:, (g % 4) * P:(g % 4 + 1) * P], prm_rows[:, g, :], C("ident"))
            last.then_inc(prm_turned, 1)
            pe.wait_ge(c_ready, 1)
            for m in range(16):
                if m not in ADA_SUMMED:
                    ada_unit(m, AB[3], first=m == 0)
                elif m % 2 == 0:
                    ada_sums(m, 0, AB[3])
            pe.wait_ge(in_landed[4], 32)
            pe.wait_ge(rel_ones, 1)
            for v in range(2):
                last = mm(AB[v][0:AH, 0:384], rel[0:33, :], bucket[0:33, v, :])
            last.then_inc(vec_mm, 1)
            pe.wait_ge(prm_ready, 1)
            root_mean_square(0)
            pe.wait_ge(mods_read, 1)
            project("dt0", token=True, norm=0)
            project("conv0")
            pe.wait_ge(vec_copied, 1)
            bias_tiles(0)
            pe.wait_ge(conv_taps, 3 * XBC_T)
            project("q0")
            project("k0")
            project("v0", token=True)
            attention(0)
            ssd()
            accumulate("out0", mix_ready, 0, lambda k: k if not isinstance(k, int) or k < 12 else k + 6)
            root_mean_square(1)
            root_mean_square(2)
            project("up0", norm=1)
            accumulate("down0", g_ready, 0, lambda k: k)
            root_mean_square(3)
            root_mean_square(4)
            project("dt1", token=True, norm=2)
            project("conv1")
            bias_tiles(1)
            pe.wait_ge(conv_taps, 3 * (XBC_T + GQ_T))
            for k in range(4):
                project("q1", some=(k,))
                lengths(2 * k)
                lengths(2 * k + 1)
            for k in range(4):
                project("k1", some=(k,))
                if k < 2:
                    lengths(8 + 2 * k)
                    lengths(9 + 2 * k)
            unit_lengths()
            attention(1)
            gdn()
            accumulate("out1", mix_ready, MIX_T, lambda k: k if not isinstance(k, int) or k < 12 else k + 6)
            root_mean_square(5)
            root_mean_square(6)
            project("up1", norm=3)
            accumulate("down1", g_ready, FT, lambda k: k)
            root_mean_square(7)

        @block.scalar
        def _(act):
            chain = [0]

            def link(ins):
                chain[0] += 1
                ins.then_inc(act_step, 1)
                act.wait_ge(act_step, chain[0])

            def round_half(n, a, i=0):
                if n >= UNITS:
                    return
                if a == 0:
                    act.wait_ge(w_landed[n % 4], 16 * i + 16 * (n // 4 + 1))
                if 2 * n + a >= 4:
                    act.wait_ge(w_used, 8 * i + 2 * n + a - 3)
                hi, _, src = w_half(n, a)
                act.activation(hi, src, ACT.Copy).then_inc(w_rounded, 1)

            def stream(name, before=None, after=None, some=None):
                n0, cnt = PARTS[name]

                def step(k, i, j):
                    n = n0 + j
                    round_half(n + 2, 0, i)
                    if before is not None:
                        act.wait_ge(w_used, 8 * i + 2 * n + 2)
                        act.nop(nofuse=True)
                        before(k, i, j, banks[n][:, 0:SEQ])
                    round_half(n + 2, 1, i)
                    if after is not None and j:
                        after(k - 1, i, j - 1)

                if some is None:
                    units(act, name, step)
                else:
                    for k in some:
                        step(k, 0, k)
                if after is not None:
                    after(cnt - 1, 0, cnt - 1)

            def conv(layer):
                dst, base = convs[layer], layer * XBC_T
                cnt = (XBC_T, GQ_T)[layer]

                def first(k, i, j, ps):
                    w = prm[:, ds(PRM[f"conv{layer}_w"] + 3 * cnt + k, 1)]
                    b = prm[:, ds(PRM["conv0_b"] + k, 1)] if layer == 0 else 0.0
                    act.activation(dst[:, ds(k, 1), :], one(ps), ACT.Identity, bias=b, scale=w).then_inc(conv_first, 1)

                def silu(k, i, j):
                    act.wait_ge(conv_taps, 3 * (base + k) + 3)
                    act.nop(nofuse=True)
                    act.activation(dst[:, ds(k, 1), :], dst[:, ds(k, 1), :], ACT.Silu).then_inc(conv_done, 1)

                stream(f"conv{layer}", first, silu)

            def up(layer):
                base = 2 * FT * layer

                def first(k, i, j, ps):
                    half, s = j % 2, j // 2 % 2
                    col = half * FT + 2 * i + j // 2
                    w = prm[:, ds(PRM["up_w"] + (3 * layer + 2) * 2 * FT + col, 1)]
                    b = prm[:, ds(PRM["up_b"] + layer * 2 * FT + col, 1)]
                    act.activation((yv if half else yg)[:, s], ps, ACT.Identity, bias=b, scale=w).then_inc(up_first, 1)

                def finish(k, i, j):
                    s = j // 2 % 2
                    pair = 2 * i + j // 2
                    if j % 2 == 0:
                        act.wait_ge(up_taps, 2 * (base + k) + 2)
                        act.activation(yg[:, s], yg[:, s], ACT.Gelu_apprx_tanh).then_inc(gelu_done, 1)
                    else:
                        act.wait_ge(prod_done, FT * layer + pair + 1)
                        act.nop(nofuse=True)
                        act.activation(a_hi[:, ds(pair, 1), :], prod[:, s:s + 1], ACT.Copy).then_inc(g_rounded, 1)

                stream(f"up{layer}", first, finish)

            def copy_unit(fn, dst):
                return lambda k, i, j, ps: act.activation(dst(k), ps, fn).then_inc(copied, 1)

            def root(event, scale=1.0 / D_MODEL):
                act.wait_ge(sums, event + 1)
                act.activation(S("rms", 0, 2), SUM_BANK[event][:, 0:2], ACT.Sqrt, bias=EPS, scale=scale).then_inc(roots, 1)

            def pre_norm(event, layer, which, after):
                for q in range(4):
                    if after is None:
                        if q == 0:
                            act.wait_ge(in_landed[2], 16)
                    else:
                        act.wait_ge(x_ready, 8 * after + 2 * q + 2)
                    act.activation(sq[:, 2 * q:2 * q + 2], x[:, 2 * q:2 * q + 2], ACT.Square).then_inc(squares, 2)
                if after is None:
                    round_half(0, 0)
                    round_half(0, 1)
                    round_half(1, 0)
                    round_half(1, 1)
                root(event)
                norm = 2 * layer + which
                for k in range(DT):
                    act.wait_ge(scaled, DT * norm + k + 1)
                    act.activation(h_hi[:, k], yr[:, k], ACT.Identity, bias=mods[:, layer, 3 * which, k:k + 1]).then_inc(h_rounded, 1)

            def post_norm(event, name):
                act.wait_ge(w_used, 2 * (PARTS[name][0] + PARTS[name][1]))
                for q in range(4):
                    act.activation(sq[:, 2 * q:2 * q + 2].rearrange("p a t -> p (a t)"), AB[q][:, :], ACT.Square).then_inc(squares, 2)
                root(event)

            def attention(layer):
                n8 = AH * layer
                if layer:
                    stream("v1", some=(0, 1))
                act.wait_ge(s_max, layer + 1)
                for h in range(AH):
                    act.activation(scores[:, h, 0:SEQ], scores[:, h, 0:SEQ], ACT.Exp, bias=S("neg_max", h, 1),
                                   accum_out=S("prob_sum", h, 1)).then_inc(s_exp, 1)
                    act.activation(scores[:, h, SEQ:384], scores[:, h, SEQ:384], ACT.Exp, bias=S("neg_max", 8 + h, 1),
                                   accum_out=S("prob_sum", 8 + h, 1)).then_inc(s_exp, 1)
                if layer == 0:
                    act.activation(S("sink_exp", 0, 16), S("sink_exp", 0, 16), ACT.Exp).then_inc(s_exp, 1)
                if layer == 0:
                    stream("z0", copy_z, some=(0, 1, 2))
                else:
                    stream("v1", some=(2, 3))
                    act.wait_ge(w_used, 2 * (PARTS["v1"][0] + 4))
                    for b in range(NB):
                        act.activation(att_v[:, b], V_BANK[b][:, :], ACT.Copy).then_inc(copied, 2)
                    for m in range(6):
                        act.wait_ge(v_turned, m + 1)
                        b, h = 4 * m // GH, 4 * m % GH
                        act.activation(v_tok[:, b, h:h + 4].rearrange("p a b -> p (a b)"), AB[m % 4][:, :], ACT.Copy).then_inc(v_copied, 1)
                for h in range(AH):
                    act.wait_ge(s_turned, n8 + h + 1)
                    if h >= 2:
                        act.wait_ge(s_out, n8 + h - 1)
                    act.activation(probs_t[:, h % 2], AB[h % 3][:, 0:384], ACT.Copy).then_inc(s_copied, 1)
                    if h % 2 == 1 and h >= 3:
                        attention_out(layer, h // 2 - 1)
                attention_out(layer, 3)

            def attention_out(layer, t):
                act.wait_ge(s_out, AH * layer + 2 * t + 2)
                act.activation(a_hi[:, 18 + t], O_BANK[t % 2][:, 0:SEQ], ACT.Copy).then_inc(s_rounded, 1)

            def gates(layer):
                n = 48 if layer == 0 else 24
                heads = (SSD_H, GH)[layer]
                act.wait_ge(gate_abs, layer + 1)
                act.activation(S("e", 0, n), S("abs", 0, n), ACT.Exp, scale=-1.0).then_inc(gate_exp, 1)
                act.activation(S("a", 0, heads), rows[:, ROW[f"a_log{layer}"]:ROW[f"a_log{layer}"] + heads], ACT.Exp).then_inc(gate_exp, 1)
                act.activation(S("be", 0, 24), S("bx", 0, 24), ACT.Exp, scale=-1.0).then_inc(gate_exp, 1)
                act.wait_ge(gate_ln, layer + 1)
                act.activation(S("ln", 0, n), S("u", 0, n), ACT.Ln).then_inc(gate_exp, 1)

            def copy_z(k, i, j, ps):
                act.activation(zs[:, k], ps, ACT.Copy).then_inc(copied, 1)

            def z_to_silu(k, i, j, ps):
                act.activation(zs[:, k], ps, ACT.Silu).then_inc(copied, 1)

            def silu_z():
                act.wait_ge(copied, last_copy["z0"])
                for g in range(4):
                    act.activation(zs[:, 3 * g:3 * g + 3], zs[:, 3 * g:3 * g + 3], ACT.Silu).then_inc(z_silu, 1)

            def ssd():
                flat = lambda ap: ap.rearrange("p a b -> p (a b)")

                def item(m, dst, width=512):
                    act.wait_ge(d_item_mm, m + 1)
                    act.activation(dst, AB[m % 4][:, 0:width], ACT.Copy).then_inc(d_item, 1)

                gates(0)
                for m in range(6):
                    item(m, xs_tok[:, m // 3, 512 * (m % 3):512 * (m % 3) + 512])
                item(6, flat(b_tok[:, :, :]))
                for b in range(NB):
                    item(7 + b, flat(cb[:, b]))
                act.wait_ge(d_cum, 1)
                act.activation(S("tail", 0, 24), S("tail", 0, 24), ACT.Exp).then_inc(d_tail, 1)
                stream("z0", copy_z, some=(3,))
                for g in range(SSD_G):
                    item(9 + g, h_in[:, 384 * g:384 * g + 384], 384)
                for n in range(12):
                    act.wait_ge(d_diff, n + 1)
                    if n >= 6:
                        act.wait_ge(d_y_mm, n - 1)
                        act.activation(flat(cexp[:, n % 2]), AB[n % 2][:, :], ACT.Exp)
                    act.activation(flat(lmat[:, n % 2]), flat(lmat[:, n % 2]), ACT.Exp).then_inc(d_decay, 1)
                    if n < 8:
                        stream("z0", copy_z, some=(4 + n,))
                silu_z()
                for g in range(SSD_G):
                    act.wait_ge(d_gated, g + 1)
                    if g >= 2:
                        act.wait_ge(d_sum, g - 1)
                    act.activation(y_sq[:, g % 2], y_ssd[:, 3 * g:3 * g + 3], ACT.Square).then_inc(d_sq, 1)
                act.wait_ge(d_sum, SSD_G)
                act.activation(S("group_rms", 0, 8), AB[0][:, 0:8], ACT.Sqrt, bias=EPS, scale=1.0 / 384).then_inc(d_root, 1)
                act.wait_ge(ada_added, 40)
                for g in range(SSD_G):
                    act.wait_ge(d_mix, g + 1)
                    act.activation(a_hi[:, 3 * g:3 * g + 3], y_mix[:, 3 * g:3 * g + 3], ACT.Copy).then_inc(d_rounded, 1)

            def square(n):
                if n >= 3:
                    act.wait_ge(n_sum, n - 2)
                act.activation(g_sq[:, n % 3], conv1[:, 2 * n:2 * n + 2], ACT.Square).then_inc(n_sq, 1)

            def lengths():
                gates(1)
                act.wait_ge(g_cum, 1)
                act.activation(S("tail", 0, 24), S("tail", 0, 24), ACT.Exp).then_inc(g_tail, 1)
                for j in range(2):
                    act.activation(S(f"tot{j}", 0, 24), S(f"tot{j}", 0, 24), ACT.Exp).then_inc(g_tot, 1)

            def gdn():
                flat = lambda ap: ap.rearrange("p a b -> p (a b)")

                for n in range(6):
                    act.wait_ge(g_diff, n + 1)
                    act.activation(flat(egc[:, 4 * n:4 * n + 4]), PB[n % 2][:, :], ACT.Exp)
                    d_ = flat(dec[:, 4 * n:4 * n + 4])
                    act.activation(d_, d_, ACT.Exp).then_inc(g_decay, 1)
                halves = (slice(0, GC), slice(GC, P))

                def transposed_bd(at, m):
                    act.wait_ge(i_inv, at)
                    for r in halves:
                        last = act.activation(inv_t_bd[r, 8 * m:8 * m + 8, r], inv_t[r, 8 * m:8 * m + 8], ACT.Copy)
                    last.then_inc(i_bd, 1)

                act.wait_ge(zeroed, 2)
                for m in range(3):
                    transposed_bd(m + 1, m)
                for lv in range(1, LEVELS):
                    for m in range(3):
                        s8 = slice(8 * m, 8 * m + 8)
                        act.wait_ge(i_y_mm, 3 * lv + m + 1)
                        if lv < LEVELS - 1:
                            act.activation(flat(step_y[:, s8]), BANKS[m][:, :], ACT.Copy).then_inc(i_y, 1)
                        if lv == 1 and m == 0:
                            act.wait_ge(zeroed, 3)
                        for r in halves:
                            last = act.activation(step_y_bd[r, s8, r], BANKS[m][r, :].rearrange("p (a d) -> p a d", a=8), ACT.Copy)
                        last.then_inc(i_y_bd, 1)
                        if 3 * (lv - 1) + m < ZT:
                            stream("z1", z_to_silu, some=(3 * (lv - 1) + m,))
                    if lv < LEVELS - 2:
                        for m in range(3):
                            transposed_bd(3 * lv + m + 1, m)
                for n, (c, g) in enumerate(SCAN):
                    b, r = c // 2, slice((c % 2) * GC, (c % 2) * GC + GC)
                    act.wait_ge(c_o_mm, n + 1)
                    for q in range(4):
                        act.activation(o_sq[r, b, 4 * g + q], BANKS[4 + n % 2][r, q * GD:q * GD + GD], ACT.Square,
                                       accum_out=S("o_rms", b * GH + 4 * g + q, 1, r.start, r.stop)).then_inc(o_sqd, 1)
                    act.activation(o_tok[r, b, 4 * g:4 * g + 4], BANKS[4 + n % 2][r, :].rearrange("p (a d) -> p a d", a=4),
                                   ACT.Copy).then_inc(c_o, 1)
                act.wait_ge(o_sqd, 48)
                act.activation(S("o_rms", 0, 24), S("o_rms", 0, 24), ACT.Sqrt, bias=EPS, scale=1.0 / GD).then_inc(o_root, 1)
                for n, (g, b) in enumerate(OUT_STEPS):
                    act.wait_ge(o_mixed, n + 1)
                    act.activation(a_hi[:, 4 * g:4 * g + 4, b * P:b * P + P], o_t[:, n % 3], ACT.Copy).then_inc(o_rounded, 1)

            def key0(k, i, j, ps):
                for kv in range(2):
                    for half in range(2):
                        last = act.activation(att_k[half * AD:half * AD + AD, kv], ps[kv * AD:kv * AD + AD], ACT.Copy)
                last.then_inc(copied, 1)

            def values(k, i, j, ps):
                act.activation(att_v[:, :, P * j:P * j + P], ps.rearrange("p (b c) -> p b c", b=NB), ACT.Copy).then_inc(copied, 1)

            def mixer(layer):
                stream(f"dt{layer}")
                conv(layer)
                for q in range(4):
                    if q == 0:
                        act.wait_ge(hankel_mm, layer + 1)
                        if layer == 0:
                            act.wait_ge(bias_vec_stored, 16)
                    last = act.activation(bias[:, 2 * q:2 * q + 2].rearrange("p a b -> p (a b)"), AB[q][:, :], ACT.Copy)
                last.then_inc(bias_ready, 1)
                query = lambda k, i, j, ps: act.activation(att_q[:, j], ps, ACT.Copy, scale=AD ** -0.5).then_inc(copied, 1)
                if layer == 0:
                    stream("q0", query)
                    stream("k0", key0)
                else:
                    act.wait_ge(conv_done, XBC_T + GQ_T)
                    square(0)
                    square(1)
                    square(2)
                    for k in range(8):
                        if k < 4:
                            stream("q1", query, some=(k,))
                        else:
                            stream("k1", copy_unit(ACT.Copy, lambda k: att_k[:, k]), some=(k - 4,))
                        for n in (2 * k + 3, 2 * k + 4):
                            if n < 12:
                                square(n)
                        if k == 6:
                            act.wait_ge(n_sum, 12)
                            act.activation(S("l2", 0, 48), PB[2][:, 0:48], ACT.Sqrt, bias=EPS).then_inc(n_root, 1)
                    lengths()
                if layer == 0:
                    stream("v0", values)
                attention(layer)
                (ssd, gdn)[layer]()
                stream(f"out{layer}")

            act.wait_ge(prm_ready, 1)
            act.wait_ge(c_zeroed, 1)
            act.activation(c_cols[:, :], prm[:, PRM["c"]:PRM["c"] + 8], ACT.Silu)
            act.activation(c_silu[:, :, C_COL], prm[:, PRM["c"]:PRM["c"] + 8], ACT.Silu).then_inc(c_ready, 1)
            pre_norm(0, 0, 0, None)
            mixer(0)
            post_norm(1, "out0")
            pre_norm(2, 0, 1, 0)
            up(0)
            stream("down0")
            post_norm(3, "down0")
            pre_norm(4, 1, 0, 1)
            mixer(1)
            post_norm(5, "out1")
            pre_norm(6, 1, 1, 2)
            up(1)
            stream("down1")
            post_norm(7, "down1")

        @block.vector
        def _(dve):
            chain = [0]

            def link(ins):
                chain[0] += 1
                ins.then_inc(dve_step, 1)
                dve.wait_ge(dve_step, chain[0])

            def fl(ap):
                return ap.rearrange("p a b -> p (a b)")

            def split_half(n, a, i=0):
                if n >= UNITS:
                    return
                hi, lo, src = w_half(n, a)
                dve.wait_ge(w_rounded, 8 * i + 2 * n + a + 1)
                dve.tensor_tensor(lo, src, hi.bitcast(F32), ALU.subtract).then_inc(w_split, 1)

            def ada_term(m, k, i=0):
                p = ada_pair(m)
                dst, w, c_ = ada_sum[:, p % 2], ada_slots(m, 2)[0][:, :, k], c_cols[:, k:k + 1]
                if k == 0:
                    for q in range(2):
                        dve.wait_ge(ada_landed[(m + q) % 8], 16 * (m // 8 + 1) + 8 * i)
                    if p >= 2:
                        dve.wait_ge(ada_added, ADA_SUMMED[2 * p - 3] + 1 + 4 * i)
                    dve.tensor_scalar(dst, w, c_, None, ALU.mult).then_inc(ada_terms, 1)
                else:
                    dve.wait_ge(ada_terms, 8 * p + k + 16 * i)
                    dve.scalar_tensor_tensor(dst, w, c_, dst, ALU.mult, ALU.add).then_inc(ada_terms, 1)

            def stream(name, work=None, after=None, some=None):
                n0, cnt = PARTS[name]

                def step(k, i, j):
                    n = n0 + j
                    halves = [lambda a=a: split_half(n + 2, a, i) for a in range(2)]
                    if has_ada(name, k):
                        m, t = ADA_WITH[name] + j // 2 * 2 - 2 * (name[:-1] == "out"), 4 * (j % 2)
                        ada_term(m, t, i)
                        halves.pop(0)()
                        ada_term(m, t + 1, i)
                        halves.pop(0)()
                        ada_term(m, t + 2, i)
                        ada_term(m, t + 3, i)
                    if work is not None:
                        work(k, i, j, banks[n][:, 0:SEQ], halves)
                    for half in halves:
                        half()
                    if after is not None and j:
                        after(k - 1, i, j - 1)

                if some is None:
                    units(dve, name, step)
                else:
                    for k in some:
                        step(k, 0, k)
                if after is not None:
                    after(cnt - 1, 0, cnt - 1)

            def taps(dst, w, ps, width, done, base, between):
                for s in range(1, width):
                    if s > 1 and between:
                        between.pop(0)()
                    if s > 1:
                        dve.wait_ge(done, base + s - 1)
                    dve.scalar_tensor_tensor(dst(slice(s, SEQ)), ps(slice(0, SEQ - s)), w(width - 1 - s), dst(slice(s, SEQ)),
                                             ALU.mult, ALU.add).then_inc(done, 1)

            def conv(layer):
                dst, base, cnt = convs[layer], layer * XBC_T, (XBC_T, GQ_T)[layer]

                def work(k, i, j, ps, halves):
                    dve.wait_ge(conv_first, base + k + 1)
                    taps(lambda t: dst[:, ds(k, 1), t], lambda tap: prm[:, ds(PRM[f"conv{layer}_w"] + tap * cnt + k, 1)],
                         lambda t: one(ps[:, t]), 4, conv_taps, 3 * (base + k), halves)

                stream(f"conv{layer}", work)

            def up(layer):
                base = 2 * FT * layer

                def work(k, i, j, ps, halves):
                    half, s = j % 2, j // 2 % 2
                    y = (yv if half else yg)[:, s]
                    col = half * FT + 2 * i + j // 2
                    dve.wait_ge(up_first, base + k + 1)
                    taps(lambda t: y[:, t], lambda tap: prm[:, ds(PRM["up_w"] + (3 * layer + tap) * 2 * FT + col, 1)],
                         lambda t: ps[:, t], 3, up_taps, 2 * (base + k), halves)
                    if half:
                        halves.pop(0)()
                        dve.wait_ge(gelu_done, FT * layer + 2 * i + j // 2 + 1)
                        dve.wait_ge(up_taps, 2 * (base + k) + 2)
                        dve.tensor_tensor(prod[:, s], yg[:, s], y, ALU.mult).then_inc(prod_done, 1)

                def after(k, i, j):
                    if j % 2:
                        pair = 2 * i + j // 2
                        dve.wait_ge(g_rounded, FT * layer + pair + 1)
                        dve.tensor_tensor(a_lo[:, ds(pair, 1), :], prod[:, j // 2 % 2:j // 2 % 2 + 1],
                                          a_hi[:, ds(pair, 1), :].bitcast(F32), ALU.subtract).then_inc(g_ready, 1)

                stream(f"up{layer}", work, after)

            def read_mods(a, b, bank):
                dve.wait_ge(ada_added, b)
                m = mods[:, :, :, :].rearrange("p l s k -> p (l s k)")
                dve.tensor_tensor(m[:, a:b], bank[:, a:b], prm[:, PRM["ada_b"] + a:PRM["ada_b"] + b], ALU.add).then_inc(mods_read, 1)

            def make_gain(layer, which, mods_at):
                dve.wait_ge(mods_read, mods_at)
                c = PRM["norm"] + (4 * layer + which) * 8
                w, g = prm[:, c:c + 8], gain[:, layer, which]
                section = {0: 1, 1: 2, 2: 4, 3: 5}[which]
                m = mods[:, layer, section]
                if which % 2 == 0:
                    link(dve.scalar_tensor_tensor(g, m, 1.0, w, ALU.add, ALU.mult))
                else:
                    link(dve.tensor_tensor(g, m, w, ALU.mult))

            def inverse_root(event):
                dve.wait_ge(roots, event + 1)
                dve.reciprocal(S("inv_rms", 0, 2), S("rms", 0, 2)).then_inc(inv_rms, 1)
                dve.wait_ge(spread, event + 1)

            def pre_norm(event, layer, which):
                inverse_root(event)
                norm = 2 * layer + which

                def rest(k):
                    dve.wait_ge(h_rounded, DT * norm + k + 1)
                    dve.scalar_tensor_tensor(h_lo[:, k], yr[:, k], mods[:, layer, 3 * which, k:k + 1], h_hi[:, k].bitcast(F32),
                                             ALU.add, ALU.subtract).then_inc(h_ready, 1)

                for k in range(DT):
                    dve.scalar_tensor_tensor(yr[:, k], x[:, k], gain[:, layer, 2 * which, k:k + 1], ROW_BANK[event][:, 0:SEQ],
                                             ALU.mult, ALU.mult).then_inc(scaled, 1)
                    if k >= 2:
                        rest(k - 2)
                rest(DT - 2)
                rest(DT - 1)

            def post_norm(event, layer, which):
                done = 8 * (2 * layer + which)
                for q in range(4):
                    dve.wait_ge(squares, DT * event + 2 * q + 2)
                    for k in (2 * q, 2 * q + 1):
                        last = dve.tensor_scalar(yr[:, k], acc(k), gain[:, layer, 2 * which + 1, k:k + 1], None, ALU.mult)
                last.then_inc(y_scaled, 4)
                inverse_root(event)
                rows_ = bc(one(ROW_BANK[event][:, 0:SEQ]), P, 2, SEQ)
                dve.wait_ge(y_scaled, done + 4)

                def add(q):
                    dve.wait_ge(y_scaled, done + 5 + q)
                    dve.tensor_tensor(x[:, 2 * q:2 * q + 2], x[:, 2 * q:2 * q + 2], yr[:, 2 * q:2 * q + 2], ALU.add).then_inc(x_ready, 2)

                for q in range(4):
                    dve.tensor_tensor(yr[:, 2 * q:2 * q + 2], yr[:, 2 * q:2 * q + 2], rows_, ALU.mult).then_inc(y_scaled, 1)
                    if q:
                        add(q - 1)
                add(3)

            def attention(layer):
                n8 = AH * layer
                if layer:
                    stream("v1", some=(0, 1))
                dve.wait_ge(bias_ready, layer + 1)
                for h in range(AH):
                    dve.wait_ge(s_scored, n8 + h + 1)
                    dve.tensor_tensor_reduce(scores[:, h, 0:SEQ], AB[h % 3][:, 0:SEQ], bias[:, h], 1.0, -3e38, ALU.add, ALU.max,
                                             S("max", h, 1)).then_inc(s_biased, 1)
                    dve.tensor_tensor_reduce(scores[:, h, SEQ:384], AB[h % 3][:, SEQ:384], bias[:, h, P:SEQ], 1.0, -3e38, ALU.add, ALU.max,
                                             S("max", 8 + h, 1)).then_inc(s_biased, 1)
                dve.wait_ge(s_biased, 2 * (n8 + AH))
                sink = bc(rows[:, ROW["sinks"]:ROW["sinks"] + 8].rearrange("p (a b) -> p a b", a=1), P, 2, 8)
                two = lambda t: S(t, 0, 16).rearrange("p (a b) -> p a b", a=2)
                if layer == 0:
                    link(dve.tensor_tensor(two("max"), two("max"), sink, ALU.max))
                    dve.tensor_tensor(two("sink_exp"), sink, two("max"), ALU.subtract)
                dve.tensor_scalar(S("neg_max", 0, 16), S("max", 0, 16), -1.0, None, ALU.mult).then_inc(s_max, 1)
                if layer == 0:
                    stream("z0", some=(0, 1, 2))
                else:
                    stream("v1", some=(2, 3))
                dve.wait_ge(s_exp, 17 if layer == 0 else 17 + 16)
                if layer == 0:
                    link(dve.tensor_tensor(S("prob_sum", 0, 16), S("prob_sum", 0, 16), S("sink_exp", 0, 16), ALU.add))
                link(dve.reciprocal(S("inv_sum", 0, 16), S("prob_sum", 0, 16)))
                for h in range(AH):
                    dve.tensor_scalar(scores[:, h, 0:SEQ], scores[:, h, 0:SEQ], S("inv_sum", h, 1), None, ALU.mult)
                    dve.tensor_scalar(scores[:, h, SEQ:384], scores[:, h, SEQ:384], S("inv_sum", 8 + h, 1), None, ALU.mult).then_inc(s_norm, 1)
                for t in range(4):
                    dve.wait_ge(s_rounded, 4 * layer + t + 1)
                    dve.tensor_tensor(a_lo[:, 18 + t], O_BANK[t % 2][:, 0:SEQ], a_hi[:, 18 + t].bitcast(F32), ALU.subtract).then_inc(s_ready, 1)

            def gates(layer):
                n, heads = (48, SSD_H) if layer == 0 else (24, GH)
                link(dve.scalar_tensor_tensor(S("abs", 0, n), S("dtx", 0, n), -1.0, S("dtx", 0, n), ALU.mult, ALU.max))
                if layer == 0:
                    link(dve.memset(S("bx", 0, 24), 0.0))
                dve.tensor_scalar(S("relu", 0, n), S("dtx", 0, n), 0.0, None, ALU.max).then_inc(gate_abs, 1)
                dve.wait_ge(gate_exp, 4 * layer + 3)
                link(dve.tensor_scalar(S("u", 0, n), S("e", 0, n), 1.0, None, ALU.add))
                link(dve.tensor_scalar(S("um", 0, n), S("u", 0, n), -1.0, None, ALU.add))
                dve.tensor_scalar(S("be1", 0, 24), S("be", 0, 24), 1.0, None, ALU.add).then_inc(gate_ln, 1)
                link(dve.tensor_tensor(S("um", 0, n), S("e", 0, n), S("um", 0, n), ALU.subtract))
                link(dve.reciprocal(S("ur", 0, n), S("u", 0, n)))
                dve.wait_ge(gate_ln, layer + 1)
                link(dve.reciprocal(S("beta", 0, 24), S("be1", 0, 24)))
                link(dve.tensor_tensor(S("um", 0, n), S("um", 0, n), S("ur", 0, n), ALU.mult))
                link(dve.tensor_tensor(S("um", 0, n), S("um", 0, n), S("relu", 0, n), ALU.add))
                dve.wait_ge(gate_exp, 4 * layer + 4)
                link(dve.tensor_tensor(S("dt", 0, n), S("um", 0, n), S("ln", 0, n), ALU.add))
                two = lambda t: S(t, 0, n).rearrange("p (a b) -> p a b", a=2)
                a_ = bc(S("a", 0, heads).rearrange("p (a b) -> p a b", a=1), P, 2, heads)
                dve.scalar_tensor_tensor(two("da"), two("dt"), -1.0, a_, ALU.mult, ALU.mult).then_inc(gate_ready, 1)

            def ssd():
                gates(0)
                dve.wait_ge(in_landed[3], 16)
                for half in range(2):
                    r = slice(half * 64, half * 64 + 64)
                    link(dve.tensor_copy(S("d", 0, 12, half * 64, half * 64 + 64), rows[r, ROW["d"] + half:ROW["d"] + 24:2]))
                dve.wait_ge(d_cum_mm, 1)
                link(dve.tensor_copy(S("cum", 0, 48), PB[2][:, 0:48]))
                dve.tensor_tensor(S("tail", 0, 24), PB[2][:, 48:72], S("cum", 0, 24), ALU.subtract).then_inc(d_cum, 1)
                dve.wait_ge(d_tail, 1)
                link(dve.tensor_tensor(S("tail", 0, 24), S("tail", 0, 24), S("dt", 0, 24), ALU.mult))
                dve.wait_ge(d_item, 3)
                dve.tensor_tensor(xd[:, :].rearrange("p (h d) -> p h d", h=24), xs_tok[:, 0].rearrange("p (h d) -> p h d", h=24),
                                  bc(S("tail", 0, 24).rearrange("p (h d) -> p h d", d=1), P, 24, 64), ALU.mult).then_inc(d_xd, 1)
                dve.wait_ge(d_item, 9)
                stream("z0", some=(3,))

                def diff(n):
                    b, h0 = n // 6, 4 * (n % 6)
                    dve.wait_ge(d_decay_mm, n + 1)
                    for q in range(4):
                        last = dve.scalar_tensor_tensor(lmat[:, n % 2, q], AB[n % 2][:, q * P:q * P + P], S("cum", 24 * b + h0 + q, 1),
                                                        C("keep"), ALU.subtract, ALU.min)
                    last.then_inc(d_diff, 1)

                def weights(n):
                    b, h0 = n // 6, 4 * (n % 6)
                    dve.wait_ge(d_decay, n + 1)
                    if n >= 2:
                        dve.wait_ge(d_y_mm, n - 1)
                    for q in range(4):
                        h = h0 + q
                        if b:
                            dve.tensor_tensor(cexp[:, n % 2, q], cexp[:, n % 2, q], conv0[:, 16 + h // HPG, P:2 * P], ALU.mult)
                        last = dve.scalar_tensor_tensor(mmat[:, n % 2, q], lmat[:, n % 2, q], S("dt", 24 * b + h, 1), cb[:, b, h // HPG],
                                                        ALU.mult, ALU.mult)
                    last.then_inc(d_mmat, 1)

                def outputs(n):
                    b, t0 = n // 6, 2 * (n % 6)
                    dve.wait_ge(d_y_mm, n + 1)
                    for q in range(2):
                        c = slice(b * P, b * P + P)
                        last = dve.scalar_tensor_tensor(y_ssd[:, t0 + q, c], conv0[:, t0 + q, c], S("d", t0 + q, 1),
                                                        Y_BANK[n % 3][:, q * P:q * P + P], ALU.mult, ALU.add)
                    last.then_inc(d_y, 1)

                diff(0)
                for n in range(12):
                    if n < 8:
                        stream("z0", some=(4 + n,))
                    if n < 11:
                        diff(n + 1)
                    weights(n)
                    if n:
                        outputs(n - 1)
                outputs(11)
                dve.wait_ge(d_y, 12)
                for g in range(SSD_G):
                    t = slice(3 * g, 3 * g + 3)
                    dve.wait_ge(z_silu, g + 1)
                    dve.tensor_tensor(y_ssd[:, t], y_ssd[:, t], zs[:, t], ALU.mult).then_inc(d_gated, 1)
                dve.wait_ge(d_root, 1)
                dve.reciprocal(S("group_inv", 0, 8), S("group_rms", 0, 8)).then_inc(d_inv, 1)
                for g in range(SSD_G):
                    dve.wait_ge(d_spread, g // 2 + 1)
                    for k in range(3 * g, 3 * g + 3):
                        last = dve.scalar_tensor_tensor(y_mix[:, k], y_ssd[:, k], prm[:, PRM["ssd_norm"] + k:PRM["ssd_norm"] + k + 1],
                                                        PB[g // 2][:, (g % 2) * SEQ:(g % 2 + 1) * SEQ], ALU.mult, ALU.mult)
                    last.then_inc(d_mix, 1)
                    if g:
                        mix_rest(g - 1)
                mix_rest(3)
                mark_attention(0)

            def mix_rest(g):
                dve.wait_ge(d_rounded, g + 1)
                for k in range(3 * g, 3 * g + 3):
                    dve.tensor_tensor(a_lo[:, k], y_mix[:, k], a_hi[:, k].bitcast(F32), ALU.subtract).then_inc(mix_ready, 1)

            def mark_attention(layer):
                dve.wait_ge(mix_ready, MIX_T * layer + 12)
                dve.sem_inc(mix_ready, 4)

            def lengths():
                gates(1)
                for n in range(12):
                    dve.wait_ge(n_spread, n + 1)
                    t = conv1[:, 2 * n:2 * n + 2]
                    dve.tensor_tensor(t, t, AB[n % 4][:, :].rearrange("p (a t) -> p a t", a=2), ALU.mult).then_inc(n_unit, 1)
                dve.wait_ge(g_cum_mm, 1)
                link(dve.tensor_copy(S("cum", 0, 24), PB[2][:, 0:24]))
                for j in range(2):
                    dve.tensor_copy(S(f"tot{j}", 0, 24), PB[2][:, 48 + 24 * j:72 + 24 * j])
                dve.tensor_tensor(S("tail", 0, 24), PB[2][:, 24:48], S("cum", 0, 24), ALU.subtract).then_inc(g_cum, 1)

            def gdn():
                stack = lambda ap, n: bc(ap.rearrange("p (s d) -> p s d", d=1), ap.shape[0], ap.shape[1], n)
                keep = bc(C("keep_chunk", 0, GC).rearrange("p (a d) -> p a d", a=1), P, 4, GC)
                for n in range(6):
                    dve.wait_ge(g_decay_mm, n + 1)
                    ps = PB[n % 2][:, :].rearrange("p (a d) -> p a d", a=4)
                    for j in range(2):
                        r = slice(j * GC, j * GC + GC)
                        last = dve.tensor_tensor(dec[r, 4 * n:4 * n + 4], ps[r, :, r], stack(S("cum", 4 * n, 4, r.start, r.stop), GC), ALU.subtract)
                    link(last)
                    dve.tensor_tensor(dec[:, 4 * n:4 * n + 4], dec[:, 4 * n:4 * n + 4], keep, ALU.min).then_inc(g_diff, 1)
                dve.wait_ge(g_tail, 1)
                for n in range(6):
                    dve.wait_ge(k_turned, n + 1)
                    b, h = 4 * n // GH, 4 * n % GH
                    dve.tensor_tensor(k_tok[:, b, h:h + 4], AB[n % 4][:, :].rearrange("p (a d) -> p a d", a=4),
                                      stack(S("tail", 4 * n, 4), GD), ALU.mult).then_inc(k_copied, 1)
                ident = bc(C("ident_chunk", 0, GC).rearrange("p (a d) -> p a d", a=1), P, 8, GC)
                three = lambda bank: bank[:, :].rearrange("p (a d) -> p a d", a=8)

                def off_blocks(lv, m):
                    s8 = slice(8 * m, 8 * m + 8)
                    for r in (slice(0, GC), slice(GC, P)):
                        mask = bc(C("level", lv * GC, GC, r.start, r.stop).rearrange("p (a d) -> p a d", a=1), GC, 8, GC)
                        last = dve.tensor_tensor(off_bd[r, s8, r], sys_t[r, s8], mask, ALU.mult)
                    last.then_inc(i_off, 1)

                for m in range(3):
                    s8 = slice(8 * m, 8 * m + 8)
                    dve.wait_ge(g_gram_mm, 2 * m + 1)
                    dve.wait_ge(g_decay, min(6, 2 * m + 2))
                    link(dve.tensor_tensor(sys_t[:, s8], three(AB[2 * m % 4]), dec[:, s8], ALU.mult))
                    link(dve.tensor_tensor(sys_t[:, s8], sys_t[:, s8], stack(S("beta", 8 * m, 8), GC), ALU.mult))
                    dve.sem_inc(g_gram, 1)
                    dve.wait_ge(g_gram_mm, 2 * m + 2)
                    dve.tensor_tensor(attn_t[:, s8], three(AB[(2 * m + 1) % 4]), dec[:, s8], ALU.mult).then_inc(g_gram, 1)
                    if m == 0:
                        dve.wait_ge(zeroed, 2)
                    off_blocks(0, m)
                    mask = bc(C("level", 0, GC).rearrange("p (a d) -> p a d", a=1), P, 8, GC)
                    link(dve.tensor_tensor(inv_t[:, s8], sys_t[:, s8], mask, ALU.mult))
                    dve.tensor_tensor(inv_t[:, s8], ident, inv_t[:, s8], ALU.subtract)
                dve.wait_ge(g_gram_mm, 6)
                for b in range(NB):
                    t = conv1[:, 12:12 + GH, b * P:b * P + P]
                    dve.tensor_tensor(t, t, egc[:, b * GH:b * GH + GH], ALU.mult).then_inc(g_scaled, 1)
                for lv in range(LEVELS):
                    if lv == 0:
                        for m in range(3):
                            s8 = slice(8 * m, 8 * m + 8)
                            dve.wait_ge(i_y_mm, m + 1)
                            dve.tensor_tensor(inv[:, s8], ident, three(BANKS[m]), ALU.subtract).then_inc(i_inv, 1)
                    if lv < LEVELS - 1:
                        for m in range(3):
                            dve.wait_ge(i_y_mm, 3 * lv + m + 1)
                            off_blocks(lv + 1, m)
                    if lv:
                        for m in range(3):
                            s8 = slice(8 * m, 8 * m + 8)
                            dve.wait_ge(i_inv, 3 * (lv - 1) + m + 1)
                            if lv < LEVELS - 1:
                                dve.wait_ge(i_z_mm, 3 * (lv - 1) + m + 1)
                                dve.tensor_tensor(inv[:, s8], inv[:, s8], three(BANKS[3 + m]), ALU.subtract)
                            dve.wait_ge(i_zt_mm, 3 * (lv - 1) + m + 1)
                            dve.tensor_tensor(inv_t[:, s8], inv_t[:, s8], three(BANKS[m]), ALU.subtract).then_inc(i_inv, 1)
                            if 3 * (lv - 1) + m < ZT:
                                stream("z1", some=(3 * (lv - 1) + m,))

                def residual(n):
                    c, g = SCAN[n]
                    b, r = c // 2, slice((c % 2) * GC, (c % 2) * GC + GC)
                    if c == 0:
                        if n >= 2:
                            dve.wait_ge(c_tr_mm, n - 1)
                        dve.tensor_copy(resid[r, 0, n % 2], v_tok[r, b, 4 * g:4 * g + 4]).then_inc(c_resid, 1)
                    else:
                        dve.wait_ge(c_ks_mm, n - 2)
                        dve.tensor_tensor(resid[r, c % 2, n % 2], v_tok[r, b, 4 * g:4 * g + 4],
                                          BANKS[0][r, :].rearrange("p (a d) -> p a d", a=4), ALU.subtract).then_inc(c_resid, 1)

                def values(n):
                    c, g = SCAN[n]
                    b, r = c // 2, slice((c % 2) * GC, (c % 2) * GC + GC)
                    dve.wait_ge(c_tr_mm, n + 1)
                    dve.tensor_tensor(v_new[r, c % 2, g], BANKS[2 + n % 2][r, :].rearrange("p (a d) -> p a d", a=4),
                                      stack(S("beta", b * GH + 4 * g, 4, r.start, r.stop), GD), ALU.mult).then_inc(c_vnew, 1)

                def states(n):
                    c, g = SCAN[n]
                    if c == 3:
                        return
                    b, j = c // 2, c % 2
                    dve.wait_ge(c_u_mm, n + 1)
                    if c == 0:
                        dve.tensor_copy(state[:, 4 * g:4 * g + 4], BANKS[6 + n % 2][:, :].rearrange("p (a d) -> p a d", a=4)).then_inc(c_state, 1)
                        return
                    for q in range(4):
                        h = 4 * g + q
                        last = dve.scalar_tensor_tensor(state[:, h], state[:, h], S(f"tot{j}", b * GH + h, 1),
                                                        BANKS[6 + n % 2][:, q * GD:q * GD + GD], ALU.mult, ALU.add)
                    last.then_inc(c_state, 1)

                dve.wait_ge(g_tot, 2)
                dve.wait_ge(zeroed, 5)
                for n in range(len(SCAN) + 2):
                    if n < len(SCAN):
                        residual(n)
                    if 0 <= n - 1 < len(SCAN):
                        values(n - 1)
                    if n >= 2:
                        states(n - 2)

                def o_rest(n):
                    g, b = OUT_STEPS[n]
                    dve.wait_ge(o_rounded, n + 1)
                    t = slice(b * P, b * P + P)
                    dve.tensor_tensor(a_lo[:, 4 * g:4 * g + 4, t], o_t[:, n % 3], a_hi[:, 4 * g:4 * g + 4, t].bitcast(F32),
                                      ALU.subtract).then_inc(o_split, 1)
                    if b:
                        dve.wait_ge(o_split, n + 1)
                        dve.sem_inc(mix_ready, 4)

                def scale(n):
                    g, b = OUT_STEPS[n]
                    o = o_tok[:, b, 4 * g:4 * g + 4]
                    dve.tensor_tensor(o, o, stack(S("o_inv", b * GH + 4 * g, 4), GD), ALU.mult).then_inc(o_scaled, 1)

                dve.wait_ge(o_root, 1)
                link(dve.reciprocal(S("o_inv", 0, 24), S("o_rms", 0, 24)))
                dve.wait_ge(c_o, 12)
                dve.wait_ge(copied, last_copy["z1"])
                scale(0)
                scale(1)
                for n, (g, b) in enumerate(OUT_STEPS):
                    if n + 2 < len(OUT_STEPS):
                        scale(n + 2)
                    dve.wait_ge(o_turned, n + 1)
                    if n >= 3:
                        dve.wait_ge(o_split, n - 2)
                    dve.scalar_tensor_tensor(o_t[:, n % 3], PB[1 + n % 3][:, :].rearrange("p (a t) -> p a t", a=4),
                                             prm[:, PRM["gdn_norm"]:PRM["gdn_norm"] + 1],
                                             zs[:, 4 * g:4 * g + 4, b * P:b * P + P], ALU.mult, ALU.mult).then_inc(o_mixed, 1)
                    if n:
                        o_rest(n - 1)
                o_rest(5)
                mark_attention(1)

            def read_dt(layer):
                def work(k, i, j, ps, halves):
                    heads = (SSD_H, GH)[layer]
                    n = PARTS[f"dt{layer}"][0]
                    dve.wait_ge(w_used, 2 * n + 2)
                    dve.wait_ge(in_landed[3], 16)
                    v = ps.rearrange("p (b c) -> p b c", b=NB)
                    two = lambda t: S(t, 0, 2 * heads).rearrange("p (a b) -> p a b", a=2)
                    r0 = ROW[f"dt_bias{layer}"]
                    b_ = bc(rows[:, r0:r0 + heads].rearrange("p (a b) -> p a b", a=1), P, 2, heads)
                    if layer:
                        link(dve.tensor_copy(two("bx"), v[:, :, 0:heads]))
                    dve.tensor_tensor(two("dtx"), v[:, :, layer * heads:(layer + 1) * heads], b_, ALU.add).then_inc(dt_read, 1)

                stream(f"dt{layer}", work)
                dve.wait_ge(dt_read, layer + 1)

            def mixer(layer):
                read_dt(layer)
                conv(layer)
                stream(f"q{layer}")
                if layer:
                    stream("k1", some=(0, 1, 2))
                    dve.wait_ge(n_root, 1)
                    link(dve.reciprocal(S("l2_inv", 0, 48), S("l2", 0, 48)))
                    dve.tensor_scalar(S("l2_inv", 0, 24), S("l2_inv", 0, 24), GD ** -0.5, None, ALU.mult).then_inc(n_inv, 1)
                    stream("k1", some=(3,))
                else:
                    stream("k0")
                if layer == 0:
                    for k in range(8):
                        ada_term(20, k)
                    stream("v0")
                    attention(0)
                    ssd()
                    read_mods(16, 40, PB[3])
                    make_gain(0, 1, 2)
                    make_gain(0, 2, 2)
                else:
                    lengths()
                    attention(1)
                    read_mods(72, 80, PB[3])
                    gdn()
                stream(f"out{layer}")

            dve.memset(rel[32:33, :], 1.0).then_inc(rel_ones, 1)
            dve.wait_ge(prm_turned, 1)
            dve.tensor_copy(prm[:, 0:512], PB[0][:, :])
            dve.tensor_copy(prm[:, 512:PRM_G * P], PB[1][:, 0:PRM_G * P - 512]).then_inc(prm_ready, 1)
            dve.wait_ge(c_ready, 1)
            for m in (2, 6, 10, 14):
                for k in range(8):
                    ada_term(m, k)
            dve.wait_ge(vec_mm, 1)
            for v in range(2):
                last = dve.tensor_copy(bias_vec[0:AH, v], AB[v][0:AH, 0:384])
            last.then_inc(vec_copied, 1)
            for n in range(2):
                split_half(n, 0)
                split_half(n, 1)
            dve.wait_ge(prm_ready, 1)
            dve.wait_ge(c_ready, 1)
            read_mods(0, 16, AB[3])
            make_gain(0, 0, 1)
            pre_norm(0, 0, 0)
            mixer(0)
            read_mods(40, 52, PB[2])
            make_gain(0, 3, 3)
            post_norm(1, 0, 0)
            pre_norm(2, 0, 1)
            up(0)
            stream("down0")
            read_mods(52, 72, PB[0])
            make_gain(1, 0, 4)
            make_gain(1, 1, 4)
            post_norm(3, 0, 1)
            pre_norm(4, 1, 0)
            mixer(1)
            read_mods(80, 92, PB[1])
            make_gain(1, 2, 6)
            post_norm(5, 1, 0)
            pre_norm(6, 1, 1)
            up(1)
            stream("down1")
            read_mods(92, 96, PB[2])
            make_gain(1, 3, 7)
            post_norm(7, 1, 1)

        @block.gpsimd
        def _(pool):
            pool.memset(c_silu[:, :, :], 0.0).then_inc(c_zeroed, 1)
            pool.wait_ge(s_ready, 8)
            pool.memset(inv_t_bd[:, :, :], 0.0).then_inc(zeroed, 1)
            pool.memset(off_bd[:, :, :], 0.0).then_inc(zeroed, 1)
            pool.wait_ge(g_gram_mm, 6)
            pool.wait_ge(g_decay, 6)
            for b in range(NB):
                t = conv1[:, 0:GH, b * P:b * P + P]
                pool.tensor_tensor(t, t, egc[:, b * GH:b * GH + GH], ALU.mult).then_inc(g_scaled, 1)
            pool.wait_ge(g_scaled, 4)
            pool.memset(step_y_bd[:, :, :], 0.0).then_inc(zeroed, 1)
            pool.wait_ge(i_z_mm, 3 * (LEVELS - 2))
            pool.wait_ge(i_off, 3 * LEVELS)
            pool.memset(v_new[:, :, :, :, :], 0.0).then_inc(zeroed, 1)
            pool.memset(resid[:, :, :, :, :], 0.0).then_inc(zeroed, 1)


def unit_columns(w, first, count, width=P):
    v = w[:, first:first + count * width].reshape(8, P, count, width)
    return v.transpose(1, 2, 0, 3).reshape(P, count, 8 * P)


def unit_rows(w):
    return w.reshape(-1, P, D_MODEL).transpose(1, 0, 2)


def unit_wide(w, first):
    return w[:, first:first + 512].reshape(4, 2, P, 512).transpose(2, 0, 1, 3).reshape(P, 4, 8 * P)


def kernel(**inputs):
    import concourse.bacc as bacc
    from concourse.bass_utils import run_bass_kernel_spmd

    v = {k: np.asarray(a) for k, a in inputs.items()}
    zeros = np.zeros((D_MODEL, P - 24), np.float32)

    def mixer_units(w, n_z, n_conv, n_att, gates_at, z_at, conv_at, att_at, wide):
        gates = np.concatenate([w[:, gates_at:gates_at + 24], zeros], axis=1)
        return ([unit_columns(gates, 0, 1), unit_columns(w, conv_at, n_conv), unit_columns(w, att_at, n_att)]
                + ([unit_wide(w, wide)] if wide else []) + [unit_columns(w, z_at, n_z)])

    def ffn_units(layer):
        w = v["ffn_w_up"][layer]
        both = np.stack([unit_columns(w, 0, FT), unit_columns(w, FT * P, FT)], axis=2)
        return [both.reshape(P, 2 * FT, 8 * P), unit_rows(v["ffn_w_down"][layer])]

    ab, cd = v["ab_w_in"][0], v["cd_w_in"][0]
    w_stream = np.ascontiguousarray(np.concatenate(
        mixer_units(ab, ZT, XBC_T, 6, 4096, 0, 1536, 4120, None) + [unit_rows(v["ab_w_out"][0])] + ffn_units(0)
        + mixer_units(cd, ZT, GQ_T, 8, 6144, 4608, 0, 6168, 7192) + [unit_rows(v["cd_w_out"][0])] + ffn_units(1), axis=1))
    ada_stream = np.ascontiguousarray(np.concatenate([unit_columns(v["ada_w"][layer], 0, 48) for layer in range(2)], axis=1))
    prm = np.concatenate([v[k].reshape(-1, P) for k in ("c", "ada_b", "norm_w", "ssd_conv_w", "ssd_conv_b", "ssd_norm_w",
                                                        "gdn_conv_w", "gdn_norm_w", "ffn_conv_w", "ffn_conv_b")])
    prm = np.concatenate([prm, np.zeros((PRM_G * P - PRM_COLS, P), np.float32)]).reshape(PRM_G, P, P).transpose(1, 0, 2)
    rows = np.concatenate([v[k].reshape(1, -1) for k in ("ssd_dt_bias", "ssd_a_log", "ssd_d", "swa_sinks", "gdn_dt_bias",
                                                         "gdn_a_log")], axis=1)
    arrays = {
        "w_stream": w_stream, "ada_stream": ada_stream,
        "x_tiles": np.ascontiguousarray(v["x"][0].T.reshape(DT, P, SEQ).transpose(1, 0, 2)),
        "prm": np.ascontiguousarray(prm), "rows": np.ascontiguousarray(rows),
        "constants": constants(), "buckets": bucket_rows(), "rel_bias": np.ascontiguousarray(v["rel_bias"]),
    }
    nc = bacc.Bacc("TRN2", target_bir_lowering=False, num_devices=1)
    aps = [nc.dram_tensor(f"in_{k}", a.shape, mybir.dt.from_np(a.dtype), kind="ExternalInput").ap() for k, a in arrays.items()]
    scratch = nc.dram_tensor("bias_scratch", (AH, 2, 384), F32).ap()
    out = nc.dram_tensor("out_tiles", (P, DT, SEQ), F32, kind="ExternalOutput").ap()
    build(nc, *aps, scratch, out)
    r = run_bass_kernel_spmd(nc, [{f"in_{k}": a for k, a in arrays.items()}], core_ids=[0])
    got = r.results[0]["out_tiles"]
    return np.ascontiguousarray(got.transpose(1, 0, 2).reshape(D_MODEL, SEQ).T).reshape(1, SEQ, D_MODEL)
```
